# Optimizing a Trainium2 kernel written in Bass

```python
import math
import jax, jax.numpy as jnp
from jax import lax
import numpy as np

D_MODEL = 1024
BATCH = 1
SEQ = 512
DEPTH = 1

CHUNK = 64
MEM_LEN = 256
NORM_EPS = 1e-6
GN_EPS = 1e-5

LRU_W = 512
LRU_BLOCKS = 8
LRU_BW = LRU_W // LRU_BLOCKS
CONV_W = 4
LRU_C = 8.0
CA_HEADS = 8
CA_HD = 64
CA_PREV = 8
CA_BAND = (CA_PREV + 1) * CHUNK
REL_CLIP = 128
RET_HEADS = 8
RET_HD = 64
RET_VD = 64
DIFF_HEADS = 4
DIFF_HD = 64
DIFF_VD = 2 * DIFF_HD
Q_BLOCK = 128
MX_HEADS = 4
MX_HD = 128
N_GROUPS = 4
EXP_PER_GROUP = 8
N_EXPERTS = N_GROUPS * EXP_PER_GROUP
TOP_K = 2
D_EXPERT = 512
MOE_BLOCK = 256
N_BRANCH = 4
BRANCH_W = 512

SPLIT_WIDTHS = (
    LRU_W, LRU_W,
    CA_HEADS * CA_HD, CA_HEADS * CA_HD, CA_HEADS * CA_HD,
    RET_HEADS * RET_HD, RET_HEADS * RET_HD, RET_HEADS * RET_VD, RET_HEADS * RET_VD,
    DIFF_HEADS * 2 * DIFF_HD, DIFF_HEADS * 2 * DIFF_HD, DIFF_HEADS * DIFF_VD,
    N_BRANCH * D_MODEL,
)
IN_COLS = sum(SPLIT_WIDTHS)

kernel_name = "hybrid_lru_chunkattn_retention_diffattn_hmoe"

def _rmsnorm(x, g, eps=NORM_EPS):
    xf = x.astype(jnp.float32)
    y = xf * lax.rsqrt(jnp.mean(xf * xf, axis=-1, keepdims=True) + eps)
    return (y * g.astype(jnp.float32)).astype(x.dtype)

def _split_columns(z):
    parts, off = [], 0
    for w in SPLIT_WIDTHS:
        parts.append(z[..., off:off + w])
        off += w
    return parts

def _rg_lru_branch(xr, xg, conv_w, conv_b, wa, ba, wx, bx, lam):
    b, n, _ = xr.shape
    f32 = jnp.float32
    xp = jnp.pad(xr, ((0, 0), (CONV_W - 1, 0), (0, 0)))
    xc = conv_b + sum(xp[:, j:j + n] * conv_w[j] for j in range(CONV_W))
    xc32 = xc.astype(f32)
    xblk = xc32.reshape(b, n, LRU_BLOCKS, LRU_BW)
    r = jax.nn.sigmoid(jnp.einsum("bnkc,kcd->bnkd", xblk, wa.astype(f32)).reshape(b, n, LRU_W) + ba.astype(f32))
    i = jax.nn.sigmoid(jnp.einsum("bnkc,kcd->bnkd", xblk, wx.astype(f32)).reshape(b, n, LRU_W) + bx.astype(f32))
    log_a = -LRU_C * r * jax.nn.softplus(-lam.astype(f32))
    a = jnp.exp(log_a)
    u = jnp.sqrt(-jnp.expm1(2.0 * log_a)) * (i * xc32)

    def combine(left, right):
        a1, b1 = left
        a2, b2 = right
        return a1 * a2, a2 * b1 + b2

    _, hseq = lax.associative_scan(combine, (a, u), axis=1)
    return (hseq * jax.nn.gelu(xg.astype(f32))).astype(xr.dtype)

def _chunk_attention(q, k, v, rel_table):
    b, n, _ = q.shape
    nc = n // CHUNK
    q = q.reshape(b, nc, CHUNK, CA_HEADS, CA_HD)
    k = k.reshape(b, nc, CHUNK, CA_HEADS, CA_HD)
    v = v.reshape(b, nc, CHUNK, CA_HEADS, CA_HD)
    pad = ((0, 0), (CA_PREV, 0), (0, 0), (0, 0), (0, 0))
    kp, vp = jnp.pad(k, pad), jnp.pad(v, pad)
    k_band = jnp.concatenate([kp[:, j:j + nc] for j in range(CA_PREV + 1)], axis=2)
    v_band = jnp.concatenate([vp[:, j:j + nc] for j in range(CA_PREV + 1)], axis=2)
    s = jnp.einsum("bcqhd,bckhd->bhcqk", q, k_band).astype(jnp.float32) * (CA_HD ** -0.5)
    qi = np.arange(CHUNK)[:, None]
    kj = np.arange(CA_BAND)[None, :]
    dist = qi + CA_PREV * CHUNK - kj
    idx = np.clip(dist, -REL_CLIP, REL_CLIP) + REL_CLIP
    bias = rel_table[:, idx].astype(jnp.float32)
    key_chunk = np.arange(nc)[:, None] - CA_PREV + (np.arange(CA_BAND) // CHUNK)[None, :]
    valid = key_chunk >= 0
    s = jnp.where(valid[None, None, :, None, :], s + bias[None, :, None], -jnp.inf)
    p = jax.nn.softmax(s, axis=-1).astype(v.dtype)
    o = jnp.einsum("bhcqk,bckhd->bcqhd", p, v_band)
    return o.reshape(b, n, CA_HEADS * CA_HD)

def _retention(q, k, v, g):
    b, n, _ = q.shape
    nc = n // CHUNK
    f32 = jnp.float32
    q = q.reshape(b, nc, CHUNK, RET_HEADS, RET_HD).astype(f32)
    k = k.reshape(b, nc, CHUNK, RET_HEADS, RET_HD).astype(f32) * (RET_HD ** -0.5)
    v = v.reshape(b, nc, CHUNK, RET_HEADS, RET_VD).astype(f32)
    log_g = np.log(1.0 - 2.0 ** (-5.0 - np.arange(RET_HEADS))).astype(np.float32)
    pos = np.arange(CHUNK)
    diff = pos[:, None] - pos[None, :]
    decay = np.where(diff[None] >= 0, np.exp(log_g[:, None, None] * np.maximum(diff, 0)[None]), 0.0).astype(np.float32)
    inner = jnp.einsum("bcihd,bcjhd->bchij", q, k) * decay[None, None]
    o_inner = jnp.einsum("bchij,bcjhe->bcihe", inner, v)
    zeta = np.exp(log_g[None, :] * (CHUNK - 1 - pos)[:, None]).astype(np.float32)
    kv = jnp.einsum("bcjhd,jh,bcjhe->bchde", k, zeta, v)
    g_chunk = np.exp(log_g * CHUNK).astype(np.float32)

    def step(state, kv_c):
        return g_chunk[:, None, None] * state + kv_c, state

    init = jnp.zeros((b, RET_HEADS, RET_HD, RET_VD), f32)
    _, r_prev = lax.scan(step, init, jnp.moveaxis(kv, 1, 0))
    r_prev = jnp.moveaxis(r_prev, 0, 1)
    xi = np.exp(log_g[None, :] * (pos + 1)[:, None]).astype(np.float32)
    o_cross = jnp.einsum("bcihd,bchde->bcihe", q, r_prev) * xi[None, None, :, :, None]
    o = o_inner + o_cross
    mu = jnp.mean(o, axis=-1, keepdims=True)
    var = jnp.mean(jnp.square(o - mu), axis=-1, keepdims=True)
    o = ((o - mu) * lax.rsqrt(var + GN_EPS)).reshape(b, n, RET_HEADS * RET_VD)
    return (jax.nn.silu(g.astype(f32)) * o).astype(g.dtype)

def _diff_attention(q, k, v, lam_vecs, subln_g, lam_init):
    b, n, _ = q.shape
    f32 = jnp.float32
    q = q.reshape(b, n, DIFF_HEADS, 2, DIFF_HD)
    k = k.reshape(b, n, DIFF_HEADS, 2, DIFF_HD)
    v = v.reshape(b, n, DIFF_HEADS, DIFF_VD)
    lv = lam_vecs.astype(f32)
    lam = jnp.exp(jnp.sum(lv[0] * lv[1])) - jnp.exp(jnp.sum(lv[2] * lv[3])) + lam_init
    slopes = (2.0 ** (-8.0 * np.arange(1, DIFF_HEADS + 1) / DIFF_HEADS)).astype(np.float32)
    nb = n // Q_BLOCK
    qb = jnp.moveaxis(q.reshape(b, nb, Q_BLOCK, DIFF_HEADS, 2, DIFF_HD), 1, 0)
    kpos = jnp.arange(n)

    def block(args):
        q_blk, blk = args
        qpos = blk * Q_BLOCK + jnp.arange(Q_BLOCK)
        s = jnp.einsum("bqhmd,bkhmd->bmhqk", q_blk, k).astype(f32) * (DIFF_HD ** -0.5)
        dist = jnp.abs(qpos[:, None] - kpos[None, :]).astype(f32)
        alibi = -slopes[:, None, None] * dist[None]
        allowed = (kpos[None, :] // CHUNK) <= (qpos[:, None] // CHUNK)
        s = jnp.where(allowed, s + alibi, -jnp.inf)
        p = jax.nn.softmax(s, axis=-1)
        attn = p[:, 0] - lam * p[:, 1]
        return jnp.einsum("bhqk,bkhe->bqhe", attn.astype(v.dtype), v)

    o = lax.map(block, (qb, jnp.arange(nb)))
    o = jnp.moveaxis(o, 0, 1).reshape(b, n, DIFF_HEADS, DIFF_VD).astype(f32)
    o = o * lax.rsqrt(jnp.mean(o * o, axis=-1, keepdims=True) + GN_EPS) * subln_g.astype(f32)
    o = o * (1.0 - lam_init)
    return o.reshape(b, n, DIFF_HEADS * DIFF_VD).astype(v.dtype)

def _memory_cross_attention(h, mem_n, wq, wk, wv, wo):
    b, n, _ = h.shape
    m = mem_n.shape[1]
    q = (h @ wq).reshape(b, n, MX_HEADS, MX_HD)
    k = (mem_n @ wk).reshape(b, m, MX_HEADS, MX_HD)
    v = (mem_n @ wv).reshape(b, m, MX_HEADS, MX_HD)
    s = jnp.einsum("bnhd,bmhd->bhnm", q, k).astype(jnp.float32) * (MX_HD ** -0.5)
    p = jax.nn.softmax(s, axis=-1).astype(v.dtype)
    o = jnp.einsum("bhnm,bmhd->bnhd", p, v).reshape(b, n, MX_HEADS * MX_HD)
    return o @ wo

def _hier_moe(h, w_group, b_group, w_router, b_router, w1, w3, w2):
    b, n, d = h.shape
    t = h.reshape(b * n, d)
    n_tok = b * n
    f32 = jnp.float32
    rows = jnp.arange(n_tok)
    g_logits = (t @ w_group).astype(f32) + b_group.astype(f32)
    g_prob = jax.nn.softmax(g_logits, axis=-1)
    g_sel = jnp.argmax(g_logits, axis=-1)
    e_logits = ((t @ w_router).astype(f32) + b_router.astype(f32)).reshape(n_tok, N_GROUPS, EXP_PER_GROUP)
    e_prob = jax.nn.softmax(e_logits[rows, g_sel], axis=-1)
    top_p, top_i = lax.top_k(e_prob, TOP_K)
    top_p = top_p / jnp.sum(top_p, axis=-1, keepdims=True) * g_prob[rows, g_sel][:, None]
    expert = g_sel[:, None] * EXP_PER_GROUP + top_i
    flat_e = expert.reshape(-1).astype(jnp.int32)
    flat_w = top_p.reshape(-1)
    n_asg = n_tok * TOP_K
    order = jnp.argsort(flat_e)
    sorted_e = flat_e[order]
    counts = jnp.bincount(flat_e, length=N_EXPERTS)
    padded = (counts + MOE_BLOCK - 1) // MOE_BLOCK * MOE_BLOCK
    pad_end = jnp.cumsum(padded)
    pad_start = pad_end - padded
    start = jnp.cumsum(counts) - counts
    dest = pad_start[sorted_e] + jnp.arange(n_asg) - start[sorted_e]
    n_blocks = -(-(n_asg + N_EXPERTS * (MOE_BLOCK - 1)) // MOE_BLOCK)
    n_slots = n_blocks * MOE_BLOCK
    slot_tok = jnp.full((n_slots,), n_tok, jnp.int32).at[dest].set((order // TOP_K).astype(jnp.int32))
    slot_w = jnp.zeros((n_slots,), f32).at[dest].set(flat_w[order])
    block_e = jnp.minimum(jnp.searchsorted(pad_end, jnp.arange(n_blocks) * MOE_BLOCK, side="right"), N_EXPERTS - 1)
    t_pad = jnp.concatenate([t, jnp.zeros((1, d), t.dtype)], axis=0)
    xs = t_pad[slot_tok].reshape(n_blocks, MOE_BLOCK, d)

    def expert_block(args):
        xb, e = args
        hid = jax.nn.silu(xb @ w1[e]) * (xb @ w3[e])
        return hid @ w2[e]

    ys = lax.map(expert_block, (xs, block_e)).reshape(n_slots, d)
    out = jax.ops.segment_sum(ys * slot_w[:, None].astype(ys.dtype), slot_tok, num_segments=n_tok + 1)[:n_tok]
    return out.reshape(b, n, d).astype(h.dtype)

def setup_inputs(seed: int = 0) -> dict:
    key = jax.random.key(seed)
    ks = iter(jax.random.split(key, 40))
    L, D = DEPTH, D_MODEL

    def normal(shape, scale):
        return jax.random.normal(next(ks), shape, jnp.float32) * scale

    def gain(shape):
        return 1.0 + 0.05 * jax.random.normal(next(ks), shape, jnp.float32)

    a0 = jax.random.uniform(next(ks), (L, LRU_W), jnp.float32, 0.9, 0.999)
    a_root = a0 ** (1.0 / LRU_C)
    lru_lambda = jnp.log(a_root) - jnp.log1p(-a_root)
    return {
        "x": normal((BATCH, SEQ, D), 1.0),
        "mem": normal((BATCH, MEM_LEN, D), 1.0),
        "norm_mix": gain((L, D)),
        "w_in": normal((L, D, IN_COLS), D ** -0.5),
        "conv_w": normal((L, CONV_W, LRU_W), CONV_W ** -0.5),
        "conv_b": normal((L, LRU_W), 0.01),
        "lru_wa": normal((L, LRU_BLOCKS, LRU_BW, LRU_BW), LRU_BW ** -0.5),
        "lru_ba": normal((L, LRU_W), 0.01),
        "lru_wx": normal((L, LRU_BLOCKS, LRU_BW, LRU_BW), LRU_BW ** -0.5),
        "lru_bx": normal((L, LRU_W), 0.01),
        "lru_lambda": lru_lambda,
        "ca_rel_bias": normal((L, CA_HEADS, 2 * REL_CLIP + 1), 0.1),
        "diff_lambda": normal((L, 4, DIFF_HD), 0.1),
        "diff_subln": gain((L, DIFF_VD)),
        "w_branch": normal((L, N_BRANCH, BRANCH_W, D), BRANCH_W ** -0.5),
        "w_out": normal((L, D, D), D ** -0.5),
        "norm_mem": gain((L, D)),
        "mem_norm": gain((D,)),
        "w_mq": normal((L, D, MX_HEADS * MX_HD), D ** -0.5),
        "w_mk": normal((L, D, MX_HEADS * MX_HD), D ** -0.5),
        "w_mv": normal((L, D, MX_HEADS * MX_HD), D ** -0.5),
        "w_mo": normal((L, MX_HEADS * MX_HD, D), (MX_HEADS * MX_HD) ** -0.5),
        "norm_ffn": gain((L, D)),
        "w_group": normal((L, D, N_GROUPS), D ** -0.5),
        "b_group": normal((L, N_GROUPS), 0.01),
        "w_router": normal((L, D, N_EXPERTS), D ** -0.5),
        "b_router": normal((L, N_EXPERTS), 0.01),
        "w1": normal((L, N_EXPERTS, D, D_EXPERT), D ** -0.5),
        "w3": normal((L, N_EXPERTS, D, D_EXPERT), D ** -0.5),
        "w2": normal((L, N_EXPERTS, D_EXPERT, D), D_EXPERT ** -0.5),
        "final_norm": gain((D,)),
    }

def reference(x, mem, norm_mix, w_in, conv_w, conv_b, lru_wa, lru_ba, lru_wx, lru_bx, lru_lambda,
              ca_rel_bias, diff_lambda, diff_subln, w_branch, w_out, norm_mem, mem_norm,
              w_mq, w_mk, w_mv, w_mo, norm_ffn, w_group, b_group, w_router, b_router,
              w1, w3, w2, final_norm):
    b, n, d = x.shape
    mem_n = _rmsnorm(mem, mem_norm)
    for l in range(DEPTH):
        lam_init = 0.8 - 0.6 * math.exp(-0.3 * l)
        h = _rmsnorm(x, norm_mix[l])
        z = h @ w_in[l]
        (a_x, a_g, b_q, b_k, b_v, c_q, c_k, c_v, c_g, d_q, d_k, d_v, gates) = _split_columns(z)
        y_a = _rg_lru_branch(a_x, a_g, conv_w[l], conv_b[l], lru_wa[l], lru_ba[l], lru_wx[l], lru_bx[l], lru_lambda[l])
        y_b = _chunk_attention(b_q, b_k, b_v, ca_rel_bias[l])
        y_c = _retention(c_q, c_k, c_v, c_g)
        y_d = _diff_attention(d_q, d_k, d_v, diff_lambda[l], diff_subln[l], lam_init)
        ys = jnp.stack([y_a, y_b, y_c, y_d], axis=2)
        proj = jnp.einsum("bnkc,kcd->bnkd", ys, w_branch[l])
        g = jax.nn.sigmoid(gates.reshape(b, n, N_BRANCH, d))
        x = x + jnp.sum(g * proj, axis=2) @ w_out[l]
        x = x + _memory_cross_attention(_rmsnorm(x, norm_mem[l]), mem_n, w_mq[l], w_mk[l], w_mv[l], w_mo[l])
        x = x + _hier_moe(_rmsnorm(x, norm_ffn[l]), w_group[l], b_group[l], w_router[l], b_router[l], w1[l], w3[l], w2[l])
    return _rmsnorm(x, final_norm)


_drawn_inputs = setup_inputs


def setup_inputs(seed=0):
    import zlib

    import numpy as np

    out = dict(_drawn_inputs(seed))
    spreads = {}
    factors = {'lru_ba': 33.554,
     'lru_bx': 23.983,
     'ca_rel_bias': 3.897,
     'norm_mem': 2.972,
     'mem_norm': 3.164,
     'b_group': 32.711,
     'b_router': 19.302,
     'norm_ffn': 3.065}
    for name, (base, spread) in spreads.items():
        noise = np.random.default_rng([zlib.crc32(name.encode()), seed]).standard_normal(out[name].shape)
        drawn = base * np.exp(spread * noise) if base else spread * noise
        out[name] = __import__('jax').numpy.asarray(drawn.astype(out[name].dtype))
    for name, factor in factors.items():
        out[name] = (out[name] * factor).astype(out[name].dtype)
    return out
```

```python
from contextlib import ExitStack

import numpy as np

import concourse.bass as bass
from concourse import mybir

F32 = mybir.dt.float32
F32R = mybir.dt.float32r
U32 = mybir.dt.uint32
I32 = mybir.dt.int32
ALU = mybir.AluOpType
ACT = mybir.ActivationFunctionType
AX_X = mybir.AxisListType.X

P = 128
D = 1024
N = 512
CHUNK = 64
MEM = 256
KD = D // P
T = N // P
BW = 512
KB = BW // P
HD = 64
HEADS = 8
DIFF_HEADS = 4
REL_CLIP = 128
MX_HEADS = 4
GROUPS = 4
PER_GROUP = 8
EXPERTS = GROUPS * PER_GROUP
FF = 512
KF = FF // P
LAM_INIT = 0.2
NORM_EPS = 1e-6
GN_EPS = 1e-5
MASKED = -1e30
NO_SLOT = 1 << 20
SLOTS = 2 * N
LOGITS = GROUPS + EXPERTS
ROUTE_CONSTS = 2 * P + EXPERTS + 3 * P + 1
SMALL = 3 * KD + 8 * KB
ROWS = D + LOGITS + 2 * HD + 4 * HD
MAX_EXTRA = SLOTS // P - 1

AX0, AG0, BQ0, BK0, CQ0, CK0, DQ0, DK0 = (4 * i for i in range(8))
BV, CV, CG, DV = range(4)
FEAT_CHUNKS = 8
TOK_CHUNKS = 4


class Steps:

    def __init__(self, eng, sem):
        self.eng, self.sem, self.n = eng, sem, 0

    def after(self, ins):
        self.n += 1
        ins.then_inc(self.sem, 1)
        self.eng.wait_ge(self.sem, self.n)


def trunk(nc, a, out):
    stack = ExitStack()
    with stack:
        held = []

        def sem(name):
            held.append(nc.alloc_semaphore(name=name))
            return held[-1]

        def free_semaphores():
            nc.clear_and_free_semaphores(held)
            held.clear()
            nc.all_engine_barrier()

        def sbuf(ctx, name, shape, dt=F32):
            return ctx.enter_context(nc.sbuf_tensor(name, shape, dt))

        def psum(ctx, name, shape=(P, 512), dt=F32):
            return ctx.enter_context(nc.psum_tensor(name, list(shape), dt))

        xn_dram = nc.dram_tensor("xn_scratch", [SLOTS, D], F32).ap()
        ys_dram = nc.dram_tensor("ys_scratch", [SLOTS, D], F32).ap()
        list_dram = nc.dram_tensor("list_scratch", [EXPERTS * N, 1], I32).ap()
        rel_dram = nc.dram_tensor("rel_scratch", [HEADS, P, 5 * P], F32).ap()
        jobs_dram = nc.dram_tensor("jobs_scratch", [1, P], I32).ap()

        x_sb = sbuf(stack, "x_sb", [P, T, D])
        ident = sbuf(stack, "ident", [P, P])
        small = sbuf(stack, "small", [P, SMALL])
        rows = sbuf(stack, "rows", [P, ROWS])
        gain_mix, gain_mem, gain_memn = (small[:, KD * i:KD * (i + 1)] for i in range(3))
        s0 = 3 * KD
        conv_w = [small[:, s0 + KB * j:s0 + KB * (j + 1)] for j in range(4)]
        conv_b, lru_ba, lru_bx, lru_lam = (small[:, s0 + KB * j:s0 + KB * (j + 1)] for j in range(4, 8))
        final_gain = rows[:, 0:D]
        router_bias = rows[:, D:D + LOGITS]
        subln = rows[:, D + LOGITS:D + LOGITS + 2 * HD]
        lam_vecs = rows[:, D + LOGITS + 2 * HD:ROWS]

        s_start = stack.enter_context(nc.semaphore("s_start"))

        def rms_transposed(ctx, pfx, src, tiles, gain, dst, first=None, keep=None, gain_row=None):
            s_ss, s_ms, s_sq, s_rinv, s_xn = (sem(f"{pfx}_{n}") for n in ("ss", "ms", "sq", "rinv", "xn"))
            s_tp, s_ev = [sem(f"{pfx}_tp{i}") for i in range(2)], [sem(f"{pfx}_ev{i}") for i in range(2)]
            s_dve = sem(f"{pfx}_dve")
            with ExitStack() as c:
                junk = sbuf(c, pfx + "_junk", [P, D])
                ss = sbuf(c, pfx + "_sums", [P, tiles])
                xn = keep if keep is not None else sbuf(c, pfx + "_xn", [P, tiles, D])
                ps = [psum(c, f"{pfx}_ps{i}") for i in range(2)]
                block = c.enter_context(nc.Block())

                @block.sync
                def _(sp):
                    if first is not None:
                        first(sp)

                @block.scalar
                def _(act):
                    if first is not None:
                        act.wait_ge(s_start, first.ready)
                    for t in range(tiles):
                        if t:
                            act.wait_ge(s_ss, t)
                        nc.scalar.activation(junk[:], src[:, t, :], ACT.Square,
                                             accum_out=ss[:, t:t + 1]).then_inc(s_ss, 1)
                    act.wait_ge(s_ms, 1)
                    nc.scalar.activation(ss[:], ss[:], ACT.Sqrt).then_inc(s_sq, 1)
                    for k in range(1, KD, 2):
                        act.wait_ge(s_tp[1], k // 2 + 1)
                        nc.scalar.activation(dst[:, k, :], ps[1][:, 0:tiles * P], ACT.Copy,
                                             scale=1.0 if gain is None else gain[:, k:k + 1]
                                             ).then_inc(s_ev[1], 1)

                @block.vector
                def _(dve):
                    dve.wait_ge(s_ss, tiles)
                    nc.vector.tensor_scalar(ss[:], ss[:], 1.0 / D, NORM_EPS, ALU.mult, ALU.add).then_inc(s_ms, 1)
                    dve.wait_ge(s_sq, 1)
                    nc.vector.reciprocal(ss[:], ss[:]).then_inc(s_rinv, 1)
                    dve.wait_ge(s_rinv, 1)
                    if gain_row is not None:
                        dve.wait_ge(s_start, first.ready)
                    for t in range(tiles):
                        if gain_row is None:
                            nc.vector.tensor_scalar(xn[:, t, :], src[:, t, :], ss[:, t:t + 1], None,
                                                    ALU.mult).then_inc(s_xn, 1)
                        else:
                            nc.vector.scalar_tensor_tensor(xn[:, t, :], src[:, t, :], ss[:, t:t + 1], gain_row,
                                                           ALU.mult, ALU.mult).then_inc(s_xn, 1)
                    for k in range(0, KD, 2):
                        dve.wait_ge(s_tp[0], k // 2 + 1)
                        nc.vector.tensor_scalar(dst[:, k, :], ps[0][:, 0:tiles * P],
                                                1.0 if gain is None else gain[:, k:k + 1], None,
                                                ALU.mult).then_inc(s_ev[0], 1)

                @block.tensor
                def _(pe):
                    for k in range(KD):
                        pe.wait_ge(s_ev[k % 2], k // 2)
                        for t in range(tiles):
                            if k == 0:
                                pe.wait_ge(s_xn, t + 1)
                            last = nc.tensor.transpose(ps[k % 2][:, t * P:(t + 1) * P],
                                                       xn[:, t, k::KD], ident[:])
                        last.then_inc(s_tp[k % 2], 1)

        mix = ExitStack()
        hT = sbuf(mix, "hT", [P, KD, N])
        zT = sbuf(mix, "zT", [P, 4 * FEAT_CHUNKS, N])
        ztok = sbuf(mix, "ztok", [P, TOK_CHUNKS, T, BW])

        def load_first(sp):
            sp.dma_start(x_sb[:], a["x"].rearrange("b (t p) d -> p (b t) d", p=P)).then_inc(s_start, 16)
            sp.dma_start(ident[:], a["ident"]).then_inc(s_start, 16)
            sp.dma_start(small[:], a["small"]).then_inc(s_start, 16)
            sp.dma_start(rows[:], bass.AP(a["rows"].tensor, 0, [[0, P], [1, ROWS]])).then_inc(s_start, 16)
            sp.wait_ge(s_start, 64)

        load_first.ready = 64
        rms_transposed(stack, "rx", x_sb, T, gain_mix, hT, first=load_first)

        with ExitStack() as c:
            w_buf = [sbuf(c, f"wmix{b}", [P, KD, BW]) for b in range(2)]
            ps = [[psum(c, f"mix_ps{b}{j}") for j in range(4)] for b in range(2)]
            w_in_buf = [sem(f"mix_w{b}") for b in range(2)]
            z_done = [sem(f"mix_z{b}") for b in range(2)]
            z_out = [sem(f"mix_out{b}") for b in range(2)]
            w_mix = a["w_mix"].rearrange("c (p k) n -> c p k n", k=KD)
            FI, TI = FEAT_CHUNKS // 2, TOK_CHUNKS // 2
            block = c.enter_context(nc.Block())

            @block.sync
            def _(sp):
                for b in range(2):
                    sp.sem_inc(z_done[b], 4)
                    sp.sem_inc(z_out[b], 4)
                with sp.Fori(0, FI + TI) as i:
                    for b in range(2):
                        sp.wait_ge(z_done[b], i * 4 + 4)
                        sp.dma_start(w_buf[b][:], w_mix[bass.ds(i * 2 + b, 1)].rearrange(
                            "o p k n -> p (o k) n")).then_inc(w_in_buf[b], 16)

            @block.tensor
            def _(pe):
                with pe.Fori(0, FI) as i:
                    for b in range(2):
                        pe.wait_ge(w_in_buf[b], i * 16 + 16)
                        pe.wait_ge(z_out[b], i * 4 + 4)
                        for j in range(4):
                            for k in range(KD):
                                last = nc.tensor.matmul(ps[b][j][:], w_buf[b][:, k, j * P:(j + 1) * P],
                                                        hT[:, k, :], start=(k == 0), stop=(k == KD - 1))
                            last.then_inc(z_done[b], 1)
                with pe.Fori(0, TI) as i:
                    for b in range(2):
                        pe.wait_ge(w_in_buf[b], i * 16 + 16 * (FI + 1))
                        pe.wait_ge(z_out[b], i * 4 + 4 * (FI + 1))
                        for t in range(T):
                            for k in range(KD):
                                last = nc.tensor.matmul(ps[b][t][:], hT[:, k, t * P:(t + 1) * P],
                                                        w_buf[b][:, k, :], start=(k == 0), stop=(k == KD - 1))
                            last.then_inc(z_done[b], 1)

            def empty(eng, copy, odd):
                with eng.Fori(0, FI) as i:
                    for b in range(2):
                        for j in range(odd, 4, 2):
                            eng.wait_ge(z_done[b], i * 4 + (4 + j + 1))
                            copy(zT[:, bass.ds(i * 8 + (b * 4 + j), 1), :].rearrange("p o n -> p (o n)"),
                                 ps[b][j][:]).then_inc(z_out[b], 1)
                with eng.Fori(0, TI) as i:
                    for b in range(2):
                        for t in range(odd, 4, 2):
                            eng.wait_ge(z_done[b], i * 4 + (4 * (FI + 1) + t + 1))
                            copy(ztok[:, bass.ds(i * 2 + b, 1), t, :].rearrange("p o n -> p (o n)"),
                                 ps[b][t][:]).then_inc(z_out[b], 1)

            @block.scalar
            def _(act):
                empty(act, nc.scalar.copy, 0)

            @block.vector
            def _(dve):
                empty(dve, nc.vector.tensor_copy, 1)

        with ExitStack() as c:
            wa_sb = sbuf(c, "wa_sb", [P, KB, P])
            wx_sb = sbuf(c, "wx_sb", [P, KB, P])
            xc = sbuf(c, "xc", [P, KB, N])
            tr = sbuf(c, "tr", [P, KB, N])
            ti = sbuf(c, "ti", [P, KB, N])
            sq = sbuf(c, "sq", [P, KB, N])
            ge = sbuf(c, "ge", [P, KB, N])
            sp_lam = sbuf(c, "sp_lam", [P, 4, KB])
            psr = [psum(c, f"lru_r{i}") for i in range(4)]
            psi = [psum(c, f"lru_i{i}") for i in range(4)]
            s_w, s_xc, s_g, s_act, s_dve, s_sp, s_sq, s_in, s_th = (
                sem("lru_" + n) for n in ("w", "xc", "g", "act", "dve", "sp", "sq", "inner", "tanh"))
            s_e = sem("lru_e")
            ax, ag = zT[:, AX0:AX0 + KB, :], zT[:, AG0:AG0 + KB, :]
            GELU_C, GELU_S = 0.044715, float(np.sqrt(2.0 / np.pi))
            block = c.enter_context(nc.Block())

            @block.sync
            def _(sp):
                sp.dma_start(wa_sb[:], a["wa_bd"].rearrange("t c d -> c t d")).then_inc(s_w, 16)
                sp.dma_start(wx_sb[:], a["wx_bd"].rearrange("t c d -> c t d")).then_inc(s_w, 16)

            @block.tensor
            def _(pe):
                pe.wait_ge(s_w, 32)
                for t in range(KB):
                    pe.wait_ge(s_xc, t + 1)
                    nc.tensor.matmul(psr[t][:], wa_sb[:, t, :], xc[:, t, :], start=True, stop=True)
                    nc.tensor.matmul(psi[t][:], wx_sb[:, t, :], xc[:, t, :], start=True,
                                     stop=True).then_inc(s_g, 1)

            @block.scalar
            def _(act):
                nc.scalar.activation(sp_lam[:, 0, :], lru_lam, ACT.Abs).then_inc(s_e, 1)
                act.wait_ge(s_e, 1)
                nc.scalar.activation(sp_lam[:, 1, :], sp_lam[:, 0, :], ACT.Exp, scale=-1.0).then_inc(s_e, 1)
                act.wait_ge(s_in, 1)
                nc.scalar.activation(ge[:], ge[:], ACT.Tanh, scale=GELU_S).then_inc(s_th, 1)
                act.wait_ge(s_sp, 1)
                n = 0
                for t in range(KB):
                    act.wait_ge(s_g, t + 1)
                    nc.scalar.activation(tr[:, t, :], psr[t][:], ACT.Tanh, scale=0.5,
                                         bias=sp_lam[:, 2, t:t + 1]).then_inc(s_act, 1)
                    nc.scalar.activation(ti[:, t, :], psi[t][:], ACT.Tanh, scale=0.5,
                                         bias=sp_lam[:, 3, t:t + 1]).then_inc(s_act, 1)
                    n += 2
                    act.wait_ge(s_act, n)
                    nc.scalar.activation(tr[:, t, :], tr[:, t, :], ACT.Tanh, scale=sp_lam[:, 0, t:t + 1],
                                         bias=sp_lam[:, 0, t:t + 1]).then_inc(s_act, 1)
                    n += 1
                act.wait_ge(s_act, n)
                for t in range(KB):
                    nc.scalar.activation(sq[:, t, :], tr[:, t, :], ACT.Sqrt).then_inc(s_sq, 1)

            @block.vector
            def _(dve):
                do = Steps(dve, s_dve)
                for t in range(KB):
                    do.after(nc.vector.tensor_scalar(xc[:, t, :], ax[:, t, :], conv_w[3][:, t:t + 1],
                                                     conv_b[:, t:t + 1], ALU.mult, ALU.add))
                    for j in (2, 1, 0):
                        sh = 3 - j
                        ins = nc.vector.scalar_tensor_tensor(xc[:, t, sh:N], ax[:, t, 0:N - sh],
                                                             conv_w[j][:, t:t + 1], xc[:, t, sh:N],
                                                             ALU.mult, ALU.add)
                        if j:
                            do.after(ins)
                    ins.then_inc(s_xc, 1)
                do.after(nc.vector.tensor_tensor(ge[:], ag, ag, ALU.mult))
                do.after(nc.vector.tensor_scalar(ge[:], ge[:], GELU_C, 1.0, ALU.mult, ALU.add))
                nc.vector.tensor_tensor(ge[:], ge[:], ag, ALU.mult).then_inc(s_in, 1)
                dve.wait_ge(s_e, 2)
                e, s1, s2 = sp_lam[:, 1, :], sp_lam[:, 2, :], sp_lam[:, 3, :]
                acc = sp_lam[:, 0, :]
                do.after(nc.vector.tensor_scalar(s1, e, 2.0, None, ALU.add))
                do.after(nc.vector.reciprocal(s1, s1))
                do.after(nc.vector.tensor_tensor(s1, s1, e, ALU.mult))
                do.after(nc.vector.tensor_tensor(s2, s1, s1, ALU.mult))
                do.after(nc.vector.tensor_scalar(acc, s2, 1.0 / 17, 1.0 / 15, ALU.mult, ALU.add))
                for m in (13, 11, 9, 7, 5, 3, 1):
                    do.after(nc.vector.tensor_tensor(acc, acc, s2, ALU.mult))
                    do.after(nc.vector.tensor_scalar(acc, acc, 1.0 / m, None, ALU.add))
                do.after(nc.vector.tensor_tensor(acc, acc, s1, ALU.mult))
                do.after(nc.vector.tensor_scalar(s1, lru_lam, -1.0, 0.0, ALU.mult, ALU.max))
                do.after(nc.vector.scalar_tensor_tensor(acc, acc, 2.0, s1, ALU.mult, ALU.add))
                do.after(nc.vector.tensor_scalar(acc, acc, 2.0, None, ALU.mult))
                do.after(nc.vector.tensor_scalar(s1, lru_ba, 0.5, None, ALU.mult))
                nc.vector.tensor_scalar(s2, lru_bx, 0.5, None, ALU.mult).then_inc(s_sp, 1)
                dve.wait_ge(s_th, 1)
                do.after(nc.vector.scalar_tensor_tensor(ge[:], ge[:], 1.0, ag, ALU.add, ALU.mult))
                for t in range(KB):
                    dve.wait_ge(s_sq, t + 1)
                    do.after(nc.vector.tensor_scalar(tr[:, t, :], tr[:, t, :], 1.0, None, ALU.add))
                    do.after(nc.vector.reciprocal(tr[:, t, :], tr[:, t, :]))
                    do.after(nc.vector.tensor_tensor(sq[:, t, :], sq[:, t, :], tr[:, t, :], ALU.mult))
                    do.after(nc.vector.tensor_scalar(tr[:, t, :], tr[:, t, :], 2.0, -1.0, ALU.mult, ALU.add))
                    do.after(nc.vector.scalar_tensor_tensor(ti[:, t, :], ti[:, t, :], 1.0, xc[:, t, :],
                                                            ALU.add, ALU.mult))
                    do.after(nc.vector.tensor_tensor(sq[:, t, :], sq[:, t, :], ti[:, t, :], ALU.mult))
                    do.after(nc.vector.tensor_tensor_scan(xc[:, t, :], tr[:, t, :], sq[:, t, :], 0.0,
                                                          ALU.mult, ALU.add))
                    do.after(nc.vector.scalar_tensor_tensor(ax[:, t, :], xc[:, t, :], 0.5, ge[:, t, :],
                                                            ALU.mult, ALU.mult))

        def to_feature_major(pe, dve, pfx, s_y, s_tp, s_ev, src, dst0, ps, ready):
            if pe is not None:
                pe.wait_ge(s_y, ready)
                for k in range(KB):
                    if k >= 2:
                        pe.wait_ge(s_ev, k - 1)
                    for t in range(T):
                        last = nc.tensor.transpose(ps[k % 2][:, t * P:(t + 1) * P],
                                                   src[:, t, k * P:(k + 1) * P], ident[:])
                    last.then_inc(s_tp, 1)
            else:
                for k in range(KB):
                    dve.wait_ge(s_tp, k + 1)
                    nc.vector.tensor_copy(zT[:, dst0 + k, :], ps[k % 2][:]).then_inc(s_ev, 1)

        with ExitStack() as c:
            bias = sbuf(c, "rel_bias", [P, HEADS, N])
            rel = sbuf(c, "rel_row", [HEADS, 5 * P])
            neg = [sbuf(c, f"b_neg{i}", [P, N]) for i in range(2)]
            pr = [sbuf(c, f"b_p{i}", [P, N]) for i in range(3)]
            pT = [sbuf(c, f"b_pT{i}", [P, N]) for i in range(2)]
            otok = sbuf(c, "b_otok", [P, T, BW])
            nmax = sbuf(c, "b_nmax", [P, HEADS * T])
            rsum = sbuf(c, "b_rsum", [P, HEADS * T])
            ps_s = [psum(c, f"b_s{i}") for i in range(3)]
            ps_t = [psum(c, f"b_t{i}") for i in range(2)]
            ps_o = [psum(c, f"b_o{i}") for i in range(2)]
            s_rel, s_ext, s_wr, s_bias, s_mask, s_s, s_neg, s_exp, s_t, s_pt, s_pv, s_o, s_dve, s_tp, s_ev = (
                sem("b_" + n) for n in ("rel", "ext", "wr", "bias", "mask", "s", "neg", "exp", "t", "pt", "pv",
                                        "o", "dve", "tp", "ev"))
            U = HEADS * T
            FAR = N - 1 - REL_CLIP
            SC = float(HD) ** -0.5
            block = c.enter_context(nc.Block())

            @block.sync
            def _(sp):
                sp.dma_start(rel[:, FAR:FAR + 2 * REL_CLIP + 1], a["rel_flipped"]).then_inc(s_rel, 16)
                sp.wait_ge(s_ext, 3)
                sp.dma_start(rel_dram, rel[:].unsqueeze(1).to_broadcast([HEADS, P, 5 * P])).then_inc(s_wr, 16)
                sp.wait_ge(s_wr, 16)
                for h in range(HEADS):
                    sp.dma_start(bias[:, h, :], bass.AP(rel_dram.tensor, h * P * 5 * P + P - 1,
                                                        [[5 * P - 1, P], [1, N]])).then_inc(s_bias, 16)

            @block.gpsimd
            def _(pool):
                pool.wait_ge(s_bias, 16 * HEADS)
                nc.gpsimd.memset(bias[0:CHUNK, :, N - CHUNK:N], MASKED).then_inc(s_mask, 1)

            @block.tensor
            def _(pe):
                for st in range(U + 3):
                    if st < U:
                        h, t = divmod(st, T)
                        lo = (h % 2) * HD
                        if st >= 3:
                            pe.wait_ge(s_neg, st - 2)
                        nc.tensor.matmul(ps_s[st % 3][:, 0:(t + 1) * P],
                                         zT[lo:lo + HD, BQ0 + h // 2, t * P:(t + 1) * P],
                                         zT[lo:lo + HD, BK0 + h // 2, 0:(t + 1) * P],
                                         start=True, stop=True).then_inc(s_s, 1)
                    if 0 <= st - 2 < U:
                        u = st - 2
                        pe.wait_ge(s_exp, u + 1)
                        if u >= 2:
                            pe.wait_ge(s_pt, u - 1)
                        for b in range(u % T + 1):
                            last = nc.tensor.transpose(ps_t[u % 2][:, b * P:(b + 1) * P],
                                                       pr[u % 3][:, b * P:(b + 1) * P], ident[:])
                        last.then_inc(s_t, 1)
                    if 0 <= st - 3:
                        u = st - 3
                        h, t = divmod(u, T)
                        pe.wait_ge(s_pt, u + 1)
                        if t == 0 and h >= 2:
                            pe.wait_ge(s_o, h - 1)
                        for b in range(t + 1):
                            last = nc.tensor.matmul(ps_o[h % 2][:, t * HD:(t + 1) * HD],
                                                    pT[u % 2][:, b * P:(b + 1) * P],
                                                    ztok[:, BV, b, h * HD:(h + 1) * HD],
                                                    start=(b == 0), stop=(b == t))
                        last.then_inc(s_pv, 1)
                to_feature_major(pe, None, "b", s_o, s_tp, s_ev, otok, BQ0, ps_t, HEADS)

            @block.scalar
            def _(act):
                for u in range(U):
                    w = (u % T + 1) * P
                    act.wait_ge(s_neg, u + 1)
                    if u >= 3:
                        act.wait_ge(s_t, u - 2)
                    nc.scalar.activation(pr[u % 3][:, 0:w], neg[u % 2][:, 0:w], ACT.Exp, scale=-1.0,
                                         bias=nmax[:, u:u + 1], accum_out=rsum[:, u:u + 1]).then_inc(s_exp, 1)

            @block.vector
            def _(dve):
                do = Steps(dve, s_dve)
                dve.wait_ge(s_rel, 16)
                nc.vector.memset(rel[:, 0:FAR], 0.0).then_inc(s_ext, 1)
                dve.wait_ge(s_ext, 1)
                nc.vector.tensor_scalar(rel[:, 0:FAR], rel[:, 0:FAR], rel[:, FAR:FAR + 1], None,
                                        ALU.add).then_inc(s_ext, 1)
                dve.wait_ge(s_ext, 2)
                nc.vector.tensor_scalar(rel[:], rel[:], 1.0 / SC, None, ALU.mult).then_inc(s_ext, 1)
                dve.wait_ge(s_mask, 1)
                for st in range(U + 4):
                    if st < U:
                        h, t = divmod(st, T)
                        w = (t + 1) * P
                        dve.wait_ge(s_s, st + 1)
                        if st >= 2:
                            dve.wait_ge(s_exp, st - 1)
                        nc.vector.tensor_tensor_reduce(neg[st % 2][:, 0:w], ps_s[st % 3][:, 0:w],
                                                       bias[:, h, N - w:N], -SC, 3e38, ALU.add, ALU.min,
                                                       nmax[:, st:st + 1]).then_inc(s_neg, 1)
                    if 0 <= st - 2 < U:
                        u = st - 2
                        w = (u % T + 1) * P
                        dve.wait_ge(s_t, u + 1)
                        if u >= 2:
                            dve.wait_ge(s_pv, u - 1)
                        nc.vector.tensor_copy(pT[u % 2][:, 0:w], ps_t[u % 2][:, 0:w]).then_inc(s_pt, 1)
                    if st >= 4 and (st - 4) % T == T - 1:
                        h = (st - 4) // T
                        rs = rsum[:, h * T:(h + 1) * T]
                        dve.wait_ge(s_pv, h * T + T)
                        do.after(nc.vector.reciprocal(rs, rs))
                        nc.vector.tensor_tensor(otok[:, :, h * HD:(h + 1) * HD],
                                                ps_o[h % 2][:, 0:T * HD].rearrange("p (t e) -> p t e", t=T),
                                                rs.unsqueeze(2).to_broadcast([P, T, HD]),
                                                ALU.mult).then_inc(s_o, 1)
                to_feature_major(None, dve, "b", s_o, s_tp, s_ev, otok, BQ0, ps_t, HEADS)

        with ExitStack() as c:
            decay = sbuf(c, "decay", [P, HEADS, N])
            pd = [sbuf(c, f"c_p{i}", [P, 10 * P]) for i in range(2)]
            otok = sbuf(c, "c_otok", [P, T, BW])
            tmp = sbuf(c, "c_tmp", [P, T, BW])
            gate = sbuf(c, "c_gate", [P, T, BW])
            mu = sbuf(c, "c_mu", [P, T * HEADS])
            var = sbuf(c, "c_var", [P, T * HEADS])
            ps_s = [psum(c, f"c_s{i}") for i in range(4)]
            ps_o = [psum(c, f"c_o{i}") for i in range(2)]
            ps_t = [psum(c, f"c_t{i}") for i in range(2)]
            s_ld, s_s, s_p, s_pv, s_o, s_dve, s_v, s_sq, s_th, s_y, s_tp, s_ev = (
                sem("c_" + n) for n in ("ld", "s", "p", "pv", "o", "dve", "var", "sqrt", "tanh", "y", "tp", "ev"))
            off = [0, 4 * P, 7 * P, 9 * P]
            block = c.enter_context(nc.Block())

            @block.sync
            def _(sp):
                sp.dma_start(decay[:], a["decay"]).then_inc(s_ld, 16)

            @block.tensor
            def _(pe):
                def scores(h):
                    lo = (h % 2) * HD
                    for j in range(T):
                        u = h * T + j
                        if u >= 4:
                            pe.wait_ge(s_p, u - 3)
                        nc.tensor.matmul(ps_s[j][:, 0:N - j * P],
                                         zT[lo:lo + HD, CK0 + h // 2, j * P:(j + 1) * P],
                                         zT[lo:lo + HD, CQ0 + h // 2, j * P:N],
                                         start=True, stop=True).then_inc(s_s, 1)

                def outputs(h):
                    if h >= 2:
                        pe.wait_ge(s_o, h - 1)
                    pe.wait_ge(s_p, h * T + T)
                    for i in range(T):
                        for j in range(i + 1):
                            o = off[j] + (i - j) * P
                            last = nc.tensor.matmul(ps_o[h % 2][:, i * HD:(i + 1) * HD],
                                                    pd[h % 2][:, o:o + P],
                                                    ztok[:, CV, j, h * HD:(h + 1) * HD],
                                                    start=(j == 0), stop=(j == i))
                    last.then_inc(s_pv, 1)

                for st in range(HEADS + 1):
                    if st < HEADS:
                        scores(st)
                    if st:
                        outputs(st - 1)
                to_feature_major(pe, None, "c", s_y, s_tp, s_ev, otok, CQ0, ps_t, 1)

            @block.scalar
            def _(act):
                nc.scalar.activation(gate[:], ztok[:, CG, :, :], ACT.Tanh, scale=0.5).then_inc(s_th, 1)
                act.wait_ge(s_v, 1)
                nc.scalar.activation(var[:], var[:], ACT.Sqrt).then_inc(s_sq, 1)

            @block.vector
            def _(dve):
                do = Steps(dve, s_dve)
                dve.wait_ge(s_ld, 16)
                for st in range(HEADS + 1):
                    if st < HEADS:
                        if st >= 2:
                            dve.wait_ge(s_pv, st - 1)
                        for j in range(T):
                            dve.wait_ge(s_s, st * T + j + 1)
                            nc.vector.tensor_tensor(pd[st % 2][:, off[j]:off[j] + N - j * P],
                                                    ps_s[j][:, 0:N - j * P], decay[:, st, 0:N - j * P],
                                                    ALU.mult).then_inc(s_p, 1)
                    if st:
                        h = st - 1
                        dve.wait_ge(s_pv, h + 1)
                        nc.vector.tensor_copy(otok[:, :, h * HD:(h + 1) * HD],
                                              ps_o[h % 2][:, 0:T * HD].rearrange("p (t e) -> p t e", t=T)
                                              ).then_inc(s_o, 1)
                dve.wait_ge(s_o, HEADS)
                o3 = otok[:].rearrange("p t (h e) -> p (t h) e", e=HD)
                t3 = tmp[:].rearrange("p t (h e) -> p (t h) e", e=HD)
                wide = [P, T * HEADS, HD]
                do.after(nc.vector.tensor_reduce(mu[:], o3, AX_X, ALU.add))
                do.after(nc.vector.tensor_scalar(mu[:], mu[:], 1.0 / HD, None, ALU.mult))
                do.after(nc.vector.tensor_tensor(o3, o3, mu[:].unsqueeze(2).to_broadcast(wide), ALU.subtract))
                do.after(nc.vector.tensor_tensor(t3, o3, o3, ALU.mult))
                do.after(nc.vector.tensor_reduce(var[:], t3, AX_X, ALU.add))
                nc.vector.tensor_scalar(var[:], var[:], 1.0 / HD, GN_EPS, ALU.mult, ALU.add).then_inc(s_v, 1)
                dve.wait_ge(s_th, 1)
                do.after(nc.vector.scalar_tensor_tensor(gate[:], gate[:], 1.0, ztok[:, CG, :, :],
                                                        ALU.add, ALU.mult))
                dve.wait_ge(s_sq, 1)
                do.after(nc.vector.reciprocal(var[:], var[:]))
                do.after(nc.vector.tensor_tensor(o3, o3, var[:].unsqueeze(2).to_broadcast(wide), ALU.mult))
                nc.vector.scalar_tensor_tensor(otok[:], otok[:], 0.5, gate[:], ALU.mult, ALU.mult
                                               ).then_inc(s_y, 1)
                to_feature_major(None, dve, "c", s_y, s_tp, s_ev, otok, CQ0, ps_t, 1)

        with ExitStack() as c:
            alibi = sbuf(c, "alibi", [P, DIFF_HEADS, N])
            neg = [[sbuf(c, f"d_neg{i}{m}", [P, N]) for m in range(2)] for i in range(2)]
            pr = [[sbuf(c, f"d_p{i}{m}", [P, N]) for m in range(2)] for i in range(2)]
            pT = [sbuf(c, f"d_pT{i}", [P, N]) for i in range(2)]
            otok = sbuf(c, "d_otok", [P, T, BW])
            tmp = sbuf(c, "d_tmp", [P, T, BW])
            U = DIFF_HEADS * T
            nmax = sbuf(c, "d_nmax", [P, 2, U])
            rsum = sbuf(c, "d_rsum", [P, 2, U])
            coef = sbuf(c, "d_coef", [P, U])
            lam = sbuf(c, "d_lam", [P, 4])
            lamt = sbuf(c, "d_lamt", [P, HD])
            ms = sbuf(c, "d_ms", [P, U])
            ps_s = [[psum(c, f"d_s{i}{m}") for m in range(2)] for i in range(2)]
            ps_t = [psum(c, f"d_t{i}") for i in range(2)]
            ps_o = [psum(c, f"d_o{i}") for i in range(2)]
            s_ld, s_s, s_neg, s_exp, s_at, s_t, s_pt, s_pv, s_o, s_dve, s_lam, s_le, s_v, s_sq, s_y, s_tp, s_ev = (
                sem("d_" + n) for n in ("ld", "s", "neg", "exp", "attn", "t", "pt", "pv", "o", "dve", "lam", "lexp",
                                        "var", "sqrt", "y", "tp", "ev"))
            SC = float(HD) ** -0.5
            block = c.enter_context(nc.Block())

            @block.sync
            def _(sp):
                sp.dma_start(alibi[:], a["alibi"]).then_inc(s_ld, 16)

            @block.tensor
            def _(pe):
                for st in range(U + 3):
                    if st < U:
                        h, t = divmod(st, T)
                        if st >= 2:
                            pe.wait_ge(s_neg, 2 * (st - 1))
                        for m in range(2):
                            nc.tensor.matmul(ps_s[st % 2][m][:, 0:(t + 1) * P],
                                             zT[m * HD:(m + 1) * HD, DQ0 + h, t * P:(t + 1) * P],
                                             zT[m * HD:(m + 1) * HD, DK0 + h, 0:(t + 1) * P],
                                             start=True, stop=True).then_inc(s_s, 1)
                    if 0 <= st - 2 < U:
                        u = st - 2
                        pe.wait_ge(s_at, u + 1)
                        if u >= 2:
                            pe.wait_ge(s_pt, u - 1)
                        for b in range(u % T + 1):
                            last = nc.tensor.transpose(ps_t[u % 2][:, b * P:(b + 1) * P],
                                                       pr[u % 2][0][:, b * P:(b + 1) * P], ident[:])
                        last.then_inc(s_t, 1)
                    if 0 <= st - 3:
                        u = st - 3
                        h, t = divmod(u, T)
                        pe.wait_ge(s_pt, u + 1)
                        if t == 0 and h >= 2:
                            pe.wait_ge(s_o, h - 1)
                        for b in range(t + 1):
                            last = nc.tensor.matmul(ps_o[h % 2][:, t * P:(t + 1) * P],
                                                    pT[u % 2][:, b * P:(b + 1) * P],
                                                    ztok[:, DV, b, h * P:(h + 1) * P],
                                                    start=(b == 0), stop=(b == t))
                        last.then_inc(s_pv, 1)
                to_feature_major(pe, None, "d", s_y, s_tp, s_ev, otok, DQ0, ps_t, 1)

            @block.scalar
            def _(act):
                act.wait_ge(s_lam, 1)
                nc.scalar.activation(lam[:, 0:2], lam[:, 0:2], ACT.Exp).then_inc(s_le, 1)
                for u in range(U):
                    w = (u % T + 1) * P
                    if u >= 2:
                        act.wait_ge(s_t, u - 1)
                    for m in range(2):
                        act.wait_ge(s_neg, 2 * u + m + 1)
                        nc.scalar.activation(pr[u % 2][m][:, 0:w], neg[u % 2][m][:, 0:w], ACT.Exp, scale=-1.0,
                                             bias=nmax[:, m, u:u + 1],
                                             accum_out=rsum[:, m, u:u + 1]).then_inc(s_exp, 1)
                act.wait_ge(s_v, 1)
                nc.scalar.activation(ms[:], ms[:], ACT.Sqrt).then_inc(s_sq, 1)

            @block.vector
            def _(dve):
                do = Steps(dve, s_dve)
                for i in range(2):
                    ins = nc.vector.tensor_tensor_reduce(lamt[:], lam_vecs[:, 2 * i * HD:(2 * i + 1) * HD],
                                                         lam_vecs[:, (2 * i + 1) * HD:(2 * i + 2) * HD],
                                                         1.0, 0.0, ALU.mult, ALU.add, lam[:, i:i + 1])
                    if i == 0:
                        do.after(ins)
                ins.then_inc(s_lam, 1)
                dve.wait_ge(s_le, 1)
                do.after(nc.vector.tensor_tensor(lam[:, 2:3], lam[:, 1:2], lam[:, 0:1], ALU.subtract))
                do.after(nc.vector.tensor_scalar(lam[:, 3:4], lam[:, 2:3], -LAM_INIT, None, ALU.add))
                dve.wait_ge(s_ld, 16)
                for st in range(U + 4):
                    if st < U:
                        h, t = divmod(st, T)
                        w = (t + 1) * P
                        if st >= 2:
                            dve.wait_ge(s_exp, 2 * (st - 1))
                        for m in range(2):
                            dve.wait_ge(s_s, 2 * st + m + 1)
                            nc.vector.tensor_tensor_reduce(neg[st % 2][m][:, 0:w], ps_s[st % 2][m][:, 0:w],
                                                           alibi[:, h, N - w:N], -SC, 3e38, ALU.add, ALU.min,
                                                           nmax[:, m, st:st + 1]).then_inc(s_neg, 1)
                    if 0 <= st - 1 < U:
                        u = st - 1
                        w = (u % T + 1) * P
                        dve.wait_ge(s_exp, 2 * u + 2)
                        do.after(nc.vector.reciprocal(coef[:, u:u + 1], rsum[:, 1, u:u + 1]))
                        do.after(nc.vector.tensor_scalar(coef[:, u:u + 1], coef[:, u:u + 1],
                                                         rsum[:, 0, u:u + 1], lam[:, 3:4], ALU.mult, ALU.mult))
                        nc.vector.scalar_tensor_tensor(pr[u % 2][0][:, 0:w], pr[u % 2][1][:, 0:w],
                                                       coef[:, u:u + 1], pr[u % 2][0][:, 0:w],
                                                       ALU.mult, ALU.add).then_inc(s_at, 1)
                    if 0 <= st - 2 < U:
                        u = st - 2
                        w = (u % T + 1) * P
                        dve.wait_ge(s_t, u + 1)
                        if u >= 2:
                            dve.wait_ge(s_pv, u - 1)
                        nc.vector.tensor_copy(pT[u % 2][:, 0:w], ps_t[u % 2][:, 0:w]).then_inc(s_pt, 1)
                    if st >= 4 and (st - 4) % T == T - 1:
                        h = (st - 4) // T
                        rs = rsum[:, 0, h * T:(h + 1) * T]
                        dve.wait_ge(s_pv, h * T + T)
                        do.after(nc.vector.reciprocal(rs, rs))
                        nc.vector.tensor_tensor(otok[:, :, h * P:(h + 1) * P],
                                                ps_o[h % 2][:].rearrange("p (t e) -> p t e", t=T),
                                                rs.unsqueeze(2).to_broadcast([P, T, P]),
                                                ALU.mult).then_inc(s_o, 1)
                dve.wait_ge(s_o, DIFF_HEADS)
                o3 = otok[:].rearrange("p t (h e) -> p (t h) e", e=P)
                t3 = tmp[:].rearrange("p t (h e) -> p (t h) e", e=P)
                wide = [P, U, P]
                do.after(nc.vector.tensor_tensor(t3, o3, o3, ALU.mult))
                do.after(nc.vector.tensor_reduce(ms[:], t3, AX_X, ALU.add))
                nc.vector.tensor_scalar(ms[:], ms[:], 1.0 / P, GN_EPS, ALU.mult, ALU.add).then_inc(s_v, 1)
                dve.wait_ge(s_sq, 1)
                do.after(nc.vector.reciprocal(ms[:], ms[:]))
                do.after(nc.vector.tensor_scalar(ms[:], ms[:], 1.0 - LAM_INIT, None, ALU.mult))
                do.after(nc.vector.tensor_tensor(o3, o3, ms[:].unsqueeze(2).to_broadcast(wide), ALU.mult))
                nc.vector.tensor_tensor(o3, o3, subln.unsqueeze(1).to_broadcast(wide), ALU.mult).then_inc(s_y, 1)
                to_feature_major(None, dve, "d", s_y, s_tp, s_ev, otok, DQ0, ps_t, 1)

        with ExitStack() as c:
            merged = sbuf(c, "merged", [P, KD, N])
            wg = [sbuf(c, f"g_w{b}", [P, KD, 4 * P]) for b in range(2)]
            wb = [sbuf(c, f"g_b{b}", [P, 4 * KB, P]) for b in range(2)]
            tg = [sbuf(c, f"g_t{b}", [P, N]) for b in range(4)]
            Y0 = (AX0, BQ0, CQ0, DQ0)
            w_gate = a["w_gate"].rearrange("t (p k) n -> t p k n", k=KD)
            w_br = a["w_branch"].rearrange("l b (k p) (t n) -> t p (l b k) n", p=P, n=P)
            HALF = KD // 2
            with ExitStack() as c2:
                ps_g = [psum(c2, f"g_g{b}") for b in range(4)]
                ps_b = [psum(c2, f"g_p{b}") for b in range(4)]
                w_in_buf = [sem(f"g_in{b}") for b in range(2)]
                s_g, s_t, s_m = ([sem(f"g_{n}{b}") for b in range(4)] for n in ("gate", "tanh", "merge"))
                s_p = [sem(f"g_proj{b}") for b in range(3)]
                s_p3 = [sem(f"g_proj3_{b}") for b in range(2)]
                s_pair = sem("g_pair")
                block = c2.enter_context(nc.Block())

                @block.sync
                def _(sp):
                    for q in (*s_p3, *s_t, *s_m):
                        sp.sem_inc(q, 1)
                    with sp.Fori(0, HALF) as i:
                        for b in range(2):
                            sp.wait_ge(s_p3[b], i + 1)
                            sp.dma_start(wg[b][:], w_gate[bass.ds(i * 2 + b, 1)].rearrange(
                                "o p k n -> p (o k) n")).then_inc(w_in_buf[b], 16)
                            sp.dma_start(wb[b][:], w_br[bass.ds(i * 2 + b, 1)].rearrange(
                                "o p k n -> p (o k) n")).then_inc(w_in_buf[b], 16)

                @block.tensor
                def _(pe):
                    with pe.Fori(0, HALF) as i:
                        for b in range(2):
                            pe.wait_ge(w_in_buf[b], i * 32 + 32)
                            for br in range(4):
                                pe.wait_ge(s_t[br], i * 2 + (b + 1))
                                for k in range(KD):
                                    last = nc.tensor.matmul(ps_g[br][:], wg[b][:, k, br * P:(br + 1) * P],
                                                            hT[:, k, :], start=(k == 0), stop=(k == KD - 1))
                                last.then_inc(s_g[br], 1)
                                pe.wait_ge(s_m[br], i * 2 + (b + 1))
                                for k in range(KB):
                                    last = nc.tensor.matmul(ps_b[br][:], wb[b][:, br * KB + k, :],
                                                            zT[:, Y0[br] + k, :],
                                                            start=(k == 0), stop=(k == KB - 1))
                                last.then_inc(s_p[br] if br < 3 else s_p3[b], 1)

                @block.scalar
                def _(act):
                    with act.Fori(0, KD) as i:
                        for br in range(4):
                            act.wait_ge(s_g[br], i + 1)
                            act.wait_ge(s_m[br], i + 1)
                            nc.scalar.activation(tg[br][:], ps_g[br][:], ACT.Tanh, scale=0.5
                                                 ).then_inc(s_t[br], 1)

                @block.vector
                def _(dve):
                    with dve.Fori(0, HALF) as i:
                        for b in range(2):
                            m = merged[:, bass.ds(i * 2 + b, 1), :].rearrange("p o n -> p (o n)")
                            for br in range(4):
                                dve.wait_ge(s_t[br], i * 2 + (b + 2))
                                if br < 3:
                                    dve.wait_ge(s_p[br], i * 2 + (b + 1))
                                else:
                                    dve.wait_ge(s_p3[b], i + 2)
                                nc.vector.scalar_tensor_tensor(m if br == 0 else tg[br][:], tg[br][:], 1.0,
                                                               ps_b[br][:], ALU.add, ALU.mult
                                                               ).then_inc(s_m[0] if br == 0 else s_pair, 1)
                                if br:
                                    dve.wait_ge(s_pair, i * 6 + (3 * b + br))
                                    dve.wait_ge(s_m[br - 1], i * 2 + (b + 2))
                                    nc.vector.tensor_tensor(m, m, tg[br][:], ALU.add).then_inc(s_m[br], 1)

            with ExitStack() as c2:
                w_o = [wg[0], wg[1]]
                ps = [psum(c2, f"o_ps{i}") for i in range(4)]
                s_w = [sem(f"o_w{h}") for h in range(2)]
                s_ps, s_x = sem("o_ps"), sem("o_x")
                block = c2.enter_context(nc.Block())

                @block.sync
                def _(sp):
                    for h in range(2):
                        sp.dma_start(w_o[h][:], a["w_out"].rearrange("l (k p) n -> p (l k) n", p=P)[
                            :, :, h * BW:(h + 1) * BW]).then_inc(s_w[h], 16)

                @block.tensor
                def _(pe):
                    for h in range(2):
                        pe.wait_ge(s_w[h], 16)
                        for t in range(T):
                            if h:
                                pe.wait_ge(s_x, t + 1)
                            for k in range(KD):
                                last = nc.tensor.matmul(ps[t][:], merged[:, k, t * P:(t + 1) * P],
                                                        w_o[h][:, k, :], start=(k == 0), stop=(k == KD - 1))
                            last.then_inc(s_ps, 1)

                @block.vector
                def _(dve):
                    for h in range(2):
                        for t in range(T):
                            dve.wait_ge(s_ps, h * T + t + 1)
                            xs = x_sb[:, t, h * BW:(h + 1) * BW]
                            nc.vector.scalar_tensor_tensor(xs, ps[t][:], 0.5, xs, ALU.mult, ALU.add
                                                           ).then_inc(s_x, 1)
        mix.close()
        free_semaphores()

        with ExitStack() as c:
            h2T = sbuf(c, "h2T", [P, KD, N])
            memT = sbuf(c, "memT", [P, KD, MEM])
            mem_sb = sbuf(c, "mem_sb", [P, MEM // P, D])
            s_mem = sem("mem_in")

            def load_mem(sp):
                sp.dma_start(mem_sb[:], a["mem"].rearrange("b (t p) d -> p (b t) d", p=P)).then_inc(s_start, 16)
                sp.wait_ge(s_start, 80)

            load_mem.ready = 80
            rms_transposed(c, "rm", mem_sb, MEM // P, gain_memn, memT, first=load_mem)
            rms_transposed(c, "rh", x_sb, T, gain_mem, h2T)
            w = {n: sbuf(c, "m_" + n, [P, KD, BW]) for n in ("w_mq", "w_mk", "w_mv")}
            wo = sbuf(c, "m_wo", [P, KB, D])
            qT = sbuf(c, "m_qT", [P, MX_HEADS, N])
            kT = sbuf(c, "m_kT", [P, MX_HEADS, MEM])
            v = sbuf(c, "m_v", [P, MEM // P, BW])
            oT = sbuf(c, "m_oT", [P, MX_HEADS, N])
            pr = [sbuf(c, f"m_p{i}", [P, MEM]) for i in range(3)]
            pT = [sbuf(c, f"m_pT{i}", [P, MEM // P, N]) for i in range(2)]
            U = MX_HEADS * T
            nmax, rsum = sbuf(c, "m_nmax", [P, U]), sbuf(c, "m_rsum", [P, U])
            MT = MEM // P
            SC = float(P) ** -0.5
            with ExitStack() as c2:
                ps = [psum(c2, f"mq{i}") for i in range(4)]
                s_w = {n: sem("m_in_" + n) for n in w}
                s_ps, s_out = sem("m_ps"), sem("m_out")
                block = c2.enter_context(nc.Block())
                groups = [("q", h) for h in range(MX_HEADS)] + [("k", h) for h in range(MX_HEADS)] + [
                    ("v", t) for t in range(MT)]

                @block.sync
                def _(sp):
                    for n in w:
                        sp.dma_start(w[n][:], a[n].rearrange("l (p k) n -> p (l k) n", k=KD)
                                     ).then_inc(s_w[n], 16)

                @block.tensor
                def _(pe):
                    for g, (kind, h) in enumerate(groups):
                        if h == 0:
                            pe.wait_ge(s_w["w_m" + kind], 16)
                        if g >= 4:
                            pe.wait_ge(s_out, g - 3)
                        for k in range(KD):
                            if kind == "v":
                                lhs, rhs, n = memT[:, k, h * P:(h + 1) * P], w["w_mv"][:, k, :], BW
                            else:
                                lhs = w["w_m" + kind][:, k, h * P:(h + 1) * P]
                                rhs, n = (h2T[:, k, :], N) if kind == "q" else (memT[:, k, :], MEM)
                            last = nc.tensor.matmul(ps[g % 4][:, 0:n], lhs, rhs, start=(k == 0),
                                                    stop=(k == KD - 1))
                        last.then_inc(s_ps, 1)

                @block.vector
                def _(dve):
                    for g, (kind, h) in enumerate(groups):
                        dst = {"q": qT, "k": kT, "v": v}[kind][:, h, :]
                        dve.wait_ge(s_ps, g + 1)
                        nc.vector.tensor_copy(dst, ps[g % 4][:, 0:MEM if kind == "k" else N]).then_inc(s_out, 1)

            with ExitStack() as c2:
                ps_s = [psum(c2, f"m_s{i}") for i in range(2)]
                ps_t = [psum(c2, f"m_t{i}") for i in range(2 * MT)]
                ps_o = [psum(c2, f"m_o{i}") for i in range(2)]
                s_wo, s_s, s_mx, s_exp, s_nrm, s_t, s_pt, s_o, s_ot, s_dve, s_x = (
                    sem("m_" + n) for n in ("wo", "s", "mx", "exp", "nrm", "t", "pt", "o", "ot", "dve", "x"))
                block = c2.enter_context(nc.Block())

                @block.sync
                def _(sp):
                    sp.dma_start(wo[:], a["w_mo"].rearrange("l (k p) n -> p (l k) n", p=P)).then_inc(s_wo, 16)

                @block.tensor
                def _(pe):
                    for st in range(U + 3):
                        if st < U:
                            h, t = divmod(st, T)
                            if st >= 2:
                                pe.wait_ge(s_exp, st - 1)
                            nc.tensor.matmul(ps_s[st % 2][:, 0:MEM], qT[:, h, t * P:(t + 1) * P], kT[:, h, :],
                                             start=True, stop=True).then_inc(s_s, 1)
                        if 0 <= st - 2 < U:
                            u = st - 2
                            h, t = divmod(u, T)
                            pe.wait_ge(s_nrm, u + 1)
                            if t == 0 and h >= 2:
                                pe.wait_ge(s_pt, MT * (h - 1))
                            for m in range(MT):
                                last = nc.tensor.transpose(ps_t[MT * (h % 2) + m][:, t * P:(t + 1) * P],
                                                           pr[u % 3][:, m * P:(m + 1) * P], ident[:])
                            last.then_inc(s_t, 1)
                        if st - 3 >= 0 and (st - 3) % T == T - 1:
                            h = (st - 3) // T
                            pe.wait_ge(s_pt, MT * (h + 1))
                            if h >= 2:
                                pe.wait_ge(s_ot, h - 1)
                            for m in range(MT):
                                last = nc.tensor.matmul(ps_o[h % 2][:], v[:, m, h * P:(h + 1) * P],
                                                        pT[h % 2][:, m, :], start=(m == 0), stop=(m == MT - 1))
                            last.then_inc(s_o, 1)
                    pe.wait_ge(s_wo, 16)
                    pe.wait_ge(s_ot, MX_HEADS)
                    for g in range(2 * T):
                        t, h = divmod(g, 2)
                        if g >= 4:
                            pe.wait_ge(s_x, g - 3)
                        for k in range(KB):
                            last = nc.tensor.matmul(ps_t[g % 4][:], oT[:, k, t * P:(t + 1) * P],
                                                    wo[:, k, h * BW:(h + 1) * BW],
                                                    start=(k == 0), stop=(k == KB - 1))
                        last.then_inc(s_o, 1)

                @block.scalar
                def _(act):
                    for u in range(U):
                        act.wait_ge(s_mx, u + 1)
                        if u >= 3:
                            act.wait_ge(s_t, u - 2)
                        nc.scalar.activation(pr[u % 3][:], ps_s[u % 2][:, 0:MEM], ACT.Exp, scale=SC,
                                             bias=nmax[:, u:u + 1], accum_out=rsum[:, u:u + 1]
                                             ).then_inc(s_exp, 1)

                @block.vector
                def _(dve):
                    do = Steps(dve, s_dve)
                    for st in range(U + 4):
                        if st < U:
                            dve.wait_ge(s_s, st + 1)
                            do.after(nc.vector.reduce_max(nmax[:, st:st + 1], ps_s[st % 2][:, 0:MEM], AX_X))
                            nc.vector.tensor_scalar(nmax[:, st:st + 1], nmax[:, st:st + 1], -SC, None,
                                                    ALU.mult).then_inc(s_mx, 1)
                        if 0 <= st - 1 < U:
                            u = st - 1
                            dve.wait_ge(s_exp, u + 1)
                            do.after(nc.vector.reciprocal(rsum[:, u:u + 1], rsum[:, u:u + 1]))
                            nc.vector.tensor_scalar(pr[u % 3][:], pr[u % 3][:], rsum[:, u:u + 1], None,
                                                    ALU.mult).then_inc(s_nrm, 1)
                        if st - 2 >= 0 and st - 2 < U and (st - 2) % T == T - 1:
                            h = (st - 2) // T
                            dve.wait_ge(s_t, h * T + T)
                            if h >= 2:
                                dve.wait_ge(s_o, h - 1)
                            for m in range(MT):
                                nc.vector.tensor_copy(pT[h % 2][:, m, :], ps_t[MT * (h % 2) + m][:]
                                                      ).then_inc(s_pt, 1)
                        if st - 3 >= 0 and (st - 3) % T == T - 1:
                            h = (st - 3) // T
                            dve.wait_ge(s_o, h + 1)
                            nc.vector.tensor_copy(oT[:, h, :], ps_o[h % 2][:]).then_inc(s_ot, 1)
                    for g in range(2 * T):
                        t, h = divmod(g, 2)
                        dve.wait_ge(s_o, MX_HEADS + g + 1)
                        xs = x_sb[:, t, h * BW:(h + 1) * BW]
                        nc.vector.tensor_tensor(xs, ps_t[g % 4][:], xs, ALU.add).then_inc(s_x, 1)

        idx = sbuf(stack, "idx", [P, EXPERTS], U32)
        wsel = sbuf(stack, "wsel", [P, 2, T])
        with ExitStack() as c:
            h3T = sbuf(c, "h3T", [P, KD, N])
            xn = sbuf(c, "xn", [P, T, D])
            ffn_gain = sbuf(c, "ffn_gain", [P, D])

            def load_gain(sp):
                sp.dma_start(ffn_gain[:], bass.AP(a["rows"].tensor, ROWS, [[0, P], [1, D]])).then_inc(s_start, 16)
                sp.wait_ge(s_start, 96)

            load_gain.ready = 96
            rms_transposed(c, "rf", x_sb, T, None, h3T, first=load_gain, keep=xn,
                           gain_row=ffn_gain[:])
            w_rt = sbuf(c, "w_rt", [P, KD, LOGITS])
            rc = sbuf(c, "rc", [P, ROUTE_CONSTS])
            before, ones = rc[:, 0:P], rc[:, P:2 * P]
            iota = rc[:, 2 * P:2 * P + EXPERTS]
            r0 = 2 * P + EXPERTS
            blk_thr, blk_no, blk_e = (rc[:, r0 + P * i:r0 + P * (i + 1)] for i in range(3))
            rank1 = rc[:, r0 + 3 * P:r0 + 3 * P + 1]
            asg = sbuf(c, "asg", [P, 2, T], I32)
            fill = sbuf(c, "fill", [P, P], I32)
            lg = sbuf(c, "lg", [P, T, LOGITS])
            gpad = sbuf(c, "gpad", [P, T, PER_GROUP])
            sel = sbuf(c, "sel", [P, T, PER_GROUP])
            top = sbuf(c, "top", [P, 2, T, PER_GROUP])
            topi = sbuf(c, "topi", [P, 2, T, PER_GROUP], U32)
            topf = sbuf(c, "topf", [P, 2, T, PER_GROUP])
            oh = sbuf(c, "oh", [P, T, GROUPS])
            junk = sbuf(c, "r_junk", [P, 2, T, EXPERTS])
            sm = sbuf(c, "r_small", [P, 8, T])
            e_of = sbuf(c, "e_of", [P, 2, T])
            hot = sbuf(c, "hot", [P, 3, T, EXPERTS])
            pos = sbuf(c, "pos", [P, T, EXPERTS])
            dest = sbuf(c, "dest", [P, 2, T])
            destu = sbuf(c, "destu", [P, 2, T], U32)
            act_b = sbuf(c, "act_b", [P, EXPERTS, 4])
            cnt = sbuf(c, "cnt", [P, EXPERTS])
            rank = sbuf(c, "rank", [P, P])
            jobs = sbuf(c, "jobs", [P, 4])
            jobsi = sbuf(c, "jobsi", [P, 4], I32)
            idr = sbuf(c, "idr", [EXPERTS, P], I32)
            idf = sbuf(c, "idf", [EXPERTS, P])
            ps_l, ps_p, ps_c, ps_i = (psum(c, "r_" + n) for n in ("l", "p", "c", "i"))
            s_w, s_c, s_xw, s_l, s_dve, s_gm, s_ex, s_d01, s_e2, s_hot, s_pc, s_dest, s_fl, s_fw, s_sc, s_rd, s_rf, s_it, s_jb, s_jw = (
                sem("r_" + n) for n in ("w", "const", "xw", "l", "dve", "gmax", "gexp", "d01", "e2", "hot", "pc",
                                        "dest", "fill", "fillw", "scat", "read", "readf", "idt", "jobs", "jobw"))
            block = c.enter_context(nc.Block())

            @block.sync
            def _(sp):
                sp.dma_start(w_rt[:], a["w_route"].rearrange("(p k) n -> p k n", k=KD)).then_inc(s_w, 16)
                sp.dma_start(rc[:], a["route_consts"]).then_inc(s_c, 16)
                sp.dma_start(asg[:], a["asg_ids"]).then_inc(s_c, 16)
                for ch in range(2):
                    sp.dma_start(xn_dram[ch * N:(ch + 1) * N, :].rearrange("(t p) d -> p t d", p=P), xn[:]
                                 ).then_inc(s_xw, 16)
                sp.wait_ge(s_sc, 16 * 2 * T)
                sp.dma_start(idr[:], list_dram.rearrange("(e s) o -> e (s o)", e=EXPERTS)[:, 0:P]
                             ).then_inc(s_rd, 16)
                sp.wait_ge(s_jb, 1)
                sp.dma_start(jobs_dram[0:1, 0:4 * PER_GROUP].rearrange("o (j q) -> (o j) q", q=4),
                             jobsi[0:PER_GROUP, :]).then_inc(s_jw, 16)
                sp.wait_ge(s_jw, 16)
                sp.wait_ge(s_xw, 32)

            @block.gpsimd
            def _(pool):
                nc.gpsimd.memset(fill[:], NO_SLOT).then_inc(s_fl, 1)
                pool.wait_ge(s_fl, 1)
                pool.dma_start(list_dram.rearrange("(q s) o -> q (s o)", q=P), fill[:]).then_inc(s_fw, 16)
                pool.wait_ge(s_fw, 16)
                pool.wait_ge(s_c, 32)
                pool.wait_ge(s_dest, 1)
                for ch in range(2):
                    for t in range(T):
                        pool.indirect_dma_start(list_dram, bass.IndirectOffsetOnAxis(destu[:, ch, t:t + 1], 0),
                                                asg[:, ch, t:t + 1], None).then_inc(s_sc, 16)

            @block.tensor
            def _(pe):
                pe.wait_ge(s_w, 16)
                for t in range(T):
                    for k in range(KD):
                        last = nc.tensor.matmul(ps_l[:, t * LOGITS:(t + 1) * LOGITS],
                                                h3T[:, k, t * P:(t + 1) * P], w_rt[:, k, :],
                                                start=(k == 0), stop=(k == KD - 1))
                last.then_inc(s_l, 1)
                pe.wait_ge(s_c, 32)
                pe.wait_ge(s_hot, 1)
                for t in range(T):
                    o = ps_p[:, t * EXPERTS:(t + 1) * EXPERTS]
                    for q in range(t):
                        nc.tensor.matmul(o, ones, hot[:, 2, q, :], start=(q == 0), stop=False)
                    nc.tensor.matmul(o, before, hot[:, 2, t, :], start=(t == 0), stop=True)
                for t in range(T):
                    last = nc.tensor.matmul(ps_c[:, 0:EXPERTS], ones, hot[:, 2, t, :],
                                            start=(t == 0), stop=(t == T - 1))
                last.then_inc(s_pc, 1)
                pe.wait_ge(s_rf, 1)
                nc.tensor.transpose(ps_i[:, 0:EXPERTS], idf[:], ident[0:EXPERTS, 0:EXPERTS]).then_inc(s_it, 1)

            @block.scalar
            def _(act):
                act.wait_ge(s_gm, 1)
                for t in range(T):
                    nc.scalar.activation(junk[:, 0, t, 0:GROUPS], lg[:, t, 0:GROUPS], ACT.Exp,
                                         bias=sm[:, 0, t:t + 1], accum_out=sm[:, 1, t:t + 1]).then_inc(s_ex, 1)
                act.wait_ge(s_d01, 1)
                nc.scalar.activation(sm[:, 3, :], sm[:, 2, :], ACT.Exp).then_inc(s_e2, 1)

            @block.vector
            def _(dve):
                do = Steps(dve, s_dve)
                do.after(nc.vector.memset(gpad[:], -3e38))
                dve.wait_ge(s_c, 32)
                dve.wait_ge(s_l, 1)
                bias = router_bias.unsqueeze(1).to_broadcast([P, T, LOGITS])
                do.after(nc.vector.tensor_tensor(lg[:], ps_l[:, 0:T * LOGITS].rearrange("p (t n) -> p t n", t=T),
                                                 bias, ALU.add))
                do.after(nc.vector.tensor_copy(gpad[:, :, 0:GROUPS], lg[:, :, 0:GROUPS]))
                for t in range(T):
                    do.after(nc.vector.max(top[:, 0, t, :], gpad[:, t, :]))
                    do.after(nc.vector.max_index(topi[:, 0, t, :], top[:, 0, t, :], gpad[:, t, :]))
                nc.vector.tensor_scalar(sm[:, 0, :], top[:, 0, :, 0], -1.0, None, ALU.mult).then_inc(s_gm, 1)
                do.after(nc.vector.tensor_copy(topf[:, 0, :, :], topi[:, 0, :, :]))
                for t in range(T):
                    do.after(nc.vector.tensor_scalar(oh[:, t, :], iota[:, 0:GROUPS], topf[:, 0, t, 0:1], None,
                                                     ALU.is_equal))
                    for g in range(GROUPS):
                        el = lg[:, t, GROUPS + g * PER_GROUP:GROUPS + (g + 1) * PER_GROUP]
                        if g == 0:
                            ins = nc.vector.tensor_scalar(sel[:, t, :], el, oh[:, t, 0:1], None, ALU.mult)
                        else:
                            ins = nc.vector.scalar_tensor_tensor(sel[:, t, :], el, oh[:, t, g:g + 1],
                                                                 sel[:, t, :], ALU.mult, ALU.add)
                        do.after(ins)
                    do.after(nc.vector.max(top[:, 1, t, :], sel[:, t, :]))
                    do.after(nc.vector.max_index(topi[:, 1, t, :], top[:, 1, t, :], sel[:, t, :]))
                do.after(nc.vector.tensor_copy(topf[:, 1, :, :], topi[:, 1, :, :]))
                nc.vector.tensor_tensor(sm[:, 2, :], top[:, 1, :, 1], top[:, 1, :, 0], ALU.subtract
                                        ).then_inc(s_d01, 1)
                for ch in range(2):
                    do.after(nc.vector.scalar_tensor_tensor(e_of[:, ch, :], topf[:, 0, :, 0], float(PER_GROUP),
                                                            topf[:, 1, :, ch], ALU.mult, ALU.add))
                    for t in range(T):
                        do.after(nc.vector.tensor_scalar(hot[:, ch, t, :], iota, e_of[:, ch, t:t + 1], None,
                                                         ALU.is_equal))
                nc.vector.tensor_tensor(hot[:, 2, :, :], hot[:, 0, :, :], hot[:, 1, :, :], ALU.add
                                        ).then_inc(s_hot, 1)
                dve.wait_ge(s_e2, 1)
                dve.wait_ge(s_ex, T)
                do.after(nc.vector.tensor_scalar(sm[:, 4, :], sm[:, 3, :], 1.0, None, ALU.add))
                do.after(nc.vector.tensor_tensor(sm[:, 4, :], sm[:, 4, :], sm[:, 1, :], ALU.mult))
                do.after(nc.vector.reciprocal(sm[:, 4, :], sm[:, 4, :]))
                do.after(nc.vector.tensor_scalar(wsel[:, 0, :], sm[:, 4, :], 0.5, None, ALU.mult))
                do.after(nc.vector.tensor_tensor(wsel[:, 1, :], wsel[:, 0, :], sm[:, 3, :], ALU.mult))
                dve.wait_ge(s_pc, 1)
                do.after(nc.vector.tensor_copy(pos[:], ps_p[:, 0:T * EXPERTS].rearrange("p (t e) -> p t e", t=T)))
                do.after(nc.vector.tensor_copy(cnt[:], ps_c[:, 0:EXPERTS]))
                for ch in range(2):
                    do.after(nc.vector.tensor_tensor(junk[:, ch, :, :], hot[:, ch, :, :], pos[:], ALU.mult))
                    do.after(nc.vector.tensor_reduce(dest[:, ch, :], junk[:, ch, :, :], AX_X, ALU.add))
                do.after(nc.vector.scalar_tensor_tensor(dest[:], e_of[:], float(N), dest[:], ALU.mult, ALU.add))
                nc.vector.tensor_copy(destu[:], dest[:]).then_inc(s_dest, 1)
                thr = blk_thr.rearrange("p (e b) -> p e b", b=4)
                do.after(nc.vector.tensor_tensor(act_b[:], cnt[:].unsqueeze(2).to_broadcast([P, EXPERTS, 4]),
                                                 thr, ALU.is_gt))
                av = act_b[:].rearrange("p e b -> p (e b)")
                do.after(nc.vector.tensor_tensor_scan(rank[:], ones, av, 0.0, ALU.mult, ALU.add))
                do.after(nc.vector.tensor_copy(jobs[:, 2:3], rank[:, P - 1:P]))
                do.after(nc.vector.tensor_tensor(rank[:], rank[:], av, ALU.mult))
                do.after(nc.vector.tensor_scalar(rank[:], rank[:], rank1, None, ALU.is_equal))
                do.after(nc.vector.tensor_tensor_reduce(av, rank[:], blk_no, 1.0, 0.0, ALU.mult, ALU.add,
                                                        jobs[:, 0:1]))
                do.after(nc.vector.tensor_tensor_reduce(av, rank[:], blk_e, 1.0, 0.0, ALU.mult, ALU.add,
                                                        jobs[:, 1:2]))
                do.after(nc.vector.memset(jobs[:, 3:4], 0.0))
                nc.vector.tensor_copy(jobsi[:], jobs[:]).then_inc(s_jb, 1)
                dve.wait_ge(s_rd, 16)
                nc.vector.tensor_copy(idf[:], idr[:]).then_inc(s_rf, 1)
                dve.wait_ge(s_it, 1)
                do.after(nc.vector.tensor_copy(idx[:], ps_i[:, 0:EXPERTS]))

        with ExitStack() as c:
            RAW, PIECES, PW = 4, 6, 2048
            raw = [sbuf(c, f"w_raw{r}", [P, PW]) for r in range(RAW)]
            w_hi = [sbuf(c, f"w_hi{j}", [P, PW], F32R) for j in range(PIECES)]
            w_lo = [sbuf(c, f"w_lo{j}", [P, PW], F32R) for j in range(PIECES)]
            ibx, iby = ([sbuf(c, f"ib{n}{b}", [P, 1], U32) for b in range(2)] for n in "xy")
            xs = [sbuf(c, f"xs{b}", [P, D]) for b in range(2)]
            xT_hi, xT_lo = (sbuf(c, "xT_" + n, [P, KD * P], F32R) for n in ("hi", "lo"))
            hT_hi, hT_lo = (sbuf(c, "hT_" + n, [P, KF * P], F32R) for n in ("hi", "lo"))
            tn = sbuf(c, "tn", [P, FF])
            hd = sbuf(c, "hd", [P, FF])
            yo = [sbuf(c, f"yo{b}", [P, D]) for b in range(2)]
            ps_x = psum(c, "e_x", (P, KD * P))
            ps_1, ps_3, ps_h = psum(c, "e_1"), psum(c, "e_3"), psum(c, "e_h")
            ps_y = psum(c, "e_y", (P, D))

            s_ibx, s_iby, s_xs, s_ys, s_stored = (
                [sem(f"e_{n}{b}") for b in range(2)] for n in ("ibx", "iby", "xs", "ys", "stored"))
            s_tx, s_xhi, s_xlo, s_th, s_hm, s_hd, s_ht, s_hhi, s_hlo, s_yo = (
                sem("e_" + n) for n in ("tx", "xhi", "xlo", "tanh", "hm", "hd", "ht", "hhi", "hlo", "yo"))
            s_raw, s_hi, s_split = ([sem(f"e_{n}{r}") for r in range(RAW)] for n in ("raw", "hi", "split"))
            s_used = [sem(f"e_used{j}") for j in range(PIECES)]
            s_init, s_lst = sem("e_init"), sem("e_list")
            s_turn = sem("e_turn")
            w13v = [a[n].rearrange("l e (p k) f -> (l e) p (k f)", k=KD) for n in ("w1", "w1", "w3", "w3")]
            w2v = a["w2"].rearrange("l e (p k) d -> (l e) p (k d)", k=KF)
            NI = EXPERTS // 2
            HALF = NI - 1
            last_row = nc.gpsimd.alloc_register("last_row")

            class Step:

                def __init__(self, s, i, odd, extra=None):
                    self.s, self.i, self.odd, self.extra = s, i, odd, extra

                def piece(self, j):
                    if self.extra is not None:
                        return (j % RAW, self.extra * (2 if j % RAW < 2 else 1) + (3 * EXPERTS // 2 + 1 + j // RAW))
                    if self.i is None:
                        return j, 1
                    m = j if self.odd else PIECES + j
                    if not self.odd and isinstance(self.s, int) and self.s == EXPERTS:
                        m = PIECES + j - 4
                    return m % RAW, self.i * 3 + (m // RAW + 2)

            first_step = Step(0, None, False)

            def pair(i):
                return Step(i * 2 + 1, i, True), Step(i * 2 + 2, i, False)

            step31, step32 = Step(EXPERTS - 1, HALF, True), Step(EXPERTS, HALF, False)

            class Job:

                def __init__(self, q, b, i, tx):
                    self.q, self.b, self.i, self.tx = q, b, i, tx

            def job(s, i, odd, shift):
                at = (1 if odd else 2) + shift
                return Job(s + shift, at % 2, i + at // 2, s + (shift + 1))

            def extra(r):
                return Job(r + EXPERTS, 0, r + NI, r + (EXPERTS + 2))

            def wait(eng, q, n):
                if not (isinstance(n, int) and n <= 0):
                    eng.wait_ge(q, n)

            def load(sp, st, j, e):
                r, n = st.piece(j)
                if not (isinstance(n, int) and n == 1):
                    sp.wait_ge(s_split[r], n - 1)
                src, h = (w13v[j], j % 2) if j < 4 else (w2v, j - 4)
                sp.dma_start(raw[r][:], src[bass.ds(e, 1), :, h * PW:(h + 1) * PW].rearrange("o p f -> p (o f)")
                             ).then_inc(s_raw[r], 16)

            def hi_part(act, st, j, q):
                r, n = st.piece(j)
                act.wait_ge(s_raw[r], n * 16)
                wait(act, s_used[j], q)
                nc.scalar.copy(w_hi[j][:], raw[r][:]).then_inc(s_hi[r], 1)

            def lo_part(dve, st, j):
                r, n = st.piece(j)
                dve.wait_ge(s_hi[r], n)
                nc.vector.tensor_tensor(w_lo[j][:], raw[r][:], w_hi[j][:].bitcast(F32), ALU.subtract
                                        ).then_inc(s_split[r], 1)

            def fetch(pool, b, n, tx):
                wait(pool, s_ibx[b], n)
                pool.wait_ge(s_tx, tx)
                pool.sem_inc(s_turn, 1)
                pool.indirect_dma_start(xs[b][:], None, xn_dram, bass.IndirectOffsetOnAxis(ibx[b][:], 0),
                                        bounds_check=last_row, oob_is_err=False).then_inc(s_xs[b], 16)

            def store(pool, jb, listed=True):
                b = jb.b
                if listed:
                    pool.wait_ge(s_iby[b], jb.i + 1)
                pool.wait_ge(s_yo, jb.q + 1)
                pool.sem_inc(s_turn, 1)
                pool.indirect_dma_start(ys_dram, bass.IndirectOffsetOnAxis(iby[b][:], 0), yo[b][:], None,
                                        bounds_check=last_row, oob_is_err=False).then_inc(s_ys[b], 16)
                pool.wait_ge(s_ys[b], jb.i * 16 + 16)
                pool.sem_inc(s_stored[b], 1)

            def turn_rows(pe, jb):
                pe.wait_ge(s_xs[jb.b], jb.i * 16 + 16)
                wait(pe, s_xlo, jb.q)
                for k in range(KD):
                    last = nc.tensor.transpose(ps_x[:, k * P:(k + 1) * P], xs[jb.b][:, k::KD], ident[:])
                last.then_inc(s_tx, 1)

            def product(o, x_parts, j, k, w_cols, start, stop):
                x_hi, x_lo = x_parts
                for n, (xp, wp) in enumerate(((x_hi, w_hi[j]), (x_hi, w_lo[j]), (x_lo, w_hi[j]))):
                    last = nc.tensor.matmul(o, xp[:, k * P:(k + 1) * P], wp[:, w_cols:w_cols + FF],
                                            start=start and n == 0, stop=stop and n == 2)
                return last

            def up(pe, st, q, pieces):
                if 0 in pieces:
                    pe.wait_ge(s_xlo, q + 1)
                    wait(pe, s_hd, q)
                for j in pieces:
                    r, n = st.piece(j)
                    pe.wait_ge(s_split[r], n)
                    half = j % 2
                    for k in range(4):
                        last = product((ps_1 if j < 2 else ps_3)[:], (xT_hi, xT_lo), j, half * 4 + k, k * FF,
                                       half == 0 and k == 0, half == 1 and k == 3)
                    last.then_inc(s_used[j], 1)

            def turn_hidden(pe, q):
                pe.wait_ge(s_hd, q + 1)
                wait(pe, s_hlo, q)
                for k in range(KF):
                    last = nc.tensor.transpose(ps_h[:, k * P:(k + 1) * P], hd[:, k::KF], ident[:])
                last.then_inc(s_ht, 1)

            def down(pe, st, q):
                pe.wait_ge(s_hlo, q + 1)
                wait(pe, s_yo, q)
                for j in (4, 5):
                    r, n = st.piece(j)
                    pe.wait_ge(s_split[r], n)
                    for h in range(2):
                        for k in range(2):
                            last = product(ps_y[:, h * FF:(h + 1) * FF], (hT_hi, hT_lo), j, (j - 4) * 2 + k,
                                           k * D + h * FF, j == 4 and k == 0, j == 5 and k == 1)
                    last.then_inc(s_used[j], 1)

            def x_hi(act, q):
                act.wait_ge(s_tx, q + 3)
                nc.scalar.copy(xT_hi[:], ps_x[:]).then_inc(s_xhi, 1)

            def tanh_step(act, q):
                act.wait_ge(s_used[1], q + 1)
                wait(act, s_hd, q)
                nc.scalar.activation(tn[:], ps_1[:], ACT.Tanh, scale=0.5).then_inc(s_th, 1)

            def h_hi(act, q):
                act.wait_ge(s_ht, q + 1)
                nc.scalar.copy(hT_hi[:], ps_h[:]).then_inc(s_hhi, 1)

            def y_copy(act, jb):
                act.wait_ge(s_used[5], jb.q + 2)
                act.wait_ge(s_stored[jb.b], jb.i + 1)
                nc.scalar.copy(yo[jb.b][:], ps_y[:]).then_inc(s_yo, 1)

            def x_lo(dve, q):
                dve.wait_ge(s_xhi, q + 1)
                nc.vector.tensor_tensor(xT_lo[:], ps_x[:], xT_hi[:].bitcast(F32), ALU.subtract).then_inc(s_xlo, 1)

            def silu_step(dve, q):
                dve.wait_ge(s_th, q + 1)
                nc.vector.scalar_tensor_tensor(tn[:], tn[:], 1.0, ps_1[:], ALU.add, ALU.mult).then_inc(s_hm, 1)

            def hidden(dve, q):
                dve.wait_ge(s_hm, q + 1)
                dve.wait_ge(s_used[3], q + 1)
                wait(dve, s_ht, q)
                nc.vector.tensor_tensor(hd[:], tn[:], ps_3[:], ALU.mult).then_inc(s_hd, 1)

            def h_lo(dve, q):
                dve.wait_ge(s_hhi, q + 1)
                nc.vector.tensor_tensor(hT_lo[:], ps_h[:], hT_hi[:].bitcast(F32), ALU.subtract).then_inc(s_hlo, 1)

            def pick_x(dve, e, jb):
                dve.wait_ge(s_tx, jb.tx)
                nc.vector.tensor_copy(ibx[jb.b][:], idx[:, bass.ds(e, 1)]).then_inc(s_ibx[jb.b], 1)

            def pick_y(dve, e, jb):
                dve.wait_ge(s_stored[jb.b], jb.i + 1)
                nc.vector.tensor_copy(iby[jb.b][:], idx[:, bass.ds(e, 1)]).then_inc(s_iby[jb.b], 1)

            def pool_step(pool, s, i, odd, rows_in):
                if rows_in:
                    jb = job(s, i, odd, 1)
                    fetch(pool, jb.b, jb.i + 1, jb.tx)
                store(pool, job(s, i, odd, -1))

            def pe_step(pe, st, s, i, odd, rows_in):
                up(pe, st, s, (0, 1, 2))
                turn_hidden(pe, s - 1)
                up(pe, st, s, (3,))
                if rows_in:
                    turn_rows(pe, job(s, i, odd, 1))
                down(pe, st, s - 1)

            def act_step(act, nxt, s, i, odd, ups, last=True):
                if ups:
                    hi_part(act, nxt, 0, s + 1)
                    hi_part(act, nxt, 1, s + 1)
                tanh_step(act, s)
                if last:
                    h_hi(act, s - 1)
                if ups:
                    hi_part(act, nxt, 2, s + 1)
                    x_hi(act, s + 1)
                    hi_part(act, nxt, 3, s + 1)
                hi_part(act, nxt, 4, s + 1)
                hi_part(act, nxt, 5, s + 1)
                if last:
                    y_copy(act, job(s, i, odd, -1))

            def dve_step(dve, nxt, s, i, odd, ups, last=True, first=False):
                if ups:
                    if first:
                        pick_y(dve, 0, Job(0, 0, 0, 2))
                        pick_x(dve, 2, Job(2, 0, 1, 3))
                    else:
                        pick_y(dve, s, job(s, i, odd, 0))
                        if ups != "no rows":
                            pick_x(dve, s + 2, job(s, i, odd, 2))
                    lo_part(dve, nxt, 0)
                    lo_part(dve, nxt, 1)
                silu_step(dve, s)
                if last:
                    h_lo(dve, s - 1)
                if ups:
                    lo_part(dve, nxt, 2)
                hidden(dve, s)
                if ups:
                    x_lo(dve, s + 1)
                    lo_part(dve, nxt, 3)
                lo_part(dve, nxt, 4)
                lo_part(dve, nxt, 5)

            block = c.enter_context(nc.Block())

            @block.sync
            def _(sp):
                sp.sem_inc(s_tx, 2)
                for q in (s_used[4], s_used[5], s_stored[0], s_stored[1]):
                    sp.sem_inc(q, 1)
                for j in range(4):
                    load(sp, first_step, j, 0)
                with sp.Fori(0, HALF) as i:
                    for st in pair(i):
                        for j in range(PIECES):
                            load(sp, st, j, st.s if j < 4 else st.s - 1)
                for j in range(PIECES):
                    load(sp, step31, j, EXPERTS - 1 if j < 4 else EXPERTS - 2)
                for j in (4, 5):
                    load(sp, step32, j, EXPERTS - 1)
                n = sp.value_load(jobs_dram[0:1, 2:3], min_val=0, max_val=MAX_EXTRA)
                with sp.If(n > 0):
                    with sp.Fori(0, n) as r:
                        e = sp.value_load(jobs_dram[0:1, bass.ds(r * 4 + 1, 1)], min_val=0, max_val=EXPERTS - 1)
                        for j in range(PIECES):
                            load(sp, Step(None, None, False, r), j, e)
                    sp.nop()

            @block.gpsimd
            def _(pool):
                for b in range(2):
                    nc.gpsimd.memset(xs[b][:], 0.0).then_inc(s_init, 1)
                pool.wait_ge(s_init, 2)
                pool.reg_mov(last_row, SLOTS - 1)
                fetch(pool, 0, 1, 1)
                fetch(pool, 1, 1, 2)
                with pool.Fori(0, HALF) as i:
                    for st in pair(i):
                        pool_step(pool, st.s, i, st.odd, True)
                store(pool, Job(EXPERTS - 2, 0, NI - 1, None))
                store(pool, Job(EXPERTS - 1, 1, NI - 1, None))
                n = pool.value_load(jobs_dram[0:1, 2:3], min_val=0, max_val=MAX_EXTRA)
                with pool.If(n > 0):
                    with pool.Fori(0, n) as r:
                        j = pool.value_load(jobs_dram[0:1, bass.ds(r * 4, 1)], min_val=0, max_val=4 * EXPERTS - 1)
                        for ib in (ibx[0], iby[0]):
                            pool.dma_start(ib[:], list_dram[bass.ds(j * P, P), :].bitcast(U32)).then_inc(s_lst, 16)
                        pool.wait_ge(s_lst, r * 32 + 32)
                        jb = extra(r)
                        fetch(pool, 0, 0, jb.tx)
                        store(pool, jb, listed=False)
                    pool.nop()

            @block.tensor
            def _(pe):
                turn_rows(pe, Job(0, 0, 0, None))
                up(pe, first_step, 0, (0, 1, 2, 3))
                turn_rows(pe, Job(1, 1, 0, None))
                with pe.Fori(0, HALF) as i:
                    for st in pair(i):
                        pe_step(pe, st, st.s, i, st.odd, True)
                pe_step(pe, step31, EXPERTS - 1, HALF, True, False)
                turn_hidden(pe, EXPERTS - 1)
                down(pe, step32, EXPERTS - 1)
                n = pe.value_load(jobs_dram[0:1, 2:3], min_val=0, max_val=MAX_EXTRA)
                with pe.If(n > 0):
                    with pe.Fori(0, n) as r:
                        jb, st = extra(r), Step(None, None, False, r)
                        turn_rows(pe, jb)
                        up(pe, st, jb.q, (0, 1, 2, 3))
                        turn_hidden(pe, jb.q)
                        down(pe, st, jb.q)
                    pe.nop()

            @block.scalar
            def _(act):
                x_hi(act, 0)
                for j in range(4):
                    hi_part(act, first_step, j, 0)
                act_step(act, Step(1, 0, True), 0, None, False, True, last=False)
                with act.Fori(0, HALF) as i:
                    odd, even = pair(i)
                    act_step(act, even, odd.s, i, True, True)
                    act_step(act, Step(i * 2 + 3, i + 1, True), even.s, i, False, True)
                act_step(act, step32, EXPERTS - 1, HALF, True, False)
                h_hi(act, EXPERTS - 1)
                y_copy(act, Job(EXPERTS - 1, 1, NI - 1, None))
                n = act.value_load(jobs_dram[0:1, 2:3], min_val=0, max_val=MAX_EXTRA)
                with act.If(n > 0):
                    with act.Fori(0, n) as r:
                        jb, st = extra(r), Step(None, None, False, r)
                        x_hi(act, jb.q)
                        for j in range(4):
                            hi_part(act, st, j, jb.q)
                        tanh_step(act, jb.q)
                        hi_part(act, st, 4, jb.q + 1)
                        hi_part(act, st, 5, jb.q + 1)
                        h_hi(act, jb.q)
                        y_copy(act, jb)
                    act.nop()

            @block.vector
            def _(dve):
                for b in range(2):
                    pick_x(dve, b, Job(b, b, 0, b + 1))
                x_lo(dve, 0)
                for j in range(4):
                    lo_part(dve, first_step, j)
                dve_step(dve, Step(1, 0, True), 0, None, False, True, last=False, first=True)
                with dve.Fori(0, HALF - 1) as i:
                    odd, even = pair(i)
                    dve_step(dve, even, odd.s, i, True, True)
                    dve_step(dve, Step(i * 2 + 3, i + 1, True), even.s, i, False, True)
                odd, even = pair(HALF - 1)
                dve_step(dve, even, odd.s, HALF - 1, True, True)
                dve_step(dve, step31, even.s, HALF - 1, False, "no rows")
                pick_y(dve, EXPERTS - 1, Job(EXPERTS - 1, 1, NI - 1, None))
                dve_step(dve, step32, EXPERTS - 1, HALF, True, False)
                h_lo(dve, EXPERTS - 1)
                n = dve.value_load(jobs_dram[0:1, 2:3], min_val=0, max_val=MAX_EXTRA)
                with dve.If(n > 0):
                    with dve.Fori(0, n) as r:
                        jb, st = extra(r), Step(None, None, False, r)
                        x_lo(dve, jb.q)
                        for j in range(4):
                            lo_part(dve, st, j)
                        silu_step(dve, jb.q)
                        hidden(dve, jb.q)
                        lo_part(dve, st, 4)
                        lo_part(dve, st, 5)
                        h_lo(dve, jb.q)
                    dve.nop()

        with ExitStack() as c:
            yk = sbuf(c, "yk", [P, 2, T, D])
            junk = sbuf(c, "f_junk", [P, D])
            ss = sbuf(c, "f_ss", [P, T])
            s_ld = [[sem(f"f_ld{ch}{t}") for t in range(T)] for ch in range(2)]
            s_dve, s_x, s_ss, s_ms, s_sq, s_o, s_done = (sem("f_" + n) for n in ("dve", "x", "ss", "ms", "sq", "o",
                                                                                "done"))
            block = c.enter_context(nc.Block())

            @block.sync
            def _(sp):
                for t in range(T):
                    for ch in range(2):
                        r = ch * N + t * P
                        sp.dma_start(yk[:, ch, t, :], ys_dram[r:r + P, :]).then_inc(s_ld[ch][t], 16)
                for t in range(T):
                    sp.wait_ge(s_o, t + 1)
                    sp.dma_start(out[0, t * P:(t + 1) * P, :], x_sb[:, t, :]).then_inc(s_done, 16)
                sp.wait_ge(s_done, 16 * T)

            @block.scalar
            def _(act):
                for t in range(T):
                    act.wait_ge(s_x, t + 1)
                    if t:
                        act.wait_ge(s_ss, t)
                    nc.scalar.activation(junk[:], x_sb[:, t, :], ACT.Square, accum_out=ss[:, t:t + 1]
                                         ).then_inc(s_ss, 1)
                act.wait_ge(s_ms, 1)
                nc.scalar.activation(ss[:], ss[:], ACT.Sqrt).then_inc(s_sq, 1)

            @block.vector
            def _(dve):
                do = Steps(dve, s_dve)
                for t in range(T):
                    for ch in range(2):
                        dve.wait_ge(s_ld[ch][t], 16)
                        ins = nc.vector.scalar_tensor_tensor(x_sb[:, t, :], yk[:, ch, t, :],
                                                             wsel[:, ch, t:t + 1], x_sb[:, t, :],
                                                             ALU.mult, ALU.add)
                        if ch == 0:
                            do.after(ins)
                    ins.then_inc(s_x, 1)
                dve.wait_ge(s_ss, T)
                nc.vector.tensor_scalar(ss[:], ss[:], 1.0 / D, NORM_EPS, ALU.mult, ALU.add).then_inc(s_ms, 1)
                dve.wait_ge(s_sq, 1)
                do.after(nc.vector.reciprocal(ss[:], ss[:]))
                for t in range(T):
                    nc.vector.scalar_tensor_tensor(x_sb[:, t, :], x_sb[:, t, :], ss[:, t:t + 1], final_gain,
                                                   ALU.mult, ALU.mult).then_inc(s_o, 1)


def constants():
    p = np.arange(P)[:, None]
    c = np.arange(N)[None, :]
    ident = np.eye(P, dtype=np.float32)
    log_g = np.log(1.0 - 2.0 ** (-5.0 - np.arange(HEADS))).astype(np.float32).astype(np.float64)
    decay = np.where((c >= p)[:, None, :], np.exp(log_g[None, :, None] * np.maximum(c - p, 0)[:, None, :]), 0.0)
    decay = (decay * HD ** -0.5).astype(np.float32)
    slopes = (2.0 ** (-8.0 * np.arange(1, DIFF_HEADS + 1) / DIFF_HEADS)).astype(np.float32)
    dist = np.abs(p - (c - (N - P))).astype(np.float32)
    alibi = -slopes[None, :, None] * dist[:, None, :] * np.float32(HD ** 0.5)
    late = (c - (N - P)) // CHUNK > p // CHUNK
    alibi = np.where(late[:, None, :], np.float32(MASKED), alibi).astype(np.float32)
    f = np.arange(P)
    thr = np.where(f % 4 == 0, 1e9, P * (f % 4))
    route = np.concatenate([
        (np.arange(P)[:, None] < np.arange(P)[None, :]).astype(np.float32),
        np.ones((P, P), np.float32),
        np.tile(np.arange(EXPERTS, dtype=np.float32), (P, 1)),
        np.tile(thr.astype(np.float32), (P, 1)),
        np.tile(f.astype(np.float32), (P, 1)),
        np.tile((f // 4).astype(np.float32), (P, 1)),
        np.arange(1, P + 1, dtype=np.float32)[:, None],
    ], axis=1)
    asg = (np.arange(2)[None, :, None] * N + np.arange(T)[None, None, :] * P + np.arange(P)[:, None, None])
    return {"ident": ident, "decay": decay, "alibi": alibi, "route_consts": route,
            "asg_ids": asg.astype(np.int32)}


def laid_out(i):
    w_in = i["w_in"][0]
    at = [512 * n for n in range(13)]
    ax, ag, bq, bk, bv, cq, ck, cv, cg, dq, dk, dv = (w_in[:, at[n]:at[n + 1]] for n in range(12))
    w_mix = np.stack([ax, ag, bq, bk, cq, ck, dq, dk, bv, cv, cg, dv])
    gates = w_in[:, at[12]:].reshape(D, 4, KD, P)
    w_gate = gates.transpose(2, 0, 1, 3).reshape(KD, D, 4 * P)

    def cols(v, k):
        return v.reshape(P, k)

    def tiles(v):
        return v.reshape(KB, P).T

    small = np.concatenate(
        [cols(i["norm_mix"], KD), cols(i["norm_mem"], KD), cols(i["mem_norm"], KD)]
        + [tiles(i["conv_w"][0, j]) for j in range(4)]
        + [tiles(i[n][0]) for n in ("conv_b", "lru_ba", "lru_bx", "lru_lambda")], axis=1)
    rows = np.concatenate([i["final_norm"], i["b_group"][0], i["b_router"][0], i["diff_subln"][0],
                           i["diff_lambda"][0].reshape(-1), i["norm_ffn"][0]])[None, :]
    got = {"small": small, "rows": rows, "w_mix": w_mix, "w_gate": w_gate,
           "rel_flipped": i["ca_rel_bias"][0, :, ::-1],
           "w_route": np.concatenate([i["w_group"][0], i["w_router"][0]], axis=1)}
    for n in ("wa", "wx"):
        blocks = i["lru_" + n][0]
        bd = np.zeros((KB, P, P), blocks.dtype)
        for k in range(2 * KB):
            o = (k % 2) * HD
            bd[k // 2, o:o + HD, o:o + HD] = blocks[k]
        got[n + "_bd"] = bd
    for n in ("x", "mem", "w_branch", "w_out", "w_mq", "w_mk", "w_mv", "w_mo", "w1", "w3", "w2"):
        got[n] = i[n]
    return got


def kernel(**inputs):
    import concourse.bacc as bacc
    from concourse.bass_utils import run_bass_kernel_spmd

    inputs = {k: np.asarray(v) for k, v in inputs.items()}
    arrays = {n: np.ascontiguousarray(v) for n, v in {**laid_out(inputs), **constants()}.items()}
    nc = bacc.Bacc("TRN2", target_bir_lowering=False, num_devices=1)
    a = {n: nc.dram_tensor("in_" + n, list(v.shape), mybir.dt.from_np(v.dtype), kind="ExternalInput").ap()
         for n, v in arrays.items()}
    out = nc.dram_tensor("out_x", [1, N, D], F32, kind="ExternalOutput").ap()
    trunk(nc, a, out)
    r = run_bass_kernel_spmd(nc, [{"in_" + n: v for n, v in arrays.items()}], core_ids=[0])
    return r.results[0]["out_x"]
```

```python
from contextlib import ExitStack

import numpy as np

import concourse.bass as bass
from concourse import mybir

F32 = mybir.dt.float32
F32R = mybir.dt.float32r
U32 = mybir.dt.uint32
I32 = mybir.dt.int32
ALU = mybir.AluOpType
ACT = mybir.ActivationFunctionType
AX_X = mybir.AxisListType.X

P = 128
D = 1024
N = 512
CHUNK = 64
MEM = 256
KD = D // P
T = N // P
BW = 512
KB = BW // P
HD = 64
HEADS = 8
DIFF_HEADS = 4
REL_CLIP = 128
MX_HEADS = 4
GROUPS = 4
PER_GROUP = 8
EXPERTS = GROUPS * PER_GROUP
FF = 512
KF = FF // P
LAM_INIT = 0.2
NORM_EPS = 1e-6
GN_EPS = 1e-5
MASKED = -1e30
NO_SLOT = 1 << 20
SLOTS = 2 * N
LOGITS = GROUPS + EXPERTS
ROUTE_CONSTS = 2 * P + EXPERTS + 3 * P + 1
SMALL = 3 * KD + 8 * KB
ROWS = D + LOGITS + 2 * HD + 4 * HD
MAX_EXTRA = SLOTS // P - 1

AX0, AG0, BQ0, BK0, CQ0, CK0, DQ0, DK0 = (4 * i for i in range(8))
BV, CV, CG, DV = range(4)
FEAT_CHUNKS = 8
TOK_CHUNKS = 4
CW = 256
UNIT = (KD + KB) * P
PIECE = 2 * BW


class Steps:

    def __init__(self, eng, sem):
        self.eng, self.sem, self.n = eng, sem, 0

    def after(self, ins):
        self.n += 1
        ins.then_inc(self.sem, 1)
        self.eng.wait_ge(self.sem, self.n)


def trunk(nc, a, out):
    stack = ExitStack()
    with stack:
        held = []

        def sem(name):
            held.append(nc.alloc_semaphore(name=name))
            return held[-1]

        def free_semaphores():
            nc.clear_and_free_semaphores(held)
            held.clear()
            nc.all_engine_barrier()

        def sbuf(ctx, name, shape, dt=F32):
            return ctx.enter_context(nc.sbuf_tensor(name, shape, dt))

        def psum(ctx, name, shape=(P, 512), dt=F32):
            return ctx.enter_context(nc.psum_tensor(name, list(shape), dt))

        xn_dram = nc.dram_tensor("xn_scratch", [SLOTS, D], F32).ap()
        ys_dram = nc.dram_tensor("ys_scratch", [SLOTS, D], F32).ap()
        list_dram = nc.dram_tensor("list_scratch", [EXPERTS * N, 1], I32).ap()
        rel_dram = nc.dram_tensor("rel_scratch", [HEADS, P, 5 * P], F32).ap()
        jobs_dram = nc.dram_tensor("jobs_scratch", [1, P], I32).ap()

        x_sb = sbuf(stack, "x_sb", [P, T, D])
        ident = sbuf(stack, "ident", [P, P])
        small = sbuf(stack, "small", [P, SMALL])
        rows = sbuf(stack, "rows", [P, ROWS])
        gain_mix, gain_mem, gain_memn = (small[:, KD * i:KD * (i + 1)] for i in range(3))
        s0 = 3 * KD
        conv_w = [small[:, s0 + KB * j:s0 + KB * (j + 1)] for j in range(4)]
        conv_b, lru_ba, lru_bx, lru_lam = (small[:, s0 + KB * j:s0 + KB * (j + 1)] for j in range(4, 8))
        final_gain = rows[:, 0:D]
        router_bias = rows[:, D:D + LOGITS]
        subln = rows[:, D + LOGITS:D + LOGITS + 2 * HD]
        lam_vecs = rows[:, D + LOGITS + 2 * HD:ROWS]

        s_start = stack.enter_context(nc.semaphore("s_start"))

        def rms_transposed(ctx, pfx, src, tiles, gain, dst, first=None, keep=None, gain_row=None):
            s_ss, s_ms, s_sq, s_rinv, s_xn = (sem(f"{pfx}_{n}") for n in ("ss", "ms", "sq", "rinv", "xn"))
            s_tp, s_ev = [sem(f"{pfx}_tp{i}") for i in range(2)], [sem(f"{pfx}_ev{i}") for i in range(2)]
            s_hi = sem(f"{pfx}_hi")
            with ExitStack() as c:
                junk = sbuf(c, pfx + "_junk", [P, D])
                ss = sbuf(c, pfx + "_sums", [P, tiles])
                xn = keep if keep is not None else sbuf(c, pfx + "_xn", [P, tiles, D])
                ps = [psum(c, f"{pfx}_ps{i}") for i in range(2)]
                block = c.enter_context(nc.Block())

                @block.sync
                def _(sp):
                    if first is not None:
                        first(sp)

                @block.scalar
                def _(act):
                    if first is not None:
                        act.wait_ge(s_start, first.ready)
                    for t in range(tiles):
                        if t:
                            act.wait_ge(s_ss, t)
                        nc.scalar.activation(junk[:], src[:, t, :], ACT.Square,
                                             accum_out=ss[:, t:t + 1]).then_inc(s_ss, 1)
                    act.wait_ge(s_ms, 1)
                    nc.scalar.activation(ss[:], ss[:], ACT.Sqrt).then_inc(s_sq, 1)
                    if isinstance(dst, tuple):
                        for k in range(KD):
                            act.wait_ge(s_tp[k % 2], k // 2 + 1)
                            nc.scalar.activation(dst[0][:, k, :], ps[k % 2][:, 0:tiles * P], ACT.Copy,
                                                 scale=gain[:, k:k + 1]).then_inc(s_hi, 1)
                        return
                    for k in range(1, KD, 2):
                        act.wait_ge(s_tp[1], k // 2 + 1)
                        nc.scalar.activation(dst[:, k, :], ps[1][:, 0:tiles * P], ACT.Copy,
                                             scale=1.0 if gain is None else gain[:, k:k + 1]
                                             ).then_inc(s_ev[1], 1)

                @block.vector
                def _(dve):
                    dve.wait_ge(s_ss, tiles)
                    nc.vector.tensor_scalar(ss[:], ss[:], 1.0 / D, NORM_EPS, ALU.mult, ALU.add).then_inc(s_ms, 1)
                    dve.wait_ge(s_sq, 1)
                    nc.vector.reciprocal(ss[:], ss[:]).then_inc(s_rinv, 1)
                    dve.wait_ge(s_rinv, 1)
                    if gain_row is not None:
                        dve.wait_ge(s_start, first.ready)
                    for t in range(tiles):
                        if gain_row is None:
                            nc.vector.tensor_scalar(xn[:, t, :], src[:, t, :], ss[:, t:t + 1], None,
                                                    ALU.mult).then_inc(s_xn, 1)
                        else:
                            nc.vector.scalar_tensor_tensor(xn[:, t, :], src[:, t, :], ss[:, t:t + 1], gain_row,
                                                           ALU.mult, ALU.mult).then_inc(s_xn, 1)
                    if isinstance(dst, tuple):
                        for k in range(KD):
                            dve.wait_ge(s_hi, k + 1)
                            nc.vector.scalar_tensor_tensor(dst[1][:, k, :], ps[k % 2][:, 0:tiles * P],
                                                           gain[:, k:k + 1], dst[0][:, k, :].bitcast(F32),
                                                           ALU.mult, ALU.subtract).then_inc(s_ev[k % 2], 1)
                        return
                    for k in range(0, KD, 2):
                        dve.wait_ge(s_tp[0], k // 2 + 1)
                        nc.vector.tensor_scalar(dst[:, k, :], ps[0][:, 0:tiles * P],
                                                1.0 if gain is None else gain[:, k:k + 1], None,
                                                ALU.mult).then_inc(s_ev[0], 1)

                @block.tensor
                def _(pe):
                    for k in range(KD):
                        if k >= 2:
                            pe.wait_ge(s_ev[k % 2], k // 2)
                        for t in range(tiles):
                            if k == 0:
                                pe.wait_ge(s_xn, t + 1)
                            last = nc.tensor.transpose(ps[k % 2][:, t * P:(t + 1) * P],
                                                       xn[:, t, k::KD], ident[:])
                        last.then_inc(s_tp[k % 2], 1)

        mix = ExitStack()
        hT_hi, hT_lo = (sbuf(mix, "hT_" + n, [P, KD, N], F32R) for n in ("hi", "lo"))
        z_at = nc.sbuf_base
        zT = sbuf(mix, "zT", [P, 4 * FEAT_CHUNKS, N])
        zR = nc.alloc_sbuf_tensor_at("zR", [P, 4 * FEAT_CHUNKS, N], F32R, offset=z_at)
        ztok_at = nc.sbuf_base
        ztok = sbuf(mix, "ztok", [P, TOK_CHUNKS, T, BW])
        s_wr = sem("rel_written")
        FAR = N - 1 - REL_CLIP


        def load_first(sp):
            sp.dma_start(x_sb[:], a["x"].rearrange("b (t p) d -> p (b t) d", p=P)).then_inc(s_start, 16)
            sp.dma_start(ident[:], a["ident"]).then_inc(s_start, 16)
            sp.dma_start(small[:], a["small"]).then_inc(s_start, 16)
            sp.dma_start(rows[:], bass.AP(a["rows"].tensor, 0, [[0, P], [1, ROWS]])).then_inc(s_start, 16)
            sp.wait_ge(s_start, 64)

        load_first.ready = 64
        rms_transposed(stack, "rx", x_sb, T, gain_mix, (hT_hi, hT_lo), first=load_first)

        with ExitStack() as c:
            w_raw = [sbuf(c, f"mix_raw{b}", [P, KD, CW]) for b in range(2)]
            w_hi = [sbuf(c, f"mix_hi{b}", [P, KD, CW], F32R) for b in range(2)]
            w_lo = [sbuf(c, f"mix_lo{b}", [P, KD, CW], F32R) for b in range(2)]
            ps = [[psum(c, f"mix_ps{b}{j}") for j in range(2)] for b in range(2)]
            s_raw, s_hi, s_split, z_done, z_out = (
                [sem(f"mix_{n}{b}") for b in range(2)] for n in ("raw", "hi", "split", "z", "out"))
            wa_sb = sbuf(c, "wa_sb", [P, KB, P])
            wx_sb = sbuf(c, "wx_sb", [P, KB, P])
            sp_lam = sbuf(c, "sp_lam", [P, 4, KB])
            rel = sbuf(c, "rel_row", [HEADS, 5 * P])
            xc, tr, ti, sq = (ztok[:, m, :, :] for m in range(TOK_CHUNKS))
            ge = zT[:, DK0:DK0 + KB, :]
            psr = [psum(c, f"lru_r{i}") for i in range(2)]
            psi = [psum(c, f"lru_i{i}") for i in range(2)]
            s_w, s_xc, s_g, s_act, s_dve, s_sp, s_sq, s_in, s_th, s_e, s_y, s_yhi, s_ylo, s_rel, s_ext = (
                sem("lru_" + n) for n in ("w", "xc", "g", "act", "dve", "sp", "sq", "inner", "tanh", "e", "y",
                                          "yhi", "ylo", "rel", "ext"))
            ax, ag = zT[:, AX0:AX0 + KB, :], zT[:, AG0:AG0 + KB, :]
            GELU_C, GELU_S = 0.044715, float(np.sqrt(2.0 / np.pi))
            EARLY = 2
            block = c.enter_context(nc.Block())

            def load(sp, i, b):
                sp.wait_ge(s_split[b], i + 1)
                sp.dma_start(w_raw[b][:], a["w_mix"][bass.ds(i * 2 + b, 1)].rearrange(
                    "o (p k) n -> p (o k) n", k=KD)).then_inc(s_raw[b], 16)

            def hi_part(act, i, b):
                act.wait_ge(s_raw[b], i * 16 + 16)
                act.wait_ge(z_done[b], i * 2 + 2)
                nc.scalar.copy(w_hi[b][:], w_raw[b][:]).then_inc(s_hi[b], 1)

            def lo_part(dve, i, b):
                dve.wait_ge(s_hi[b], i + 1)
                nc.vector.tensor_tensor(w_lo[b][:], w_raw[b][:], w_hi[b][:].bitcast(F32), ALU.subtract
                                        ).then_inc(s_split[b], 1)

            def products(pe, i, b, token_major):
                pe.wait_ge(s_split[b], i + 2)
                pe.wait_ge(z_out[b], i * 2 + 2)
                for j in range(2):
                    for t in range(2 if token_major else 1):
                        for k in range(KD):
                            for n, (hp, wp) in enumerate(((hT_hi, w_hi[b]), (hT_hi, w_lo[b]), (hT_lo, w_hi[b]))):
                                ends = {"start": k == 0 and n == 0, "stop": k == KD - 1 and n == 2}
                                if token_major:
                                    at = (j * 2 + t) * P
                                    last = nc.tensor.matmul(ps[b][j][:, t * CW:(t + 1) * CW],
                                                            hp[:, k, at:at + P], wp[:, k, :], **ends)
                                else:
                                    last = nc.tensor.matmul(ps[b][j][:], wp[:, k, j * P:(j + 1) * P],
                                                            hp[:, k, :], **ends)
                    last.then_inc(z_done[b], 1)

            def empty(eng, copy, i, b, j, token_major):
                eng.wait_ge(z_done[b], i * 2 + (2 + j + 1))
                if token_major:
                    m = i - FEAT_CHUNKS
                    dst = ztok[:, bass.ds(m, 1), 2 * j:2 * j + 2, b * CW:(b + 1) * CW].rearrange(
                        "p o t n -> p (o t) n")
                    src = ps[b][j][:].rearrange("p (t n) -> p t n", t=2)
                else:
                    dst = zT[:, bass.ds(i * 4 + (b * 2 + j), 1), :].rearrange("p o n -> p (o n)")
                    src = ps[b][j][:]
                copy(dst, src).then_inc(z_out[b], 1)

            def over_chunks(eng, step, extras, first=0):
                with eng.Fori(0, EARLY) as i:
                    for b in range(2):
                        step(i, b, False, True)
                for ch in range(2 * EARLY, 2 * FEAT_CHUNKS):
                    step(ch // 2, ch % 2, False, True)
                    for x in extras.get(ch, ()):
                        x()
                with eng.Fori(FEAT_CHUNKS, FEAT_CHUNKS + TOK_CHUNKS - 1) as i:
                    for b in range(2):
                        step(i, b, True, True)
                for b in range(2):
                    step(FEAT_CHUNKS + TOK_CHUNKS - 1, b, True, b == 0)

            @block.sync
            def _(sp):
                for b in range(2):
                    sp.sem_inc(s_split[b], 1)
                    sp.sem_inc(z_done[b], 2)
                    sp.sem_inc(z_out[b], 2)
                with sp.Fori(0, EARLY) as i:
                    for b in range(2):
                        load(sp, i, b)
                sp.dma_start(rel[:, FAR:FAR + 2 * REL_CLIP + 1], a["rel_flipped"]).then_inc(s_rel, 16)
                sp.dma_start(wa_sb[:], a["wa_bd"].rearrange("t c d -> c t d")).then_inc(s_w, 16)
                sp.dma_start(wx_sb[:], a["wx_bd"].rearrange("t c d -> c t d")).then_inc(s_w, 16)
                with sp.Fori(EARLY, FEAT_CHUNKS) as i:
                    for b in range(2):
                        load(sp, i, b)
                sp.wait_ge(s_ext, 3)
                sp.dma_start(rel_dram, rel[:].unsqueeze(1).to_broadcast([HEADS, P, 5 * P])).then_inc(s_wr, 16)
                with sp.Fori(FEAT_CHUNKS, FEAT_CHUNKS + TOK_CHUNKS) as i:
                    for b in range(2):
                        load(sp, i, b)
                sp.wait_ge(s_wr, 16)

            @block.tensor
            def _(pe):
                def lru_gates(t):
                    if t == 0:
                        pe.wait_ge(s_w, 32)
                    pe.wait_ge(s_xc, t + 1)
                    if t >= 2:
                        pe.wait_ge(s_act, 3 * (t - 1))
                    nc.tensor.matmul(psr[t % 2][:], wa_sb[:, t, :], xc[:, t, :], start=True, stop=True)
                    nc.tensor.matmul(psi[t % 2][:], wx_sb[:, t, :], xc[:, t, :], start=True,
                                     stop=True).then_inc(s_g, 1)

                over_chunks(pe, lambda i, b, tm, more: products(pe, i, b, tm),
                            {6: [lambda: lru_gates(0), lambda: lru_gates(1)],
                             8: [lambda: lru_gates(2), lambda: lru_gates(3)]})

            @block.scalar
            def _(act):
                def step(i, b, tm, more):
                    if more:
                        hi_part(act, i + b, 1 - b)
                    if isinstance(i, int):
                        if i * 2 + b == 2 * DK0 // 4:
                            act.wait_ge(s_y, KB)
                        if i * 2 + b == 2 * (FEAT_CHUNKS - 1) + 1:
                            act.wait_ge(s_ylo, KB)
                    empty(act, nc.scalar.copy, i, b, 0, tm)

                def decay_terms():
                    nc.scalar.activation(sp_lam[:, 0, :], lru_lam, ACT.Abs).then_inc(s_e, 1)
                    act.wait_ge(s_e, 1)
                    nc.scalar.activation(sp_lam[:, 1, :], sp_lam[:, 0, :], ACT.Exp, scale=-1.0).then_inc(s_e, 1)

                def gelu_tanh():
                    act.wait_ge(s_in, 1)
                    nc.scalar.activation(ge, ge, ACT.Tanh, scale=GELU_S).then_inc(s_th, 1)

                def gates_tanh(t):
                    if t == 0:
                        act.wait_ge(s_sp, 1)
                    act.wait_ge(s_g, t + 1)
                    nc.scalar.activation(tr[:, t, :], psr[t % 2][:], ACT.Tanh, scale=0.5,
                                         bias=sp_lam[:, 2, t:t + 1]).then_inc(s_act, 1)
                    nc.scalar.activation(ti[:, t, :], psi[t % 2][:], ACT.Tanh, scale=0.5,
                                         bias=sp_lam[:, 3, t:t + 1]).then_inc(s_act, 1)
                    act.wait_ge(s_act, 3 * t + 2)
                    nc.scalar.activation(tr[:, t, :], tr[:, t, :], ACT.Tanh, scale=sp_lam[:, 0, t:t + 1],
                                         bias=sp_lam[:, 0, t:t + 1]).then_inc(s_act, 1)

                def roots():
                    act.wait_ge(s_act, 3 * KB)
                    for t in range(KB):
                        nc.scalar.activation(sq[:, t, :], tr[:, t, :], ACT.Sqrt).then_inc(s_sq, 1)

                def y_hi(t):
                    act.wait_ge(s_y, t + 1)
                    nc.scalar.copy(zR[:, AX0 + t, :], tr[:, t, :]).then_inc(s_yhi, 1)

                hi_part(act, 0, 0)
                over_chunks(act, step, {
                    4: [decay_terms], 6: [gelu_tanh],
                    7: [lambda: gates_tanh(0), lambda: gates_tanh(1)],
                    9: [lambda: gates_tanh(2), lambda: gates_tanh(3), roots],
                    11: [lambda: y_hi(0)], 12: [lambda: y_hi(1)], 13: [lambda: y_hi(2), lambda: y_hi(3)]})

            @block.vector
            def _(dve):
                do = Steps(dve, s_dve)

                def step(i, b, tm, more):
                    if more:
                        lo_part(dve, i + b, 1 - b)
                    empty(dve, nc.vector.tensor_copy, i, b, 1, tm)

                def rel_rows():
                    dve.wait_ge(s_rel, 16)
                    nc.vector.memset(rel[:, 0:FAR], 0.0).then_inc(s_ext, 1)
                    dve.wait_ge(s_ext, 1)
                    nc.vector.tensor_scalar(rel[:, 0:FAR], rel[:, 0:FAR], rel[:, FAR:FAR + 1], None,
                                            ALU.add).then_inc(s_ext, 1)
                    dve.wait_ge(s_ext, 2)
                    nc.vector.tensor_scalar(rel[:], rel[:], float(HD) ** 0.5, None, ALU.mult).then_inc(s_ext, 1)

                def convolve(t):
                    if t == 0:
                        for b in range(2):
                            dve.wait_ge(z_out[b], 2 + 2 * EARLY)
                    do.after(nc.vector.tensor_scalar(xc[:, t, :], ax[:, t, :], conv_w[3][:, t:t + 1],
                                                     conv_b[:, t:t + 1], ALU.mult, ALU.add))
                    for j in (2, 1, 0):
                        sh = 3 - j
                        ins = nc.vector.scalar_tensor_tensor(xc[:, t, sh:N], ax[:, t, 0:N - sh],
                                                             conv_w[j][:, t:t + 1], xc[:, t, sh:N],
                                                             ALU.mult, ALU.add)
                        if j:
                            do.after(ins)
                    ins.then_inc(s_xc, 1)

                def gelu_inner():
                    do.after(nc.vector.tensor_tensor(ge, ag, ag, ALU.mult))
                    do.after(nc.vector.tensor_scalar(ge, ge, GELU_C, 1.0, ALU.mult, ALU.add))
                    nc.vector.tensor_tensor(ge, ge, ag, ALU.mult).then_inc(s_in, 1)

                def softplus():
                    dve.wait_ge(s_e, 2)
                    e, s1, s2 = sp_lam[:, 1, :], sp_lam[:, 2, :], sp_lam[:, 3, :]
                    acc = sp_lam[:, 0, :]
                    do.after(nc.vector.tensor_scalar(s1, e, 2.0, None, ALU.add))
                    do.after(nc.vector.reciprocal(s1, s1))
                    do.after(nc.vector.tensor_tensor(s1, s1, e, ALU.mult))
                    do.after(nc.vector.tensor_tensor(s2, s1, s1, ALU.mult))
                    do.after(nc.vector.tensor_scalar(acc, s2, 1.0 / 17, 1.0 / 15, ALU.mult, ALU.add))
                    for m in (13, 11, 9, 7, 5, 3, 1):
                        do.after(nc.vector.tensor_tensor(acc, acc, s2, ALU.mult))
                        do.after(nc.vector.tensor_scalar(acc, acc, 1.0 / m, None, ALU.add))
                    do.after(nc.vector.tensor_tensor(acc, acc, s1, ALU.mult))
                    do.after(nc.vector.tensor_scalar(s1, lru_lam, -1.0, 0.0, ALU.mult, ALU.max))
                    do.after(nc.vector.scalar_tensor_tensor(acc, acc, 2.0, s1, ALU.mult, ALU.add))
                    do.after(nc.vector.tensor_scalar(acc, acc, 2.0, None, ALU.mult))
                    do.after(nc.vector.tensor_scalar(s1, lru_ba, 0.5, None, ALU.mult))
                    nc.vector.tensor_scalar(s2, lru_bx, 0.5, None, ALU.mult).then_inc(s_sp, 1)

                def gelu():
                    dve.wait_ge(s_th, 1)
                    do.after(nc.vector.scalar_tensor_tensor(ge, ge, 1.0, ag, ALU.add, ALU.mult))

                def recur(t):
                    dve.wait_ge(s_sq, t + 1)
                    do.after(nc.vector.tensor_scalar(tr[:, t, :], tr[:, t, :], 1.0, None, ALU.add))
                    do.after(nc.vector.reciprocal(tr[:, t, :], tr[:, t, :]))
                    do.after(nc.vector.tensor_tensor(sq[:, t, :], sq[:, t, :], tr[:, t, :], ALU.mult))
                    do.after(nc.vector.tensor_scalar(tr[:, t, :], tr[:, t, :], 2.0, -1.0, ALU.mult, ALU.add))
                    do.after(nc.vector.scalar_tensor_tensor(ti[:, t, :], ti[:, t, :], 1.0, xc[:, t, :],
                                                            ALU.add, ALU.mult))
                    do.after(nc.vector.tensor_tensor(sq[:, t, :], sq[:, t, :], ti[:, t, :], ALU.mult))
                    do.after(nc.vector.tensor_tensor_scan(xc[:, t, :], tr[:, t, :], sq[:, t, :], 0.0,
                                                          ALU.mult, ALU.add))
                    nc.vector.scalar_tensor_tensor(tr[:, t, :], xc[:, t, :], 0.5, ge[:, t, :],
                                                   ALU.mult, ALU.mult).then_inc(s_y, 1)

                def y_lo(t):
                    dve.wait_ge(s_yhi, t + 1)
                    nc.vector.tensor_tensor(zR[:, AG0 + t, :], tr[:, t, :], zR[:, AX0 + t, :].bitcast(F32),
                                            ALU.subtract
                                            ).then_inc(s_ylo, 1)

                lo_part(dve, 0, 0)
                over_chunks(dve, step, {
                    4: [rel_rows, softplus, lambda: convolve(0)], 5: [lambda: convolve(1), lambda: convolve(2)],
                    6: [gelu_inner, lambda: convolve(3)], 8: [gelu],
                    9: [lambda: recur(0)], 10: [lambda: recur(1)], 11: [lambda: recur(2), lambda: y_lo(0)],
                    12: [lambda: recur(3), lambda: y_lo(1)], 13: [lambda: y_lo(2)], 14: [lambda: y_lo(3)]})

        def y_turn(pe, s_y, s_tp, s_lo, src, ps, ready):
            pe.wait_ge(s_y, ready)
            for k in range(KB):
                if k >= 2:
                    pe.wait_ge(s_lo, k - 1)
                for t in range(T):
                    last = nc.tensor.transpose(ps[k % 2][:, t * P:(t + 1) * P], src[:, t, k * P:(k + 1) * P],
                                               ident[:])
                last.then_inc(s_tp, 1)

        def y_hi_parts(act, s_tp, s_hi, at, ps):
            for k in range(KB):
                act.wait_ge(s_tp, k + 1)
                nc.scalar.copy(zR[:, at + k, :], ps[k % 2][:]).then_inc(s_hi, 1)

        def y_lo_parts(dve, s_hi, s_lo, at, ps):
            for k in range(KB):
                dve.wait_ge(s_hi, k + 1)
                nc.vector.tensor_tensor(zR[:, at + KB + k, :], ps[k % 2][:], zR[:, at + k, :].bitcast(F32),
                                        ALU.subtract
                                        ).then_inc(s_lo, 1)

        with ExitStack() as c:
            bias = sbuf(c, "rel_bias", [P, HEADS, N])
            neg = [sbuf(c, f"b_neg{i}", [P, N]) for i in range(2)]
            pr = [sbuf(c, f"b_p{i}", [P, N]) for i in range(3)]
            pT = [sbuf(c, f"b_pT{i}", [P, N]) for i in range(2)]
            otok = sbuf(c, "b_otok", [P, T, BW])
            nmax = sbuf(c, "b_nmax", [P, HEADS * T])
            rsum = sbuf(c, "b_rsum", [P, HEADS * T])
            ps_s = [psum(c, f"b_s{i}") for i in range(3)]
            ps_t = [psum(c, f"b_t{i}") for i in range(2)]
            ps_o = [psum(c, f"b_o{i}") for i in range(2)]
            s_bias, s_mask, s_s, s_neg, s_exp, s_t, s_pt, s_pv, s_o, s_dve, s_tp, s_yhi, s_lo = (
                sem("b_" + n) for n in ("bias", "mask", "s", "neg", "exp", "t", "pt", "pv", "o", "dve", "tp", "yhi",
                                        "ylo"))
            U = HEADS * T
            SC = float(HD) ** -0.5
            block = c.enter_context(nc.Block())

            @block.sync
            def _(sp):
                for h in range(HEADS):
                    sp.dma_start(bias[:, h, :], bass.AP(rel_dram.tensor, h * P * 5 * P + P - 1,
                                                        [[5 * P - 1, P], [1, N]])).then_inc(s_bias, 16)

            @block.gpsimd
            def _(pool):
                pool.wait_ge(s_bias, 16 * HEADS)
                nc.gpsimd.memset(bias[0:CHUNK, :, N - CHUNK:N], MASKED).then_inc(s_mask, 1)

            @block.tensor
            def _(pe):
                for st in range(U + 3):
                    if st < U:
                        h, t = divmod(st, T)
                        lo = (h % 2) * HD
                        if st >= 3:
                            pe.wait_ge(s_neg, st - 2)
                        nc.tensor.matmul(ps_s[st % 3][:, 0:(t + 1) * P],
                                         zT[lo:lo + HD, BQ0 + h // 2, t * P:(t + 1) * P],
                                         zT[lo:lo + HD, BK0 + h // 2, 0:(t + 1) * P],
                                         start=True, stop=True).then_inc(s_s, 1)
                    if 0 <= st - 2 < U:
                        u = st - 2
                        pe.wait_ge(s_exp, u + 1)
                        if u >= 2:
                            pe.wait_ge(s_pt, u - 1)
                        for b in range(u % T + 1):
                            last = nc.tensor.transpose(ps_t[u % 2][:, b * P:(b + 1) * P],
                                                       pr[u % 3][:, b * P:(b + 1) * P], ident[:])
                        last.then_inc(s_t, 1)
                    if 0 <= st - 3:
                        u = st - 3
                        h, t = divmod(u, T)
                        pe.wait_ge(s_pt, u + 1)
                        if t == 0 and h >= 2:
                            pe.wait_ge(s_o, h - 1)
                        for b in range(t + 1):
                            last = nc.tensor.matmul(ps_o[h % 2][:, t * HD:(t + 1) * HD],
                                                    pT[u % 2][:, b * P:(b + 1) * P],
                                                    ztok[:, BV, b, h * HD:(h + 1) * HD],
                                                    start=(b == 0), stop=(b == t))
                        last.then_inc(s_pv, 1)
                y_turn(pe, s_o, s_tp, s_lo, otok, ps_t, HEADS)

            @block.scalar
            def _(act):
                for u in range(U):
                    w = (u % T + 1) * P
                    act.wait_ge(s_neg, u + 1)
                    if u >= 3:
                        act.wait_ge(s_t, u - 2)
                    nc.scalar.activation(pr[u % 3][:, 0:w], neg[u % 2][:, 0:w], ACT.Exp, scale=-1.0,
                                         bias=nmax[:, u:u + 1], accum_out=rsum[:, u:u + 1]).then_inc(s_exp, 1)
                y_hi_parts(act, s_tp, s_yhi, BQ0, ps_t)

            @block.vector
            def _(dve):
                do = Steps(dve, s_dve)
                dve.wait_ge(s_mask, 1)
                for st in range(U + 4):
                    if st < U:
                        h, t = divmod(st, T)
                        w = (t + 1) * P
                        dve.wait_ge(s_s, st + 1)
                        if st >= 2:
                            dve.wait_ge(s_exp, st - 1)
                        nc.vector.tensor_tensor_reduce(neg[st % 2][:, 0:w], ps_s[st % 3][:, 0:w],
                                                       bias[:, h, N - w:N], -SC, 3e38, ALU.add, ALU.min,
                                                       nmax[:, st:st + 1]).then_inc(s_neg, 1)
                    if 0 <= st - 2 < U:
                        u = st - 2
                        w = (u % T + 1) * P
                        dve.wait_ge(s_t, u + 1)
                        if u >= 2:
                            dve.wait_ge(s_pv, u - 1)
                        nc.vector.tensor_copy(pT[u % 2][:, 0:w], ps_t[u % 2][:, 0:w]).then_inc(s_pt, 1)
                    if st >= 4 and (st - 4) % T == T - 1:
                        h = (st - 4) // T
                        rs = rsum[:, h * T:(h + 1) * T]
                        dve.wait_ge(s_pv, h * T + T)
                        do.after(nc.vector.reciprocal(rs, rs))
                        nc.vector.tensor_tensor(otok[:, :, h * HD:(h + 1) * HD],
                                                ps_o[h % 2][:, 0:T * HD].rearrange("p (t e) -> p t e", t=T),
                                                rs.unsqueeze(2).to_broadcast([P, T, HD]),
                                                ALU.mult).then_inc(s_o, 1)
                y_lo_parts(dve, s_yhi, s_lo, BQ0, ps_t)

        with ExitStack() as c:
            decay = sbuf(c, "decay", [P, HEADS, N])
            pd = [sbuf(c, f"c_p{i}", [P, 10 * P]) for i in range(2)]
            otok = sbuf(c, "c_otok", [P, T, BW])
            tmp = sbuf(c, "c_tmp", [P, T, BW])
            gate = sbuf(c, "c_gate", [P, T, BW])
            mu = sbuf(c, "c_mu", [P, T * HEADS])
            var = sbuf(c, "c_var", [P, T * HEADS])
            ps_s = [psum(c, f"c_s{i}") for i in range(4)]
            ps_o = [psum(c, f"c_o{i}") for i in range(2)]
            ps_t = [psum(c, f"c_t{i}") for i in range(2)]
            s_ld, s_s, s_p, s_pv, s_o, s_dve, s_v, s_sq, s_th, s_y, s_tp, s_yhi, s_lo = (
                sem("c_" + n) for n in ("ld", "s", "p", "pv", "o", "dve", "var", "sqrt", "tanh", "y", "tp", "yhi",
                                        "ylo"))
            off = [0, 4 * P, 7 * P, 9 * P]
            block = c.enter_context(nc.Block())

            @block.sync
            def _(sp):
                sp.dma_start(decay[:], a["decay"]).then_inc(s_ld, 16)

            @block.tensor
            def _(pe):
                def scores(h):
                    lo = (h % 2) * HD
                    for j in range(T):
                        u = h * T + j
                        if u >= 4:
                            pe.wait_ge(s_p, u - 3)
                        nc.tensor.matmul(ps_s[j][:, 0:N - j * P],
                                         zT[lo:lo + HD, CK0 + h // 2, j * P:(j + 1) * P],
                                         zT[lo:lo + HD, CQ0 + h // 2, j * P:N],
                                         start=True, stop=True).then_inc(s_s, 1)

                def outputs(h):
                    if h >= 2:
                        pe.wait_ge(s_o, h - 1)
                    pe.wait_ge(s_p, h * T + T)
                    for i in range(T):
                        for j in range(i + 1):
                            o = off[j] + (i - j) * P
                            last = nc.tensor.matmul(ps_o[h % 2][:, i * HD:(i + 1) * HD],
                                                    pd[h % 2][:, o:o + P],
                                                    ztok[:, CV, j, h * HD:(h + 1) * HD],
                                                    start=(j == 0), stop=(j == i))
                    last.then_inc(s_pv, 1)

                for st in range(HEADS + 1):
                    if st < HEADS:
                        scores(st)
                    if st:
                        outputs(st - 1)
                y_turn(pe, s_y, s_tp, s_lo, otok, ps_t, 1)

            @block.scalar
            def _(act):
                nc.scalar.activation(gate[:], ztok[:, CG, :, :], ACT.Tanh, scale=0.5).then_inc(s_th, 1)
                act.wait_ge(s_v, 1)
                nc.scalar.activation(var[:], var[:], ACT.Sqrt).then_inc(s_sq, 1)
                y_hi_parts(act, s_tp, s_yhi, CQ0, ps_t)

            @block.vector
            def _(dve):
                do = Steps(dve, s_dve)
                dve.wait_ge(s_ld, 16)
                for st in range(HEADS + 1):
                    if st < HEADS:
                        if st >= 2:
                            dve.wait_ge(s_pv, st - 1)
                        for j in range(T):
                            dve.wait_ge(s_s, st * T + j + 1)
                            nc.vector.tensor_tensor(pd[st % 2][:, off[j]:off[j] + N - j * P],
                                                    ps_s[j][:, 0:N - j * P], decay[:, st, 0:N - j * P],
                                                    ALU.mult).then_inc(s_p, 1)
                    if st:
                        h = st - 1
                        dve.wait_ge(s_pv, h + 1)
                        nc.vector.tensor_copy(otok[:, :, h * HD:(h + 1) * HD],
                                              ps_o[h % 2][:, 0:T * HD].rearrange("p (t e) -> p t e", t=T)
                                              ).then_inc(s_o, 1)
                dve.wait_ge(s_o, HEADS)
                o3 = otok[:].rearrange("p t (h e) -> p (t h) e", e=HD)
                t3 = tmp[:].rearrange("p t (h e) -> p (t h) e", e=HD)
                wide = [P, T * HEADS, HD]
                do.after(nc.vector.tensor_reduce(mu[:], o3, AX_X, ALU.add))
                do.after(nc.vector.tensor_scalar(mu[:], mu[:], 1.0 / HD, None, ALU.mult))
                do.after(nc.vector.tensor_tensor(o3, o3, mu[:].unsqueeze(2).to_broadcast(wide), ALU.subtract))
                do.after(nc.vector.tensor_tensor(t3, o3, o3, ALU.mult))
                do.after(nc.vector.tensor_reduce(var[:], t3, AX_X, ALU.add))
                nc.vector.tensor_scalar(var[:], var[:], 1.0 / HD, GN_EPS, ALU.mult, ALU.add).then_inc(s_v, 1)
                dve.wait_ge(s_th, 1)
                do.after(nc.vector.scalar_tensor_tensor(gate[:], gate[:], 1.0, ztok[:, CG, :, :],
                                                        ALU.add, ALU.mult))
                dve.wait_ge(s_sq, 1)
                do.after(nc.vector.reciprocal(var[:], var[:]))
                do.after(nc.vector.tensor_tensor(o3, o3, var[:].unsqueeze(2).to_broadcast(wide), ALU.mult))
                nc.vector.scalar_tensor_tensor(otok[:], otok[:], 0.5, gate[:], ALU.mult, ALU.mult
                                               ).then_inc(s_y, 1)
                y_lo_parts(dve, s_yhi, s_lo, CQ0, ps_t)

        with ExitStack() as c:
            alibi = sbuf(c, "alibi", [P, DIFF_HEADS, N])
            neg = [[sbuf(c, f"d_neg{i}{m}", [P, N]) for m in range(2)] for i in range(2)]
            pr = [[sbuf(c, f"d_p{i}{m}", [P, N]) for m in range(2)] for i in range(2)]
            pT = [sbuf(c, f"d_pT{i}", [P, N]) for i in range(2)]
            otok = sbuf(c, "d_otok", [P, T, BW])
            tmp = sbuf(c, "d_tmp", [P, T, BW])
            U = DIFF_HEADS * T
            nmax = sbuf(c, "d_nmax", [P, 2, U])
            rsum = sbuf(c, "d_rsum", [P, 2, U])
            coef = sbuf(c, "d_coef", [P, U])
            lam = sbuf(c, "d_lam", [P, 4])
            lamt = sbuf(c, "d_lamt", [P, HD])
            ms = sbuf(c, "d_ms", [P, U])
            ps_s = [[psum(c, f"d_s{i}{m}") for m in range(2)] for i in range(2)]
            ps_t = [psum(c, f"d_t{i}") for i in range(2)]
            ps_o = [psum(c, f"d_o{i}") for i in range(2)]
            s_ld, s_s, s_neg, s_exp, s_at, s_t, s_pt, s_pv, s_o, s_dve, s_lam, s_le, s_v, s_sq, s_y, s_tp, s_yhi, s_lo = (
                sem("d_" + n) for n in ("ld", "s", "neg", "exp", "attn", "t", "pt", "pv", "o", "dve", "lam", "lexp",
                                        "var", "sqrt", "y", "tp", "yhi", "ylo"))
            SC = float(HD) ** -0.5
            block = c.enter_context(nc.Block())

            @block.sync
            def _(sp):
                sp.dma_start(alibi[:], a["alibi"]).then_inc(s_ld, 16)

            @block.tensor
            def _(pe):
                for st in range(U + 3):
                    if st < U:
                        h, t = divmod(st, T)
                        if st >= 2:
                            pe.wait_ge(s_neg, 2 * (st - 1))
                        for m in range(2):
                            nc.tensor.matmul(ps_s[st % 2][m][:, 0:(t + 1) * P],
                                             zT[m * HD:(m + 1) * HD, DQ0 + h, t * P:(t + 1) * P],
                                             zT[m * HD:(m + 1) * HD, DK0 + h, 0:(t + 1) * P],
                                             start=True, stop=True).then_inc(s_s, 1)
                    if 0 <= st - 2 < U:
                        u = st - 2
                        pe.wait_ge(s_at, u + 1)
                        if u >= 2:
                            pe.wait_ge(s_pt, u - 1)
                        for b in range(u % T + 1):
                            last = nc.tensor.transpose(ps_t[u % 2][:, b * P:(b + 1) * P],
                                                       pr[u % 2][0][:, b * P:(b + 1) * P], ident[:])
                        last.then_inc(s_t, 1)
                    if 0 <= st - 3:
                        u = st - 3
                        h, t = divmod(u, T)
                        pe.wait_ge(s_pt, u + 1)
                        if t == 0 and h >= 2:
                            pe.wait_ge(s_o, h - 1)
                        for b in range(t + 1):
                            last = nc.tensor.matmul(ps_o[h % 2][:, t * P:(t + 1) * P],
                                                    pT[u % 2][:, b * P:(b + 1) * P],
                                                    ztok[:, DV, b, h * P:(h + 1) * P],
                                                    start=(b == 0), stop=(b == t))
                        last.then_inc(s_pv, 1)
                y_turn(pe, s_y, s_tp, s_lo, otok, ps_t, 1)

            @block.scalar
            def _(act):
                act.wait_ge(s_lam, 1)
                nc.scalar.activation(lam[:, 0:2], lam[:, 0:2], ACT.Exp).then_inc(s_le, 1)
                for u in range(U):
                    w = (u % T + 1) * P
                    if u >= 2:
                        act.wait_ge(s_t, u - 1)
                    for m in range(2):
                        act.wait_ge(s_neg, 2 * u + m + 1)
                        nc.scalar.activation(pr[u % 2][m][:, 0:w], neg[u % 2][m][:, 0:w], ACT.Exp, scale=-1.0,
                                             bias=nmax[:, m, u:u + 1],
                                             accum_out=rsum[:, m, u:u + 1]).then_inc(s_exp, 1)
                act.wait_ge(s_v, 1)
                nc.scalar.activation(ms[:], ms[:], ACT.Sqrt).then_inc(s_sq, 1)
                y_hi_parts(act, s_tp, s_yhi, DQ0, ps_t)

            @block.vector
            def _(dve):
                do = Steps(dve, s_dve)
                for i in range(2):
                    ins = nc.vector.tensor_tensor_reduce(lamt[:], lam_vecs[:, 2 * i * HD:(2 * i + 1) * HD],
                                                         lam_vecs[:, (2 * i + 1) * HD:(2 * i + 2) * HD],
                                                         1.0, 0.0, ALU.mult, ALU.add, lam[:, i:i + 1])
                    if i == 0:
                        do.after(ins)
                ins.then_inc(s_lam, 1)
                dve.wait_ge(s_le, 1)
                do.after(nc.vector.tensor_tensor(lam[:, 2:3], lam[:, 1:2], lam[:, 0:1], ALU.subtract))
                do.after(nc.vector.tensor_scalar(lam[:, 3:4], lam[:, 2:3], -LAM_INIT, None, ALU.add))
                dve.wait_ge(s_ld, 16)
                for st in range(U + 4):
                    if st < U:
                        h, t = divmod(st, T)
                        w = (t + 1) * P
                        if st >= 2:
                            dve.wait_ge(s_exp, 2 * (st - 1))
                        for m in range(2):
                            dve.wait_ge(s_s, 2 * st + m + 1)
                            nc.vector.tensor_tensor_reduce(neg[st % 2][m][:, 0:w], ps_s[st % 2][m][:, 0:w],
                                                           alibi[:, h, N - w:N], -SC, 3e38, ALU.add, ALU.min,
                                                           nmax[:, m, st:st + 1]).then_inc(s_neg, 1)
                    if 0 <= st - 1 < U:
                        u = st - 1
                        w = (u % T + 1) * P
                        dve.wait_ge(s_exp, 2 * u + 2)
                        do.after(nc.vector.reciprocal(coef[:, u:u + 1], rsum[:, 1, u:u + 1]))
                        do.after(nc.vector.tensor_scalar(coef[:, u:u + 1], coef[:, u:u + 1],
                                                         rsum[:, 0, u:u + 1], lam[:, 3:4], ALU.mult, ALU.mult))
                        nc.vector.scalar_tensor_tensor(pr[u % 2][0][:, 0:w], pr[u % 2][1][:, 0:w],
                                                       coef[:, u:u + 1], pr[u % 2][0][:, 0:w],
                                                       ALU.mult, ALU.add).then_inc(s_at, 1)
                    if 0 <= st - 2 < U:
                        u = st - 2
                        w = (u % T + 1) * P
                        dve.wait_ge(s_t, u + 1)
                        if u >= 2:
                            dve.wait_ge(s_pv, u - 1)
                        nc.vector.tensor_copy(pT[u % 2][:, 0:w], ps_t[u % 2][:, 0:w]).then_inc(s_pt, 1)
                    if st >= 4 and (st - 4) % T == T - 1:
                        h = (st - 4) // T
                        rs = rsum[:, 0, h * T:(h + 1) * T]
                        dve.wait_ge(s_pv, h * T + T)
                        do.after(nc.vector.reciprocal(rs, rs))
                        nc.vector.tensor_tensor(otok[:, :, h * P:(h + 1) * P],
                                                ps_o[h % 2][:].rearrange("p (t e) -> p t e", t=T),
                                                rs.unsqueeze(2).to_broadcast([P, T, P]),
                                                ALU.mult).then_inc(s_o, 1)
                dve.wait_ge(s_o, DIFF_HEADS)
                o3 = otok[:].rearrange("p t (h e) -> p (t h) e", e=P)
                t3 = tmp[:].rearrange("p t (h e) -> p (t h) e", e=P)
                wide = [P, U, P]
                do.after(nc.vector.tensor_tensor(t3, o3, o3, ALU.mult))
                do.after(nc.vector.tensor_reduce(ms[:], t3, AX_X, ALU.add))
                nc.vector.tensor_scalar(ms[:], ms[:], 1.0 / P, GN_EPS, ALU.mult, ALU.add).then_inc(s_v, 1)
                dve.wait_ge(s_sq, 1)
                do.after(nc.vector.reciprocal(ms[:], ms[:]))
                do.after(nc.vector.tensor_scalar(ms[:], ms[:], 1.0 - LAM_INIT, None, ALU.mult))
                do.after(nc.vector.tensor_tensor(o3, o3, ms[:].unsqueeze(2).to_broadcast(wide), ALU.mult))
                nc.vector.tensor_tensor(o3, o3, subln.unsqueeze(1).to_broadcast(wide), ALU.mult).then_inc(s_y, 1)
                y_lo_parts(dve, s_yhi, s_lo, DQ0, ps_t)

        with ExitStack() as c:
            w_raw = [sbuf(c, f"g_raw{b}", [P, UNIT]) for b in range(2)]
            w_hi = [sbuf(c, f"g_hi{b}", [P, UNIT], F32R) for b in range(2)]
            w_lo = [sbuf(c, f"g_lo{b}", [P, UNIT], F32R) for b in range(2)]
            tg = [sbuf(c, f"g_t{b}", [P, N]) for b in range(4)]
            m_sum = [sbuf(c, f"g_m{b}", [P, N]) for b in range(2)]
            m_hi, m_lo = (nc.alloc_sbuf_tensor_at(f"merged_{n}", [P, KD, N], F32R, offset=ztok_at + o)
                          for n, o in (("hi", 0), ("lo", KD * N * 4)))
            Y_HI = (AX0, BQ0, CQ0, DQ0)
            ps_g = [psum(c, f"g_g{b}") for b in range(2)]
            ps_b = [psum(c, f"g_p{b}") for b in range(2)]
            ps_w = [[psum(c, f"o_ps{t}") for t in range(T)], [ps_g[0], ps_g[1], ps_b[0], ps_b[1]]]
            s_raw, s_hi, s_split, s_unit = ([sem(f"g_{n}{b}") for b in range(2)] for n in ("raw", "hi", "split", "unit"))
            s_g, s_t, s_mul = ([sem(f"g_{n}{b}") for b in range(4)] for n in ("gate", "tanh", "mul"))
            s_sum, s_mhi, s_mlo, s_x = sem("g_sum"), sem("g_mhi"), sem("g_mlo"), sem("o_x")
            PIECES = 2 * KD // 2
            block = c.enter_context(nc.Block())

            def hi_part(act, n, b, w=UNIT):
                act.wait_ge(s_raw[b], n * 16 + 16)
                act.wait_ge(s_unit[b], n + 1)
                nc.scalar.copy(w_hi[b][:, 0:w], w_raw[b][:, 0:w]).then_inc(s_hi[b], 1)

            def lo_part(dve, n, b, w=UNIT):
                dve.wait_ge(s_hi[b], n + 1)
                nc.vector.tensor_tensor(w_lo[b][:, 0:w], w_raw[b][:, 0:w], w_hi[b][:, 0:w].bitcast(F32),
                                        ALU.subtract).then_inc(s_split[b], 1)

            def part_after(part, i, br, last=False):
                if last and br == 3:
                    part(2 * KD, 0, w=PIECE)
                else:
                    part(i * 2 + (br + 1) // 2, (br + 1) % 2)

            def passes(x_hi, x_lo, hi, lo):
                return (x_hi, hi), (x_hi, lo), (x_lo, hi)

            @block.sync
            def _(sp):
                for q in (*s_split, *s_unit, *s_t, *s_mul):
                    sp.sem_inc(q, 1)
                with sp.Fori(0, KD) as i:
                    for br in range(4):
                        b = br % 2
                        sp.wait_ge(s_split[b], i * 2 + (br // 2 + 1))
                        sp.dma_start(w_raw[b][:], a["w_gb"][bass.ds(i * 4 + br, 1)].rearrange("o p n -> p (o n)")
                                     ).then_inc(s_raw[b], 16)
                for u in range(PIECES):
                    b = u % 2
                    sp.wait_ge(s_split[b], 2 * KD + u // 2 + 1)
                    sp.dma_start(w_raw[b][:, 0:PIECE], a["w_out_pieces"][u]).then_inc(s_raw[b], 16)

            @block.tensor
            def _(pe):
                with pe.Fori(0, KD) as i:
                    for br in range(4):
                        b = br % 2
                        pe.wait_ge(s_split[b], i * 2 + (br // 2 + 2))
                        pe.wait_ge(s_t[(br + 2) % 4], i + (2 if br >= 2 else 1))
                        for k in range(KD):
                            for n, (hp, wp) in enumerate(passes(hT_hi, hT_lo, w_hi[b], w_lo[b])):
                                last = nc.tensor.matmul(ps_g[b][:], wp[:, k * P:(k + 1) * P], hp[:, k, :],
                                                        start=(k == 0 and n == 0), stop=(k == KD - 1 and n == 2))
                        last.then_inc(s_g[br], 1)
                        pe.wait_ge(s_mul[(br + 2) % 4], i + (2 if br >= 2 else 1))
                        for k in range(KB):
                            for n, (at, wp) in enumerate(passes(Y_HI[br] + k, Y_HI[br] + KB + k,
                                                                w_hi[b], w_lo[b])):
                                last = nc.tensor.matmul(ps_b[b][:], wp[:, (KD + k) * P:(KD + k + 1) * P],
                                                        zR[:, at, :], start=(k == 0 and n == 0),
                                                        stop=(k == KB - 1 and n == 2))
                        last.then_inc(s_unit[b], 1)
                for u in range(PIECES):
                    b, half, pair = u % 2, u // (KD // 2), u % (KD // 2)
                    pe.wait_ge(s_split[b], 2 * KD + u // 2 + 2)
                    pe.wait_ge(s_mlo, min(KD, 2 * pair + 2) if half == 0 else KD)
                    if u == PIECES // 2:
                        for q in s_mul[2:]:
                            pe.wait_ge(q, KD + 1)
                    for t in range(T):
                        for kk in range(2):
                            k = pair * 2 + kk
                            for n, (mp, wp) in enumerate(passes(m_hi, m_lo, w_hi[b], w_lo[b])):
                                last = nc.tensor.matmul(ps_w[half][t][:], mp[:, k, t * P:(t + 1) * P],
                                                        wp[:, kk * BW:(kk + 1) * BW],
                                                        start=(k == 0 and n == 0), stop=(k == KD - 1 and n == 2))
                    last.then_inc(s_unit[b], 1)

            @block.scalar
            def _(act):
                def part(n, b, w=UNIT):
                    hi_part(act, n, b, w)

                def tile(i, m, last):
                    for br in range(4):
                        part_after(part, i, br, last)
                        act.wait_ge(s_g[br], i + 1)
                        act.wait_ge(s_mul[br], i + 1)
                        nc.scalar.activation(tg[br][:], ps_g[br % 2][:], ACT.Tanh, scale=0.5).then_inc(s_t[br], 1)
                    act.wait_ge(s_sum, i * 3 + 3)
                    nc.scalar.copy(m_hi[:, bass.ds(i, 1), :].rearrange("p o n -> p (o n)"), m_sum[m][:]
                                   ).then_inc(s_mhi, 1)

                hi_part(act, 0, 0)
                with act.Fori(0, KD // 2 - 1) as i:
                    tile(i * 2, 0, False)
                    tile(i * 2 + 1, 1, False)
                tile(KD - 2, 0, False)
                tile(KD - 1, 1, True)
                for u in range(1, PIECES):
                    hi_part(act, 2 * KD + u // 2, u % 2, PIECE)

            @block.vector
            def _(dve):
                def part(n, b, w=UNIT):
                    lo_part(dve, n, b, w)

                def tile(i, m, last):
                    m_sb = m_sum[m][:]
                    for br in range(4):
                        part_after(part, i, br, last)
                        b = br % 2
                        dve.wait_ge(s_t[br], i + 2)
                        dve.wait_ge(s_unit[b], i * 2 + (br // 2 + 2))
                        nc.vector.scalar_tensor_tensor(m_sb if br == 0 else tg[br][:], tg[br][:], 1.0,
                                                       ps_b[b][:], ALU.add, ALU.mult).then_inc(s_mul[br], 1)
                        if br:
                            dve.wait_ge(s_mul[br], i + 2)
                            if br == 1:
                                dve.wait_ge(s_mul[0], i + 2)
                            else:
                                dve.wait_ge(s_sum, i * 3 + (br - 1))
                            nc.vector.tensor_tensor(m_sb, m_sb, tg[br][:], ALU.add).then_inc(s_sum, 1)
                    dve.wait_ge(s_mhi, i + 1)
                    o = bass.ds(i, 1)
                    nc.vector.tensor_tensor(m_lo[:, o, :].rearrange("p o n -> p (o n)"), m_sb,
                                            m_hi[:, o, :].rearrange("p o n -> p (o n)").bitcast(F32),
                                            ALU.subtract).then_inc(s_mlo, 1)

                lo_part(dve, 0, 0)
                with dve.Fori(0, KD // 2 - 1) as i:
                    tile(i * 2, 0, False)
                    tile(i * 2 + 1, 1, False)
                tile(KD - 2, 0, False)
                tile(KD - 1, 1, True)

                def add(half):
                    u = (half + 1) * PIECES // 2 - 1
                    dve.wait_ge(s_unit[u % 2], 2 * KD + u // 2 + 2)
                    for t in range(T):
                        xs = x_sb[:, t, half * BW:(half + 1) * BW]
                        nc.vector.scalar_tensor_tensor(xs, ps_w[half][t][:], 0.5, xs, ALU.mult, ALU.add
                                                       ).then_inc(s_x, 1)

                for u in range(1, PIECES):
                    lo_part(dve, 2 * KD + u // 2, u % 2, PIECE)
                    if u == PIECES // 2:
                        add(0)
                add(1)
        mix.close()
        free_semaphores()

        with ExitStack() as c:
            h2T = sbuf(c, "h2T", [P, KD, N])
            memT = sbuf(c, "memT", [P, KD, MEM])
            mem_sb = sbuf(c, "mem_sb", [P, MEM // P, D])
            s_mem = sem("mem_in")

            def load_mem(sp):
                sp.dma_start(mem_sb[:], a["mem"].rearrange("b (t p) d -> p (b t) d", p=P)).then_inc(s_start, 16)
                sp.wait_ge(s_start, 80)

            load_mem.ready = 80
            rms_transposed(c, "rm", mem_sb, MEM // P, gain_memn, memT, first=load_mem)
            rms_transposed(c, "rh", x_sb, T, gain_mem, h2T)
            w = {n: sbuf(c, "m_" + n, [P, KD, BW]) for n in ("w_mq", "w_mk", "w_mv")}
            wo = sbuf(c, "m_wo", [P, KB, D])
            qT = sbuf(c, "m_qT", [P, MX_HEADS, N])
            kT = sbuf(c, "m_kT", [P, MX_HEADS, MEM])
            v = sbuf(c, "m_v", [P, MEM // P, BW])
            oT = sbuf(c, "m_oT", [P, MX_HEADS, N])
            pr = [sbuf(c, f"m_p{i}", [P, MEM]) for i in range(3)]
            pT = [sbuf(c, f"m_pT{i}", [P, MEM // P, N]) for i in range(2)]
            U = MX_HEADS * T
            nmax, rsum = sbuf(c, "m_nmax", [P, U]), sbuf(c, "m_rsum", [P, U])
            MT = MEM // P
            SC = float(P) ** -0.5
            with ExitStack() as c2:
                ps = [psum(c2, f"mq{i}") for i in range(4)]
                s_w = {n: sem("m_in_" + n) for n in w}
                s_ps, s_out = sem("m_ps"), sem("m_out")
                block = c2.enter_context(nc.Block())
                groups = [("q", h) for h in range(MX_HEADS)] + [("k", h) for h in range(MX_HEADS)] + [
                    ("v", t) for t in range(MT)]

                @block.sync
                def _(sp):
                    for n in w:
                        sp.dma_start(w[n][:], a[n].rearrange("l (p k) n -> p (l k) n", k=KD)
                                     ).then_inc(s_w[n], 16)

                @block.tensor
                def _(pe):
                    for g, (kind, h) in enumerate(groups):
                        if h == 0:
                            pe.wait_ge(s_w["w_m" + kind], 16)
                        if g >= 4:
                            pe.wait_ge(s_out, g - 3)
                        for k in range(KD):
                            if kind == "v":
                                lhs, rhs, n = memT[:, k, h * P:(h + 1) * P], w["w_mv"][:, k, :], BW
                            else:
                                lhs = w["w_m" + kind][:, k, h * P:(h + 1) * P]
                                rhs, n = (h2T[:, k, :], N) if kind == "q" else (memT[:, k, :], MEM)
                            last = nc.tensor.matmul(ps[g % 4][:, 0:n], lhs, rhs, start=(k == 0),
                                                    stop=(k == KD - 1))
                        last.then_inc(s_ps, 1)

                @block.vector
                def _(dve):
                    for g, (kind, h) in enumerate(groups):
                        dst = {"q": qT, "k": kT, "v": v}[kind][:, h, :]
                        dve.wait_ge(s_ps, g + 1)
                        nc.vector.tensor_copy(dst, ps[g % 4][:, 0:MEM if kind == "k" else N]).then_inc(s_out, 1)

            with ExitStack() as c2:
                ps_s = [psum(c2, f"m_s{i}") for i in range(2)]
                ps_t = [psum(c2, f"m_t{i}") for i in range(2 * MT)]
                ps_o = [psum(c2, f"m_o{i}") for i in range(2)]
                s_wo, s_s, s_mx, s_exp, s_nrm, s_t, s_pt, s_o, s_ot, s_dve, s_x = (
                    sem("m_" + n) for n in ("wo", "s", "mx", "exp", "nrm", "t", "pt", "o", "ot", "dve", "x"))
                block = c2.enter_context(nc.Block())

                @block.sync
                def _(sp):
                    sp.dma_start(wo[:], a["w_mo"].rearrange("l (k p) n -> p (l k) n", p=P)).then_inc(s_wo, 16)

                @block.tensor
                def _(pe):
                    for st in range(U + 3):
                        if st < U:
                            h, t = divmod(st, T)
                            if st >= 2:
                                pe.wait_ge(s_exp, st - 1)
                            nc.tensor.matmul(ps_s[st % 2][:, 0:MEM], qT[:, h, t * P:(t + 1) * P], kT[:, h, :],
                                             start=True, stop=True).then_inc(s_s, 1)
                        if 0 <= st - 2 < U:
                            u = st - 2
                            h, t = divmod(u, T)
                            pe.wait_ge(s_nrm, u + 1)
                            if t == 0 and h >= 2:
                                pe.wait_ge(s_pt, MT * (h - 1))
                            for m in range(MT):
                                last = nc.tensor.transpose(ps_t[MT * (h % 2) + m][:, t * P:(t + 1) * P],
                                                           pr[u % 3][:, m * P:(m + 1) * P], ident[:])
                            last.then_inc(s_t, 1)
                        if st - 3 >= 0 and (st - 3) % T == T - 1:
                            h = (st - 3) // T
                            pe.wait_ge(s_pt, MT * (h + 1))
                            if h >= 2:
                                pe.wait_ge(s_ot, h - 1)
                            for m in range(MT):
                                last = nc.tensor.matmul(ps_o[h % 2][:], v[:, m, h * P:(h + 1) * P],
                                                        pT[h % 2][:, m, :], start=(m == 0), stop=(m == MT - 1))
                            last.then_inc(s_o, 1)
                    pe.wait_ge(s_wo, 16)
                    pe.wait_ge(s_ot, MX_HEADS)
                    for g in range(2 * T):
                        t, h = divmod(g, 2)
                        if g >= 4:
                            pe.wait_ge(s_x, g - 3)
                        for k in range(KB):
                            last = nc.tensor.matmul(ps_t[g % 4][:], oT[:, k, t * P:(t + 1) * P],
                                                    wo[:, k, h * BW:(h + 1) * BW],
                                                    start=(k == 0), stop=(k == KB - 1))
                        last.then_inc(s_o, 1)

                @block.scalar
                def _(act):
                    for u in range(U):
                        act.wait_ge(s_mx, u + 1)
                        if u >= 3:
                            act.wait_ge(s_t, u - 2)
                        nc.scalar.activation(pr[u % 3][:], ps_s[u % 2][:, 0:MEM], ACT.Exp, scale=SC,
                                             bias=nmax[:, u:u + 1], accum_out=rsum[:, u:u + 1]
                                             ).then_inc(s_exp, 1)

                @block.vector
                def _(dve):
                    do = Steps(dve, s_dve)
                    for st in range(U + 4):
                        if st < U:
                            dve.wait_ge(s_s, st + 1)
                            do.after(nc.vector.reduce_max(nmax[:, st:st + 1], ps_s[st % 2][:, 0:MEM], AX_X))
                            nc.vector.tensor_scalar(nmax[:, st:st + 1], nmax[:, st:st + 1], -SC, None,
                                                    ALU.mult).then_inc(s_mx, 1)
                        if 0 <= st - 1 < U:
                            u = st - 1
                            dve.wait_ge(s_exp, u + 1)
                            do.after(nc.vector.reciprocal(rsum[:, u:u + 1], rsum[:, u:u + 1]))
                            nc.vector.tensor_scalar(pr[u % 3][:], pr[u % 3][:], rsum[:, u:u + 1], None,
                                                    ALU.mult).then_inc(s_nrm, 1)
                        if st - 2 >= 0 and st - 2 < U and (st - 2) % T == T - 1:
                            h = (st - 2) // T
                            dve.wait_ge(s_t, h * T + T)
                            if h >= 2:
                                dve.wait_ge(s_o, h - 1)
                            for m in range(MT):
                                nc.vector.tensor_copy(pT[h % 2][:, m, :], ps_t[MT * (h % 2) + m][:]
                                                      ).then_inc(s_pt, 1)
                        if st - 3 >= 0 and (st - 3) % T == T - 1:
                            h = (st - 3) // T
                            dve.wait_ge(s_o, h + 1)
                            nc.vector.tensor_copy(oT[:, h, :], ps_o[h % 2][:]).then_inc(s_ot, 1)
                    for g in range(2 * T):
                        t, h = divmod(g, 2)
                        dve.wait_ge(s_o, MX_HEADS + g + 1)
                        xs = x_sb[:, t, h * BW:(h + 1) * BW]
                        nc.vector.tensor_tensor(xs, ps_t[g % 4][:], xs, ALU.add).then_inc(s_x, 1)

        idx = sbuf(stack, "idx", [P, EXPERTS], U32)
        wsel = sbuf(stack, "wsel", [P, 2, T])
        with ExitStack() as c:
            h3T = sbuf(c, "h3T", [P, KD, N])
            xn = sbuf(c, "xn", [P, T, D])
            ffn_gain = sbuf(c, "ffn_gain", [P, D])

            def load_gain(sp):
                sp.dma_start(ffn_gain[:], bass.AP(a["rows"].tensor, ROWS, [[0, P], [1, D]])).then_inc(s_start, 16)
                sp.wait_ge(s_start, 96)

            load_gain.ready = 96
            rms_transposed(c, "rf", x_sb, T, None, h3T, first=load_gain, keep=xn,
                           gain_row=ffn_gain[:])
            w_rt = sbuf(c, "w_rt", [P, KD, LOGITS])
            rc = sbuf(c, "rc", [P, ROUTE_CONSTS])
            before, ones = rc[:, 0:P], rc[:, P:2 * P]
            iota = rc[:, 2 * P:2 * P + EXPERTS]
            r0 = 2 * P + EXPERTS
            blk_thr, blk_no, blk_e = (rc[:, r0 + P * i:r0 + P * (i + 1)] for i in range(3))
            rank1 = rc[:, r0 + 3 * P:r0 + 3 * P + 1]
            asg = sbuf(c, "asg", [P, 2, T], I32)
            fill = sbuf(c, "fill", [P, P], I32)
            lg = sbuf(c, "lg", [P, T, LOGITS])
            gpad = sbuf(c, "gpad", [P, T, PER_GROUP])
            sel = sbuf(c, "sel", [P, T, PER_GROUP])
            top = sbuf(c, "top", [P, 2, T, PER_GROUP])
            topi = sbuf(c, "topi", [P, 2, T, PER_GROUP], U32)
            topf = sbuf(c, "topf", [P, 2, T, PER_GROUP])
            oh = sbuf(c, "oh", [P, T, GROUPS])
            junk = sbuf(c, "r_junk", [P, 2, T, EXPERTS])
            sm = sbuf(c, "r_small", [P, 8, T])
            e_of = sbuf(c, "e_of", [P, 2, T])
            hot = sbuf(c, "hot", [P, 3, T, EXPERTS])
            pos = sbuf(c, "pos", [P, T, EXPERTS])
            dest = sbuf(c, "dest", [P, 2, T])
            destu = sbuf(c, "destu", [P, 2, T], U32)
            act_b = sbuf(c, "act_b", [P, EXPERTS, 4])
            cnt = sbuf(c, "cnt", [P, EXPERTS])
            rank = sbuf(c, "rank", [P, P])
            jobs = sbuf(c, "jobs", [P, 4])
            jobsi = sbuf(c, "jobsi", [P, 4], I32)
            idr = sbuf(c, "idr", [EXPERTS, P], I32)
            idf = sbuf(c, "idf", [EXPERTS, P])
            ps_l, ps_p, ps_c, ps_i = (psum(c, "r_" + n) for n in ("l", "p", "c", "i"))
            s_w, s_c, s_xw, s_l, s_dve, s_gm, s_ex, s_d01, s_e2, s_hot, s_pc, s_dest, s_fl, s_fw, s_sc, s_rd, s_rf, s_it, s_jb, s_jw = (
                sem("r_" + n) for n in ("w", "const", "xw", "l", "dve", "gmax", "gexp", "d01", "e2", "hot", "pc",
                                        "dest", "fill", "fillw", "scat", "read", "readf", "idt", "jobs", "jobw"))
            block = c.enter_context(nc.Block())

            @block.sync
            def _(sp):
                sp.dma_start(w_rt[:], a["w_route"].rearrange("(p k) n -> p k n", k=KD)).then_inc(s_w, 16)
                sp.dma_start(rc[:], a["route_consts"]).then_inc(s_c, 16)
                sp.dma_start(asg[:], a["asg_ids"]).then_inc(s_c, 16)
                for ch in range(2):
                    sp.dma_start(xn_dram[ch * N:(ch + 1) * N, :].rearrange("(t p) d -> p t d", p=P), xn[:]
                                 ).then_inc(s_xw, 16)
                sp.wait_ge(s_sc, 16 * 2 * T)
                sp.dma_start(idr[:], list_dram.rearrange("(e s) o -> e (s o)", e=EXPERTS)[:, 0:P]
                             ).then_inc(s_rd, 16)
                sp.wait_ge(s_jb, 1)
                sp.dma_start(jobs_dram[0:1, 0:4 * PER_GROUP].rearrange("o (j q) -> (o j) q", q=4),
                             jobsi[0:PER_GROUP, :]).then_inc(s_jw, 16)
                sp.wait_ge(s_jw, 16)
                sp.wait_ge(s_xw, 32)

            @block.gpsimd
            def _(pool):
                nc.gpsimd.memset(fill[:], NO_SLOT).then_inc(s_fl, 1)
                pool.wait_ge(s_fl, 1)
                pool.dma_start(list_dram.rearrange("(q s) o -> q (s o)", q=P), fill[:]).then_inc(s_fw, 16)
                pool.wait_ge(s_fw, 16)
                pool.wait_ge(s_c, 32)
                pool.wait_ge(s_dest, 1)
                for ch in range(2):
                    for t in range(T):
                        pool.indirect_dma_start(list_dram, bass.IndirectOffsetOnAxis(destu[:, ch, t:t + 1], 0),
                                                asg[:, ch, t:t + 1], None).then_inc(s_sc, 16)

            @block.tensor
            def _(pe):
                pe.wait_ge(s_w, 16)
                for t in range(T):
                    for k in range(KD):
                        last = nc.tensor.matmul(ps_l[:, t * LOGITS:(t + 1) * LOGITS],
                                                h3T[:, k, t * P:(t + 1) * P], w_rt[:, k, :],
                                                start=(k == 0), stop=(k == KD - 1))
                last.then_inc(s_l, 1)
                pe.wait_ge(s_c, 32)
                pe.wait_ge(s_hot, 1)
                for t in range(T):
                    o = ps_p[:, t * EXPERTS:(t + 1) * EXPERTS]
                    for q in range(t):
                        nc.tensor.matmul(o, ones, hot[:, 2, q, :], start=(q == 0), stop=False)
                    nc.tensor.matmul(o, before, hot[:, 2, t, :], start=(t == 0), stop=True)
                for t in range(T):
                    last = nc.tensor.matmul(ps_c[:, 0:EXPERTS], ones, hot[:, 2, t, :],
                                            start=(t == 0), stop=(t == T - 1))
                last.then_inc(s_pc, 1)
                pe.wait_ge(s_rf, 1)
                nc.tensor.transpose(ps_i[:, 0:EXPERTS], idf[:], ident[0:EXPERTS, 0:EXPERTS]).then_inc(s_it, 1)

            @block.scalar
            def _(act):
                act.wait_ge(s_gm, 1)
                for t in range(T):
                    nc.scalar.activation(junk[:, 0, t, 0:GROUPS], lg[:, t, 0:GROUPS], ACT.Exp,
                                         bias=sm[:, 0, t:t + 1], accum_out=sm[:, 1, t:t + 1]).then_inc(s_ex, 1)
                act.wait_ge(s_d01, 1)
                nc.scalar.activation(sm[:, 3, :], sm[:, 2, :], ACT.Exp).then_inc(s_e2, 1)

            @block.vector
            def _(dve):
                do = Steps(dve, s_dve)
                do.after(nc.vector.memset(gpad[:], -3e38))
                dve.wait_ge(s_c, 32)
                dve.wait_ge(s_l, 1)
                bias = router_bias.unsqueeze(1).to_broadcast([P, T, LOGITS])
                do.after(nc.vector.tensor_tensor(lg[:], ps_l[:, 0:T * LOGITS].rearrange("p (t n) -> p t n", t=T),
                                                 bias, ALU.add))
                do.after(nc.vector.tensor_copy(gpad[:, :, 0:GROUPS], lg[:, :, 0:GROUPS]))
                for t in range(T):
                    do.after(nc.vector.max(top[:, 0, t, :], gpad[:, t, :]))
                    do.after(nc.vector.max_index(topi[:, 0, t, :], top[:, 0, t, :], gpad[:, t, :]))
                nc.vector.tensor_scalar(sm[:, 0, :], top[:, 0, :, 0], -1.0, None, ALU.mult).then_inc(s_gm, 1)
                do.after(nc.vector.tensor_copy(topf[:, 0, :, :], topi[:, 0, :, :]))
                for t in range(T):
                    do.after(nc.vector.tensor_scalar(oh[:, t, :], iota[:, 0:GROUPS], topf[:, 0, t, 0:1], None,
                                                     ALU.is_equal))
                    for g in range(GROUPS):
                        el = lg[:, t, GROUPS + g * PER_GROUP:GROUPS + (g + 1) * PER_GROUP]
                        if g == 0:
                            ins = nc.vector.tensor_scalar(sel[:, t, :], el, oh[:, t, 0:1], None, ALU.mult)
                        else:
                            ins = nc.vector.scalar_tensor_tensor(sel[:, t, :], el, oh[:, t, g:g + 1],
                                                                 sel[:, t, :], ALU.mult, ALU.add)
                        do.after(ins)
                    do.after(nc.vector.max(top[:, 1, t, :], sel[:, t, :]))
                    do.after(nc.vector.max_index(topi[:, 1, t, :], top[:, 1, t, :], sel[:, t, :]))
                do.after(nc.vector.tensor_copy(topf[:, 1, :, :], topi[:, 1, :, :]))
                nc.vector.tensor_tensor(sm[:, 2, :], top[:, 1, :, 1], top[:, 1, :, 0], ALU.subtract
                                        ).then_inc(s_d01, 1)
                for ch in range(2):
                    do.after(nc.vector.scalar_tensor_tensor(e_of[:, ch, :], topf[:, 0, :, 0], float(PER_GROUP),
                                                            topf[:, 1, :, ch], ALU.mult, ALU.add))
                    for t in range(T):
                        do.after(nc.vector.tensor_scalar(hot[:, ch, t, :], iota, e_of[:, ch, t:t + 1], None,
                                                         ALU.is_equal))
                nc.vector.tensor_tensor(hot[:, 2, :, :], hot[:, 0, :, :], hot[:, 1, :, :], ALU.add
                                        ).then_inc(s_hot, 1)
                dve.wait_ge(s_e2, 1)
                dve.wait_ge(s_ex, T)
                do.after(nc.vector.tensor_scalar(sm[:, 4, :], sm[:, 3, :], 1.0, None, ALU.add))
                do.after(nc.vector.tensor_tensor(sm[:, 4, :], sm[:, 4, :], sm[:, 1, :], ALU.mult))
                do.after(nc.vector.reciprocal(sm[:, 4, :], sm[:, 4, :]))
                do.after(nc.vector.tensor_scalar(wsel[:, 0, :], sm[:, 4, :], 0.5, None, ALU.mult))
                do.after(nc.vector.tensor_tensor(wsel[:, 1, :], wsel[:, 0, :], sm[:, 3, :], ALU.mult))
                dve.wait_ge(s_pc, 1)
                do.after(nc.vector.tensor_copy(pos[:], ps_p[:, 0:T * EXPERTS].rearrange("p (t e) -> p t e", t=T)))
                do.after(nc.vector.tensor_copy(cnt[:], ps_c[:, 0:EXPERTS]))
                for ch in range(2):
                    do.after(nc.vector.tensor_tensor(junk[:, ch, :, :], hot[:, ch, :, :], pos[:], ALU.mult))
                    do.after(nc.vector.tensor_reduce(dest[:, ch, :], junk[:, ch, :, :], AX_X, ALU.add))
                do.after(nc.vector.scalar_tensor_tensor(dest[:], e_of[:], float(N), dest[:], ALU.mult, ALU.add))
                nc.vector.tensor_copy(destu[:], dest[:]).then_inc(s_dest, 1)
                thr = blk_thr.rearrange("p (e b) -> p e b", b=4)
                do.after(nc.vector.tensor_tensor(act_b[:], cnt[:].unsqueeze(2).to_broadcast([P, EXPERTS, 4]),
                                                 thr, ALU.is_gt))
                av = act_b[:].rearrange("p e b -> p (e b)")
                do.after(nc.vector.tensor_tensor_scan(rank[:], ones, av, 0.0, ALU.mult, ALU.add))
                do.after(nc.vector.tensor_copy(jobs[:, 2:3], rank[:, P - 1:P]))
                do.after(nc.vector.tensor_tensor(rank[:], rank[:], av, ALU.mult))
                do.after(nc.vector.tensor_scalar(rank[:], rank[:], rank1, None, ALU.is_equal))
                do.after(nc.vector.tensor_tensor_reduce(av, rank[:], blk_no, 1.0, 0.0, ALU.mult, ALU.add,
                                                        jobs[:, 0:1]))
                do.after(nc.vector.tensor_tensor_reduce(av, rank[:], blk_e, 1.0, 0.0, ALU.mult, ALU.add,
                                                        jobs[:, 1:2]))
                do.after(nc.vector.memset(jobs[:, 3:4], 0.0))
                nc.vector.tensor_copy(jobsi[:], jobs[:]).then_inc(s_jb, 1)
                dve.wait_ge(s_rd, 16)
                nc.vector.tensor_copy(idf[:], idr[:]).then_inc(s_rf, 1)
                dve.wait_ge(s_it, 1)
                do.after(nc.vector.tensor_copy(idx[:], ps_i[:, 0:EXPERTS]))

        with ExitStack() as c:
            RAW, PIECES, PW = 4, 6, 2048
            raw = [sbuf(c, f"w_raw{r}", [P, PW]) for r in range(RAW)]
            w_hi = [sbuf(c, f"w_hi{j}", [P, PW], F32R) for j in range(PIECES)]
            w_lo = [sbuf(c, f"w_lo{j}", [P, PW], F32R) for j in range(PIECES)]
            ibx, iby = ([sbuf(c, f"ib{n}{b}", [P, 1], U32) for b in range(2)] for n in "xy")
            xs = [sbuf(c, f"xs{b}", [P, D]) for b in range(2)]
            xT_hi, xT_lo = (sbuf(c, "xT_" + n, [P, KD * P], F32R) for n in ("hi", "lo"))
            hT_hi, hT_lo = (sbuf(c, "hidT_" + n, [P, KF * P], F32R) for n in ("hi", "lo"))
            tn = sbuf(c, "tn", [P, FF])
            hd = sbuf(c, "hd", [P, FF])
            yo = [sbuf(c, f"yo{b}", [P, D]) for b in range(2)]
            ps_x = psum(c, "e_x", (P, KD * P))
            ps_1, ps_3, ps_h = psum(c, "e_1"), psum(c, "e_3"), psum(c, "e_h")
            ps_y = psum(c, "e_y", (P, D))

            s_ibx, s_iby, s_xs, s_ys, s_stored = (
                [sem(f"e_{n}{b}") for b in range(2)] for n in ("ibx", "iby", "xs", "ys", "stored"))
            s_tx, s_xhi, s_xlo, s_th, s_hm, s_hd, s_ht, s_hhi, s_hlo, s_yo = (
                sem("e_" + n) for n in ("tx", "xhi", "xlo", "tanh", "hm", "hd", "ht", "hhi", "hlo", "yo"))
            s_raw, s_hi, s_split = ([sem(f"e_{n}{r}") for r in range(RAW)] for n in ("raw", "hi", "split"))
            s_used = [sem(f"e_used{j}") for j in range(PIECES)]
            s_init, s_lst = sem("e_init"), sem("e_list")
            s_turn = sem("e_turn")
            w13v = [a[n].rearrange("l e (p k) f -> (l e) p (k f)", k=KD) for n in ("w1", "w1", "w3", "w3")]
            w2v = a["w2"].rearrange("l e (p k) d -> (l e) p (k d)", k=KF)
            NI = EXPERTS // 2
            HALF = NI - 1
            last_row = nc.gpsimd.alloc_register("last_row")

            class Step:

                def __init__(self, s, i, odd, extra=None):
                    self.s, self.i, self.odd, self.extra = s, i, odd, extra

                def piece(self, j):
                    if self.extra is not None:
                        return (j % RAW, self.extra * (2 if j % RAW < 2 else 1) + (3 * EXPERTS // 2 + 1 + j // RAW))
                    if self.i is None:
                        return j, 1
                    m = j if self.odd else PIECES + j
                    if not self.odd and isinstance(self.s, int) and self.s == EXPERTS:
                        m = PIECES + j - 4
                    return m % RAW, self.i * 3 + (m // RAW + 2)

            first_step = Step(0, None, False)

            def pair(i):
                return Step(i * 2 + 1, i, True), Step(i * 2 + 2, i, False)

            step31, step32 = Step(EXPERTS - 1, HALF, True), Step(EXPERTS, HALF, False)

            class Job:

                def __init__(self, q, b, i, tx):
                    self.q, self.b, self.i, self.tx = q, b, i, tx

            def job(s, i, odd, shift):
                at = (1 if odd else 2) + shift
                return Job(s + shift, at % 2, i + at // 2, s + (shift + 1))

            def extra(r):
                return Job(r + EXPERTS, 0, r + NI, r + (EXPERTS + 2))

            def wait(eng, q, n):
                if not (isinstance(n, int) and n <= 0):
                    eng.wait_ge(q, n)

            def load(sp, st, j, e):
                r, n = st.piece(j)
                if not (isinstance(n, int) and n == 1):
                    sp.wait_ge(s_split[r], n - 1)
                src, h = (w13v[j], j % 2) if j < 4 else (w2v, j - 4)
                sp.dma_start(raw[r][:], src[bass.ds(e, 1), :, h * PW:(h + 1) * PW].rearrange("o p f -> p (o f)")
                             ).then_inc(s_raw[r], 16)

            def hi_part(act, st, j, q):
                r, n = st.piece(j)
                act.wait_ge(s_raw[r], n * 16)
                wait(act, s_used[j], q)
                nc.scalar.copy(w_hi[j][:], raw[r][:]).then_inc(s_hi[r], 1)

            def lo_part(dve, st, j):
                r, n = st.piece(j)
                dve.wait_ge(s_hi[r], n)
                nc.vector.tensor_tensor(w_lo[j][:], raw[r][:], w_hi[j][:].bitcast(F32), ALU.subtract
                                        ).then_inc(s_split[r], 1)

            def fetch(pool, b, n, tx):
                wait(pool, s_ibx[b], n)
                pool.wait_ge(s_tx, tx)
                pool.sem_inc(s_turn, 1)
                pool.indirect_dma_start(xs[b][:], None, xn_dram, bass.IndirectOffsetOnAxis(ibx[b][:], 0),
                                        bounds_check=last_row, oob_is_err=False).then_inc(s_xs[b], 16)

            def store(pool, jb, listed=True):
                b = jb.b
                if listed:
                    pool.wait_ge(s_iby[b], jb.i + 1)
                pool.wait_ge(s_yo, jb.q + 1)
                pool.sem_inc(s_turn, 1)
                pool.indirect_dma_start(ys_dram, bass.IndirectOffsetOnAxis(iby[b][:], 0), yo[b][:], None,
                                        bounds_check=last_row, oob_is_err=False).then_inc(s_ys[b], 16)
                pool.wait_ge(s_ys[b], jb.i * 16 + 16)
                pool.sem_inc(s_stored[b], 1)

            def turn_rows(pe, jb):
                pe.wait_ge(s_xs[jb.b], jb.i * 16 + 16)
                wait(pe, s_xlo, jb.q)
                for k in range(KD):
                    last = nc.tensor.transpose(ps_x[:, k * P:(k + 1) * P], xs[jb.b][:, k::KD], ident[:])
                last.then_inc(s_tx, 1)

            def product(o, x_parts, j, k, w_cols, start, stop):
                x_hi, x_lo = x_parts
                for n, (xp, wp) in enumerate(((x_hi, w_hi[j]), (x_hi, w_lo[j]), (x_lo, w_hi[j]))):
                    last = nc.tensor.matmul(o, xp[:, k * P:(k + 1) * P], wp[:, w_cols:w_cols + FF],
                                            start=start and n == 0, stop=stop and n == 2)
                return last

            def up(pe, st, q, pieces):
                if 0 in pieces:
                    pe.wait_ge(s_xlo, q + 1)
                    wait(pe, s_hd, q)
                for j in pieces:
                    r, n = st.piece(j)
                    pe.wait_ge(s_split[r], n)
                    half = j % 2
                    for k in range(4):
                        last = product((ps_1 if j < 2 else ps_3)[:], (xT_hi, xT_lo), j, half * 4 + k, k * FF,
                                       half == 0 and k == 0, half == 1 and k == 3)
                    last.then_inc(s_used[j], 1)

            def turn_hidden(pe, q):
                pe.wait_ge(s_hd, q + 1)
                wait(pe, s_hlo, q)
                for k in range(KF):
                    last = nc.tensor.transpose(ps_h[:, k * P:(k + 1) * P], hd[:, k::KF], ident[:])
                last.then_inc(s_ht, 1)

            def down(pe, st, q):
                pe.wait_ge(s_hlo, q + 1)
                wait(pe, s_yo, q)
                for j in (4, 5):
                    r, n = st.piece(j)
                    pe.wait_ge(s_split[r], n)
                    for h in range(2):
                        for k in range(2):
                            last = product(ps_y[:, h * FF:(h + 1) * FF], (hT_hi, hT_lo), j, (j - 4) * 2 + k,
                                           k * D + h * FF, j == 4 and k == 0, j == 5 and k == 1)
                    last.then_inc(s_used[j], 1)

            def x_hi(act, q):
                act.wait_ge(s_tx, q + 3)
                nc.scalar.copy(xT_hi[:], ps_x[:]).then_inc(s_xhi, 1)

            def tanh_step(act, q):
                act.wait_ge(s_used[1], q + 1)
                wait(act, s_hd, q)
                nc.scalar.activation(tn[:], ps_1[:], ACT.Tanh, scale=0.5).then_inc(s_th, 1)

            def h_hi(act, q):
                act.wait_ge(s_ht, q + 1)
                nc.scalar.copy(hT_hi[:], ps_h[:]).then_inc(s_hhi, 1)

            def y_copy(act, jb):
                act.wait_ge(s_used[5], jb.q + 2)
                act.wait_ge(s_stored[jb.b], jb.i + 1)
                nc.scalar.copy(yo[jb.b][:], ps_y[:]).then_inc(s_yo, 1)

            def x_lo(dve, q):
                dve.wait_ge(s_xhi, q + 1)
                nc.vector.tensor_tensor(xT_lo[:], ps_x[:], xT_hi[:].bitcast(F32), ALU.subtract).then_inc(s_xlo, 1)

            def silu_step(dve, q):
                dve.wait_ge(s_th, q + 1)
                nc.vector.scalar_tensor_tensor(tn[:], tn[:], 1.0, ps_1[:], ALU.add, ALU.mult).then_inc(s_hm, 1)

            def hidden(dve, q):
                dve.wait_ge(s_hm, q + 1)
                dve.wait_ge(s_used[3], q + 1)
                wait(dve, s_ht, q)
                nc.vector.tensor_tensor(hd[:], tn[:], ps_3[:], ALU.mult).then_inc(s_hd, 1)

            def h_lo(dve, q):
                dve.wait_ge(s_hhi, q + 1)
                nc.vector.tensor_tensor(hT_lo[:], ps_h[:], hT_hi[:].bitcast(F32), ALU.subtract).then_inc(s_hlo, 1)

            def pick_x(dve, e, jb):
                dve.wait_ge(s_tx, jb.tx)
                nc.vector.tensor_copy(ibx[jb.b][:], idx[:, bass.ds(e, 1)]).then_inc(s_ibx[jb.b], 1)

            def pick_y(dve, e, jb):
                dve.wait_ge(s_stored[jb.b], jb.i + 1)
                nc.vector.tensor_copy(iby[jb.b][:], idx[:, bass.ds(e, 1)]).then_inc(s_iby[jb.b], 1)

            def pool_step(pool, s, i, odd, rows_in):
                if rows_in:
                    jb = job(s, i, odd, 1)
                    fetch(pool, jb.b, jb.i + 1, jb.tx)
                store(pool, job(s, i, odd, -1))

            def pe_step(pe, st, s, i, odd, rows_in):
                up(pe, st, s, (0, 1, 2))
                turn_hidden(pe, s - 1)
                up(pe, st, s, (3,))
                if rows_in:
                    turn_rows(pe, job(s, i, odd, 1))
                down(pe, st, s - 1)

            def act_step(act, nxt, s, i, odd, ups, last=True):
                if ups:
                    hi_part(act, nxt, 0, s + 1)
                    hi_part(act, nxt, 1, s + 1)
                tanh_step(act, s)
                if last:
                    h_hi(act, s - 1)
                if ups:
                    hi_part(act, nxt, 2, s + 1)
                    x_hi(act, s + 1)
                    hi_part(act, nxt, 3, s + 1)
                hi_part(act, nxt, 4, s + 1)
                hi_part(act, nxt, 5, s + 1)
                if last:
                    y_copy(act, job(s, i, odd, -1))

            def dve_step(dve, nxt, s, i, odd, ups, last=True, first=False):
                if ups:
                    if first:
                        pick_y(dve, 0, Job(0, 0, 0, 2))
                        pick_x(dve, 2, Job(2, 0, 1, 3))
                    else:
                        pick_y(dve, s, job(s, i, odd, 0))
                        if ups != "no rows":
                            pick_x(dve, s + 2, job(s, i, odd, 2))
                    lo_part(dve, nxt, 0)
                    lo_part(dve, nxt, 1)
                silu_step(dve, s)
                if last:
                    h_lo(dve, s - 1)
                if ups:
                    lo_part(dve, nxt, 2)
                hidden(dve, s)
                if ups:
                    x_lo(dve, s + 1)
                    lo_part(dve, nxt, 3)
                lo_part(dve, nxt, 4)
                lo_part(dve, nxt, 5)

            block = c.enter_context(nc.Block())

            @block.sync
            def _(sp):
                sp.sem_inc(s_tx, 2)
                for q in (s_used[4], s_used[5], s_stored[0], s_stored[1]):
                    sp.sem_inc(q, 1)
                for j in range(4):
                    load(sp, first_step, j, 0)
                with sp.Fori(0, HALF) as i:
                    for st in pair(i):
                        for j in range(PIECES):
                            load(sp, st, j, st.s if j < 4 else st.s - 1)
                for j in range(PIECES):
                    load(sp, step31, j, EXPERTS - 1 if j < 4 else EXPERTS - 2)
                for j in (4, 5):
                    load(sp, step32, j, EXPERTS - 1)
                n = sp.value_load(jobs_dram[0:1, 2:3], min_val=0, max_val=MAX_EXTRA)
                with sp.If(n > 0):
                    with sp.Fori(0, n) as r:
                        e = sp.value_load(jobs_dram[0:1, bass.ds(r * 4 + 1, 1)], min_val=0, max_val=EXPERTS - 1)
                        for j in range(PIECES):
                            load(sp, Step(None, None, False, r), j, e)
                    sp.nop()

            @block.gpsimd
            def _(pool):
                for b in range(2):
                    nc.gpsimd.memset(xs[b][:], 0.0).then_inc(s_init, 1)
                pool.wait_ge(s_init, 2)
                pool.reg_mov(last_row, SLOTS - 1)
                fetch(pool, 0, 1, 1)
                fetch(pool, 1, 1, 2)
                with pool.Fori(0, HALF) as i:
                    for st in pair(i):
                        pool_step(pool, st.s, i, st.odd, True)
                store(pool, Job(EXPERTS - 2, 0, NI - 1, None))
                store(pool, Job(EXPERTS - 1, 1, NI - 1, None))
                n = pool.value_load(jobs_dram[0:1, 2:3], min_val=0, max_val=MAX_EXTRA)
                with pool.If(n > 0):
                    with pool.Fori(0, n) as r:
                        j = pool.value_load(jobs_dram[0:1, bass.ds(r * 4, 1)], min_val=0, max_val=4 * EXPERTS - 1)
                        for ib in (ibx[0], iby[0]):
                            pool.dma_start(ib[:], list_dram[bass.ds(j * P, P), :].bitcast(U32)).then_inc(s_lst, 16)
                        pool.wait_ge(s_lst, r * 32 + 32)
                        jb = extra(r)
                        fetch(pool, 0, 0, jb.tx)
                        store(pool, jb, listed=False)
                    pool.nop()

            @block.tensor
            def _(pe):
                turn_rows(pe, Job(0, 0, 0, None))
                up(pe, first_step, 0, (0, 1, 2, 3))
                turn_rows(pe, Job(1, 1, 0, None))
                with pe.Fori(0, HALF) as i:
                    for st in pair(i):
                        pe_step(pe, st, st.s, i, st.odd, True)
                pe_step(pe, step31, EXPERTS - 1, HALF, True, False)
                turn_hidden(pe, EXPERTS - 1)
                down(pe, step32, EXPERTS - 1)
                n = pe.value_load(jobs_dram[0:1, 2:3], min_val=0, max_val=MAX_EXTRA)
                with pe.If(n > 0):
                    with pe.Fori(0, n) as r:
                        jb, st = extra(r), Step(None, None, False, r)
                        turn_rows(pe, jb)
                        up(pe, st, jb.q, (0, 1, 2, 3))
                        turn_hidden(pe, jb.q)
                        down(pe, st, jb.q)
                    pe.nop()

            @block.scalar
            def _(act):
                x_hi(act, 0)
                for j in range(4):
                    hi_part(act, first_step, j, 0)
                act_step(act, Step(1, 0, True), 0, None, False, True, last=False)
                with act.Fori(0, HALF) as i:
                    odd, even = pair(i)
                    act_step(act, even, odd.s, i, True, True)
                    act_step(act, Step(i * 2 + 3, i + 1, True), even.s, i, False, True)
                act_step(act, step32, EXPERTS - 1, HALF, True, False)
                h_hi(act, EXPERTS - 1)
                y_copy(act, Job(EXPERTS - 1, 1, NI - 1, None))
                n = act.value_load(jobs_dram[0:1, 2:3], min_val=0, max_val=MAX_EXTRA)
                with act.If(n > 0):
                    with act.Fori(0, n) as r:
                        jb, st = extra(r), Step(None, None, False, r)
                        x_hi(act, jb.q)
                        for j in range(4):
                            hi_part(act, st, j, jb.q)
                        tanh_step(act, jb.q)
                        hi_part(act, st, 4, jb.q + 1)
                        hi_part(act, st, 5, jb.q + 1)
                        h_hi(act, jb.q)
                        y_copy(act, jb)
                    act.nop()

            @block.vector
            def _(dve):
                for b in range(2):
                    pick_x(dve, b, Job(b, b, 0, b + 1))
                x_lo(dve, 0)
                for j in range(4):
                    lo_part(dve, first_step, j)
                dve_step(dve, Step(1, 0, True), 0, None, False, True, last=False, first=True)
                with dve.Fori(0, HALF - 1) as i:
                    odd, even = pair(i)
                    dve_step(dve, even, odd.s, i, True, True)
                    dve_step(dve, Step(i * 2 + 3, i + 1, True), even.s, i, False, True)
                odd, even = pair(HALF - 1)
                dve_step(dve, even, odd.s, HALF - 1, True, True)
                dve_step(dve, step31, even.s, HALF - 1, False, "no rows")
                pick_y(dve, EXPERTS - 1, Job(EXPERTS - 1, 1, NI - 1, None))
                dve_step(dve, step32, EXPERTS - 1, HALF, True, False)
                h_lo(dve, EXPERTS - 1)
                n = dve.value_load(jobs_dram[0:1, 2:3], min_val=0, max_val=MAX_EXTRA)
                with dve.If(n > 0):
                    with dve.Fori(0, n) as r:
                        jb, st = extra(r), Step(None, None, False, r)
                        x_lo(dve, jb.q)
                        for j in range(4):
                            lo_part(dve, st, j)
                        silu_step(dve, jb.q)
                        hidden(dve, jb.q)
                        lo_part(dve, st, 4)
                        lo_part(dve, st, 5)
                        h_lo(dve, jb.q)
                    dve.nop()

        with ExitStack() as c:
            yk = sbuf(c, "yk", [P, 2, T, D])
            junk = sbuf(c, "f_junk", [P, D])
            ss = sbuf(c, "f_ss", [P, T])
            s_ld = [[sem(f"f_ld{ch}{t}") for t in range(T)] for ch in range(2)]
            s_dve, s_x, s_ss, s_ms, s_sq, s_o, s_done = (sem("f_" + n) for n in ("dve", "x", "ss", "ms", "sq", "o",
                                                                                "done"))
            block = c.enter_context(nc.Block())

            @block.sync
            def _(sp):
                for t in range(T):
                    for ch in range(2):
                        r = ch * N + t * P
                        sp.dma_start(yk[:, ch, t, :], ys_dram[r:r + P, :]).then_inc(s_ld[ch][t], 16)
                for t in range(T):
                    sp.wait_ge(s_o, t + 1)
                    sp.dma_start(out[0, t * P:(t + 1) * P, :], x_sb[:, t, :]).then_inc(s_done, 16)
                sp.wait_ge(s_done, 16 * T)

            @block.scalar
            def _(act):
                for t in range(T):
                    act.wait_ge(s_x, t + 1)
                    if t:
                        act.wait_ge(s_ss, t)
                    nc.scalar.activation(junk[:], x_sb[:, t, :], ACT.Square, accum_out=ss[:, t:t + 1]
                                         ).then_inc(s_ss, 1)
                act.wait_ge(s_ms, 1)
                nc.scalar.activation(ss[:], ss[:], ACT.Sqrt).then_inc(s_sq, 1)

            @block.vector
            def _(dve):
                do = Steps(dve, s_dve)
                for t in range(T):
                    for ch in range(2):
                        dve.wait_ge(s_ld[ch][t], 16)
                        ins = nc.vector.scalar_tensor_tensor(x_sb[:, t, :], yk[:, ch, t, :],
                                                             wsel[:, ch, t:t + 1], x_sb[:, t, :],
                                                             ALU.mult, ALU.add)
                        if ch == 0:
                            do.after(ins)
                    ins.then_inc(s_x, 1)
                dve.wait_ge(s_ss, T)
                nc.vector.tensor_scalar(ss[:], ss[:], 1.0 / D, NORM_EPS, ALU.mult, ALU.add).then_inc(s_ms, 1)
                dve.wait_ge(s_sq, 1)
                do.after(nc.vector.reciprocal(ss[:], ss[:]))
                for t in range(T):
                    nc.vector.scalar_tensor_tensor(x_sb[:, t, :], x_sb[:, t, :], ss[:, t:t + 1], final_gain,
                                                   ALU.mult, ALU.mult).then_inc(s_o, 1)


def constants():
    p = np.arange(P)[:, None]
    c = np.arange(N)[None, :]
    ident = np.eye(P, dtype=np.float32)
    log_g = np.log(1.0 - 2.0 ** (-5.0 - np.arange(HEADS))).astype(np.float32).astype(np.float64)
    decay = np.where((c >= p)[:, None, :], np.exp(log_g[None, :, None] * np.maximum(c - p, 0)[:, None, :]), 0.0)
    decay = (decay * HD ** -0.5).astype(np.float32)
    slopes = (2.0 ** (-8.0 * np.arange(1, DIFF_HEADS + 1) / DIFF_HEADS)).astype(np.float32)
    dist = np.abs(p - (c - (N - P))).astype(np.float32)
    alibi = -slopes[None, :, None] * dist[:, None, :] * np.float32(HD ** 0.5)
    late = (c - (N - P)) // CHUNK > p // CHUNK
    alibi = np.where(late[:, None, :], np.float32(MASKED), alibi).astype(np.float32)
    f = np.arange(P)
    thr = np.where(f % 4 == 0, 1e9, P * (f % 4))
    route = np.concatenate([
        (np.arange(P)[:, None] < np.arange(P)[None, :]).astype(np.float32),
        np.ones((P, P), np.float32),
        np.tile(np.arange(EXPERTS, dtype=np.float32), (P, 1)),
        np.tile(thr.astype(np.float32), (P, 1)),
        np.tile(f.astype(np.float32), (P, 1)),
        np.tile((f // 4).astype(np.float32), (P, 1)),
        np.arange(1, P + 1, dtype=np.float32)[:, None],
    ], axis=1)
    asg = (np.arange(2)[None, :, None] * N + np.arange(T)[None, None, :] * P + np.arange(P)[:, None, None])
    return {"ident": ident, "decay": decay, "alibi": alibi, "route_consts": route,
            "asg_ids": asg.astype(np.int32)}


def laid_out(i):
    w_in = i["w_in"][0]
    at = [512 * n for n in range(13)]
    ax, ag, bq, bk, bv, cq, ck, cv, cg, dq, dk, dv = (w_in[:, at[n]:at[n + 1]] for n in range(12))
    w_mix = np.stack([ax, ag, bq, bk, cq, ck, dq, dk, bv, cv, cg, dv])
    w_mix = w_mix.reshape(12, D, 2, CW).transpose(0, 2, 1, 3).reshape(24, D, CW)
    gates = w_in[:, at[12]:].reshape(P, KD, 4, KD, P).transpose(3, 2, 0, 1, 4)
    branch = i["w_branch"][0].reshape(4, KB, P, KD, P).transpose(3, 0, 2, 1, 4)
    w_gb = np.concatenate([gates, branch], axis=3).reshape(4 * KD, P, UNIT)
    w_out = i["w_out"][0].reshape(KD // 2, 2, P, 2, BW).transpose(3, 0, 2, 1, 4).reshape(KD, P, PIECE)

    def cols(v, k):
        return v.reshape(P, k)

    def tiles(v):
        return v.reshape(KB, P).T

    small = np.concatenate(
        [cols(i["norm_mix"], KD), cols(i["norm_mem"], KD), cols(i["mem_norm"], KD)]
        + [tiles(i["conv_w"][0, j]) for j in range(4)]
        + [tiles(i[n][0]) for n in ("conv_b", "lru_ba", "lru_bx", "lru_lambda")], axis=1)
    rows = np.concatenate([i["final_norm"], i["b_group"][0], i["b_router"][0], i["diff_subln"][0],
                           i["diff_lambda"][0].reshape(-1), i["norm_ffn"][0]])[None, :]
    got = {"small": small, "rows": rows, "w_mix": w_mix, "w_gb": w_gb, "w_out_pieces": w_out,
           "rel_flipped": i["ca_rel_bias"][0, :, ::-1],
           "w_route": np.concatenate([i["w_group"][0], i["w_router"][0]], axis=1)}
    for n in ("wa", "wx"):
        blocks = i["lru_" + n][0]
        bd = np.zeros((KB, P, P), blocks.dtype)
        for k in range(2 * KB):
            o = (k % 2) * HD
            bd[k // 2, o:o + HD, o:o + HD] = blocks[k]
        got[n + "_bd"] = bd
    for n in ("x", "mem", "w_mq", "w_mk", "w_mv", "w_mo", "w1", "w3", "w2"):
        got[n] = i[n]
    return got


def kernel(**inputs):
    import concourse.bacc as bacc
    from concourse.bass_utils import run_bass_kernel_spmd

    inputs = {k: np.asarray(v) for k, v in inputs.items()}
    arrays = {n: np.ascontiguousarray(v) for n, v in {**laid_out(inputs), **constants()}.items()}
    nc = bacc.Bacc("TRN2", target_bir_lowering=False, num_devices=1)
    a = {n: nc.dram_tensor("in_" + n, list(v.shape), mybir.dt.from_np(v.dtype), kind="ExternalInput").ap()
         for n, v in arrays.items()}
    out = nc.dram_tensor("out_x", [1, N, D], F32, kind="ExternalOutput").ap()
    trunk(nc, a, out)
    r = run_bass_kernel_spmd(nc, [{"in_" + n: v for n, v in arrays.items()}], core_ids=[0])
    return r.results[0]["out_x"]
```

```python
from contextlib import ExitStack

import numpy as np

import concourse.bass as bass
from concourse import mybir

F32 = mybir.dt.float32
F32R = mybir.dt.float32r
U32 = mybir.dt.uint32
I32 = mybir.dt.int32
ALU = mybir.AluOpType
ACT = mybir.ActivationFunctionType
AX_X = mybir.AxisListType.X

P = 128
D = 1024
N = 512
CHUNK = 64
MEM = 256
KD = D // P
T = N // P
BW = 512
KB = BW // P
HD = 64
HEADS = 8
DIFF_HEADS = 4
REL_CLIP = 128
MX_HEADS = 4
GROUPS = 4
PER_GROUP = 8
EXPERTS = GROUPS * PER_GROUP
FF = 512
KF = FF // P
LAM_INIT = 0.2
NORM_EPS = 1e-6
GN_EPS = 1e-5
MASKED = -1e30
NO_SLOT = 1 << 20
SLOTS = 2 * N
LOGITS = GROUPS + EXPERTS
ROUTE_CONSTS = 2 * P + EXPERTS + 4 * P + 1
SMALL = 3 * KD + 8 * KB
ROWS = D + LOGITS + 2 * HD + 4 * HD
FIRST = 80
LIST = N + P
MAX_EXTRA = SLOTS // FIRST
JOBS = 16
LIST_UNIT = 16

AX0, AG0, BQ0, BK0, CQ0, CK0, DQ0, DK0 = (4 * i for i in range(8))
BV, CV, CG, DV = range(4)
FEAT_CHUNKS = 8
TOK_CHUNKS = 4
CW = 256
UNIT = (KD + KB) * P
PIECE = 2 * BW


class Steps:

    def __init__(self, eng, sem):
        self.eng, self.sem, self.n = eng, sem, 0

    def after(self, ins):
        self.n += 1
        ins.then_inc(self.sem, 1)
        self.eng.wait_ge(self.sem, self.n)


def trunk(nc, a, out):
    stack = ExitStack()
    with stack:
        held = []

        def sem(name):
            held.append(nc.alloc_semaphore(name=name))
            return held[-1]

        def free_semaphores():
            nc.clear_and_free_semaphores(held)
            held.clear()
            nc.all_engine_barrier()

        def sbuf(ctx, name, shape, dt=F32):
            return ctx.enter_context(nc.sbuf_tensor(name, shape, dt))

        def psum(ctx, name, shape=(P, 512), dt=F32):
            return ctx.enter_context(nc.psum_tensor(name, list(shape), dt))

        xn_dram = nc.dram_tensor("xn_scratch", [SLOTS, D], F32).ap()
        ys_dram = nc.dram_tensor("ys_scratch", [SLOTS, D], F32).ap()
        list_dram = nc.dram_tensor("list_scratch", [EXPERTS * LIST, 1], I32).ap()
        rel_dram = nc.dram_tensor("rel_scratch", [HEADS, P, 5 * P], F32).ap()
        jobs_dram = nc.dram_tensor("jobs_scratch", [1, P], I32).ap()

        x_sb = sbuf(stack, "x_sb", [P, T, D])
        ident = sbuf(stack, "ident", [P, P])
        small = sbuf(stack, "small", [P, SMALL])
        rows = sbuf(stack, "rows", [P, ROWS])
        gain_mix, gain_mem, gain_memn = (small[:, KD * i:KD * (i + 1)] for i in range(3))
        s0 = 3 * KD
        conv_w = [small[:, s0 + KB * j:s0 + KB * (j + 1)] for j in range(4)]
        conv_b, lru_ba, lru_bx, lru_lam = (small[:, s0 + KB * j:s0 + KB * (j + 1)] for j in range(4, 8))
        final_gain = rows[:, 0:D]
        router_bias = rows[:, D:D + LOGITS]
        subln = rows[:, D + LOGITS:D + LOGITS + 2 * HD]
        lam_vecs = rows[:, D + LOGITS + 2 * HD:ROWS]

        s_start = stack.enter_context(nc.semaphore("s_start"))

        def rms_transposed(ctx, pfx, src, tiles, gain, dst, first=None, keep=None, gain_row=None):
            s_ss, s_ms, s_sq, s_rinv, s_xn = (sem(f"{pfx}_{n}") for n in ("ss", "ms", "sq", "rinv", "xn"))
            s_tp, s_ev = [sem(f"{pfx}_tp{i}") for i in range(2)], [sem(f"{pfx}_ev{i}") for i in range(2)]
            s_hi = sem(f"{pfx}_hi")
            with ExitStack() as c:
                junk = sbuf(c, pfx + "_junk", [P, D])
                ss = sbuf(c, pfx + "_sums", [P, tiles])
                xn = keep if keep is not None else sbuf(c, pfx + "_xn", [P, tiles, D])
                ps = [psum(c, f"{pfx}_ps{i}") for i in range(2)]
                block = c.enter_context(nc.Block())

                @block.sync
                def _(sp):
                    if first is not None:
                        first(sp)

                @block.scalar
                def _(act):
                    for st in range(tiles + 1):
                        if st < tiles:
                            if first.tiles is not None:
                                act.wait_ge(first.tiles[st], 16)
                            if st:
                                act.wait_ge(s_ss, st)
                            nc.scalar.activation(junk[:], src[:, st, :], ACT.Square,
                                                 accum_out=ss[:, st:st + 1]).then_inc(s_ss, 1)
                        if st:
                            act.wait_ge(s_ms, st)
                            nc.scalar.activation(ss[:, st - 1:st], ss[:, st - 1:st], ACT.Sqrt).then_inc(s_sq, 1)
                    act.wait_ge(s_start, first.ready)
                    if isinstance(dst, tuple):
                        for k in range(KD):
                            act.wait_ge(s_tp[k % 2], k // 2 + 1)
                            nc.scalar.activation(dst[0][:, k, :], ps[k % 2][:, 0:tiles * P], ACT.Copy,
                                                 scale=gain[:, k:k + 1]).then_inc(s_hi, 1)
                        if first.beside is not None:
                            first.beside[0](act)
                        return
                    for k in range(1, KD, 2):
                        act.wait_ge(s_tp[1], k // 2 + 1)
                        nc.scalar.activation(dst[:, k, :], ps[1][:, 0:tiles * P], ACT.Copy,
                                             scale=1.0 if gain is None else gain[:, k:k + 1]
                                             ).then_inc(s_ev[1], 1)

                @block.vector
                def _(dve):
                    if gain_row is not None:
                        dve.wait_ge(s_start, first.ready)
                    for st in range(tiles + 1):
                        if st < tiles:
                            dve.wait_ge(s_ss, st + 1)
                            nc.vector.tensor_scalar(ss[:, st:st + 1], ss[:, st:st + 1], 1.0 / D, NORM_EPS,
                                                    ALU.mult, ALU.add).then_inc(s_ms, 1)
                        if st:
                            t = st - 1
                            dve.wait_ge(s_sq, st)
                            nc.vector.reciprocal(ss[:, t:st], ss[:, t:st]).then_inc(s_rinv, 1)
                            dve.wait_ge(s_rinv, st)
                            if gain_row is None:
                                nc.vector.tensor_scalar(xn[:, t, :], src[:, t, :], ss[:, t:st], None,
                                                        ALU.mult).then_inc(s_xn, 1)
                            else:
                                nc.vector.scalar_tensor_tensor(xn[:, t, :], src[:, t, :], ss[:, t:st], gain_row,
                                                               ALU.mult, ALU.mult).then_inc(s_xn, 1)
                    if isinstance(dst, tuple):
                        for k in range(KD):
                            dve.wait_ge(s_hi, k + 1)
                            nc.vector.scalar_tensor_tensor(dst[1][:, k, :], ps[k % 2][:, 0:tiles * P],
                                                           gain[:, k:k + 1], dst[0][:, k, :].bitcast(F32),
                                                           ALU.mult, ALU.subtract).then_inc(s_ev[k % 2], 1)
                        if first.beside is not None:
                            first.beside[1](dve)
                        return
                    for k in range(0, KD, 2):
                        dve.wait_ge(s_tp[0], k // 2 + 1)
                        nc.vector.tensor_scalar(dst[:, k, :], ps[0][:, 0:tiles * P],
                                                1.0 if gain is None else gain[:, k:k + 1], None,
                                                ALU.mult).then_inc(s_ev[0], 1)

                @block.tensor
                def _(pe):
                    pe.wait_ge(s_start, first.ready)
                    for k in range(KD):
                        if k >= 2:
                            pe.wait_ge(s_ev[k % 2], k // 2)
                        for t in range(tiles):
                            if k == 0:
                                pe.wait_ge(s_xn, t + 1)
                            last = nc.tensor.transpose(ps[k % 2][:, t * P:(t + 1) * P],
                                                       xn[:, t, k::KD], ident[:])
                        last.then_inc(s_tp[k % 2], 1)

        mix = ExitStack()
        hT_hi, hT_lo = (sbuf(mix, "hT_" + n, [P, KD, N], F32R) for n in ("hi", "lo"))
        z_at = nc.sbuf_base
        zT = sbuf(mix, "zT", [P, 4 * FEAT_CHUNKS, N])
        zR = nc.alloc_sbuf_tensor_at("zR", [P, 4 * FEAT_CHUNKS, N], F32R, offset=z_at)
        ztok_at = nc.sbuf_base
        ztok = sbuf(mix, "ztok", [P, TOK_CHUNKS, T, BW])
        s_wr = sem("rel_written")
        FAR = N - 1 - REL_CLIP


        mix_in = ExitStack()
        mix_raw = [sbuf(mix_in, f"mix_raw{b}", [P, KD, CW]) for b in range(2)]
        mix_hi, mix_lo = ([sbuf(mix_in, f"mix_{n}{b}", [P, KD, CW], F32R) for b in range(2)] for n in ("hi", "lo"))
        s_mix_raw, s_mix_hi, s_mix_split = (
            [sem(f"mix_{n}{b}") for b in range(2)] for n in ("raw", "hi", "split"))

        s_x_in = [sem(f"x_in{t}") for t in range(T)]

        def load_first(sp):
            for t in range(T):
                sp.dma_start(x_sb[:, t, :], a["x"][0, t * P:(t + 1) * P, :]).then_inc(s_x_in[t], 16)
            sp.dma_start(ident[:], a["ident"]).then_inc(s_start, 16)
            sp.dma_start(small[:], a["small"]).then_inc(s_start, 16)
            sp.dma_start(rows[:], bass.AP(a["rows"].tensor, 0, [[0, P], [1, ROWS]])).then_inc(s_start, 16)
            sp.wait_ge(s_start, 48)

            for b in range(2):
                sp.dma_start(mix_raw[b][:], a["w_mix"][b].rearrange("(p k) n -> p k n", k=KD)
                             ).then_inc(s_mix_raw[b], 16)

        load_first.ready = 48
        load_first.tiles = s_x_in

        def first_hi(act):
            act.wait_ge(s_mix_raw[0], 16)
            nc.scalar.copy(mix_hi[0][:], mix_raw[0][:]).then_inc(s_mix_hi[0], 1)

        def first_lo(dve):
            dve.wait_ge(s_mix_hi[0], 1)
            nc.vector.tensor_tensor(mix_lo[0][:], mix_raw[0][:], mix_hi[0][:].bitcast(F32), ALU.subtract
                                    ).then_inc(s_mix_split[0], 1)

        load_first.beside = first_hi, first_lo
        rms_transposed(stack, "rx", x_sb, T, gain_mix, (hT_hi, hT_lo), first=load_first,
                       keep=ztok[:, 0:2, :, :].rearrange("p c t n -> p (c t n)").rearrange("p (t d) -> p t d", t=T))

        with ExitStack() as c:
            w_raw, s_raw, w_hi, w_lo, s_hi, s_split = mix_raw, s_mix_raw, mix_hi, mix_lo, s_mix_hi, s_mix_split
            ps = [[psum(c, f"mix_ps{b}{j}") for j in range(2)] for b in range(2)]
            z_done, z_out = ([sem(f"mix_{n}{b}") for b in range(2)] for n in ("z", "out"))
            wa_sb = sbuf(c, "wa_sb", [P, KB, P])
            wx_sb = sbuf(c, "wx_sb", [P, KB, P])
            sp_lam = sbuf(c, "sp_lam", [P, 4, KB])
            rel = sbuf(c, "rel_row", [HEADS, 5 * P])
            xc, tr, ti, sq = (ztok[:, m, :, :] for m in range(TOK_CHUNKS))
            ge = zT[:, DK0:DK0 + KB, :]
            psr = [psum(c, f"lru_r{i}") for i in range(2)]
            psi = [psum(c, f"lru_i{i}") for i in range(2)]
            s_w, s_xc, s_g, s_act, s_dve, s_sp, s_sq, s_in, s_th, s_e, s_y, s_yhi, s_ylo, s_rel, s_ext = (
                sem("lru_" + n) for n in ("w", "xc", "g", "act", "dve", "sp", "sq", "inner", "tanh", "e", "y",
                                          "yhi", "ylo", "rel", "ext"))
            ax, ag = zT[:, AX0:AX0 + KB, :], zT[:, AG0:AG0 + KB, :]
            GELU_C, GELU_S = 0.044715, float(np.sqrt(2.0 / np.pi))
            EARLY = 2
            block = c.enter_context(nc.Block())

            def load(sp, i, b):
                sp.wait_ge(s_split[b], i + 1)
                sp.dma_start(w_raw[b][:], a["w_mix"][bass.ds(i * 2 + b, 1)].rearrange(
                    "o (p k) n -> p (o k) n", k=KD)).then_inc(s_raw[b], 16)

            def hi_part(act, i, b):
                act.wait_ge(s_raw[b], i * 16 + 16)
                act.wait_ge(z_done[b], i * 2 + 2)
                nc.scalar.copy(w_hi[b][:], w_raw[b][:]).then_inc(s_hi[b], 1)

            def lo_part(dve, i, b):
                dve.wait_ge(s_hi[b], i + 1)
                nc.vector.tensor_tensor(w_lo[b][:], w_raw[b][:], w_hi[b][:].bitcast(F32), ALU.subtract
                                        ).then_inc(s_split[b], 1)

            def products(pe, i, b, token_major):
                pe.wait_ge(s_split[b], i + 2)
                pe.wait_ge(z_out[b], i * 2 + 2)
                for j in range(2):
                    for t in range(2 if token_major else 1):
                        for k in range(KD):
                            for n, (hp, wp) in enumerate(((hT_hi, w_hi[b]), (hT_hi, w_lo[b]), (hT_lo, w_hi[b]))):
                                ends = {"start": k == 0 and n == 0, "stop": k == KD - 1 and n == 2}
                                if token_major:
                                    at = (j * 2 + t) * P
                                    last = nc.tensor.matmul(ps[b][j][:, t * CW:(t + 1) * CW],
                                                            hp[:, k, at:at + P], wp[:, k, :], **ends)
                                else:
                                    last = nc.tensor.matmul(ps[b][j][:], wp[:, k, j * P:(j + 1) * P],
                                                            hp[:, k, :], **ends)
                    last.then_inc(z_done[b], 1)

            def empty(eng, copy, i, b, j, token_major):
                eng.wait_ge(z_done[b], i * 2 + (2 + j + 1))
                if token_major:
                    m = i - FEAT_CHUNKS
                    dst = ztok[:, bass.ds(m, 1), 2 * j:2 * j + 2, b * CW:(b + 1) * CW].rearrange(
                        "p o t n -> p (o t) n")
                    src = ps[b][j][:].rearrange("p (t n) -> p t n", t=2)
                else:
                    dst = zT[:, bass.ds(i * 4 + (b * 2 + j), 1), :].rearrange("p o n -> p (o n)")
                    src = ps[b][j][:]
                copy(dst, src).then_inc(z_out[b], 1)

            def over_chunks(eng, step, extras):
                with eng.Fori(0, EARLY) as i:
                    for b in range(2):
                        step(i, b, False, True)
                for ch in range(2 * EARLY, 2 * FEAT_CHUNKS):
                    step(ch // 2, ch % 2, False, True)
                    for x in extras.get(ch, ()):
                        x()
                with eng.Fori(FEAT_CHUNKS, FEAT_CHUNKS + TOK_CHUNKS - 1) as i:
                    for b in range(2):
                        step(i, b, True, True)
                for b in range(2):
                    step(FEAT_CHUNKS + TOK_CHUNKS - 1, b, True, b == 0)

            @block.sync
            def _(sp):
                for b in range(2):
                    sp.sem_inc(s_split[b], 1)
                    sp.sem_inc(z_done[b], 2)
                    sp.sem_inc(z_out[b], 2)
                with sp.Fori(1, EARLY) as i:
                    for b in range(2):
                        load(sp, i, b)
                sp.dma_start(rel[:, FAR:FAR + 2 * REL_CLIP + 1], a["rel_flipped"]).then_inc(s_rel, 16)
                sp.dma_start(wa_sb[:], a["wa_bd"].rearrange("t c d -> c t d")).then_inc(s_w, 16)
                sp.dma_start(wx_sb[:], a["wx_bd"].rearrange("t c d -> c t d")).then_inc(s_w, 16)
                with sp.Fori(EARLY, FEAT_CHUNKS) as i:
                    for b in range(2):
                        load(sp, i, b)
                sp.wait_ge(s_ext, 3)
                sp.dma_start(rel_dram, rel[:].unsqueeze(1).to_broadcast([HEADS, P, 5 * P])).then_inc(s_wr, 16)
                with sp.Fori(FEAT_CHUNKS, FEAT_CHUNKS + TOK_CHUNKS) as i:
                    for b in range(2):
                        load(sp, i, b)
                sp.wait_ge(s_wr, 16)

            @block.tensor
            def _(pe):
                def lru_gates(t):
                    if t == 0:
                        pe.wait_ge(s_w, 32)
                    pe.wait_ge(s_xc, t + 1)
                    if t >= 2:
                        pe.wait_ge(s_act, 3 * (t - 1))
                    nc.tensor.matmul(psr[t % 2][:], wa_sb[:, t, :], xc[:, t, :], start=True, stop=True)
                    nc.tensor.matmul(psi[t % 2][:], wx_sb[:, t, :], xc[:, t, :], start=True,
                                     stop=True).then_inc(s_g, 1)

                over_chunks(pe, lambda i, b, tm, more: products(pe, i, b, tm),
                            {6: [lambda: lru_gates(0), lambda: lru_gates(1)],
                             8: [lambda: lru_gates(2), lambda: lru_gates(3)]})

            @block.scalar
            def _(act):
                def step(i, b, tm, more):
                    if more:
                        hi_part(act, i + b, 1 - b)
                    if isinstance(i, int):
                        if i * 2 + b == 2 * DK0 // 4:
                            act.wait_ge(s_y, KB)
                        if i * 2 + b == 2 * (FEAT_CHUNKS - 1) + 1:
                            act.wait_ge(s_ylo, KB)
                    empty(act, nc.scalar.copy, i, b, 0, tm)

                def decay_terms():
                    nc.scalar.activation(sp_lam[:, 0, :], lru_lam, ACT.Abs).then_inc(s_e, 1)
                    act.wait_ge(s_e, 1)
                    nc.scalar.activation(sp_lam[:, 1, :], sp_lam[:, 0, :], ACT.Exp, scale=-1.0).then_inc(s_e, 1)

                def gelu_tanh():
                    act.wait_ge(s_in, 1)
                    nc.scalar.activation(ge, ge, ACT.Tanh, scale=GELU_S).then_inc(s_th, 1)

                def gates_tanh(t):
                    if t == 0:
                        act.wait_ge(s_sp, 1)
                    act.wait_ge(s_g, t + 1)
                    nc.scalar.activation(tr[:, t, :], psr[t % 2][:], ACT.Tanh, scale=0.5,
                                         bias=sp_lam[:, 2, t:t + 1]).then_inc(s_act, 1)
                    nc.scalar.activation(ti[:, t, :], psi[t % 2][:], ACT.Tanh, scale=0.5,
                                         bias=sp_lam[:, 3, t:t + 1]).then_inc(s_act, 1)
                    act.wait_ge(s_act, 3 * t + 2)
                    nc.scalar.activation(tr[:, t, :], tr[:, t, :], ACT.Tanh, scale=sp_lam[:, 0, t:t + 1],
                                         bias=sp_lam[:, 0, t:t + 1]).then_inc(s_act, 1)

                def roots():
                    act.wait_ge(s_act, 3 * KB)
                    for t in range(KB):
                        nc.scalar.activation(sq[:, t, :], tr[:, t, :], ACT.Sqrt).then_inc(s_sq, 1)

                def y_hi(t):
                    act.wait_ge(s_y, t + 1)
                    nc.scalar.copy(zR[:, AX0 + t, :], tr[:, t, :]).then_inc(s_yhi, 1)

                over_chunks(act, step, {
                    4: [decay_terms], 6: [gelu_tanh],
                    7: [lambda: gates_tanh(0), lambda: gates_tanh(1)],
                    9: [lambda: gates_tanh(2), lambda: gates_tanh(3), roots],
                    11: [lambda: y_hi(0)], 12: [lambda: y_hi(1)], 13: [lambda: y_hi(2), lambda: y_hi(3)]})

            @block.vector
            def _(dve):
                do = Steps(dve, s_dve)

                def step(i, b, tm, more):
                    if more:
                        lo_part(dve, i + b, 1 - b)
                    empty(dve, nc.vector.tensor_copy, i, b, 1, tm)

                def rel_rows():
                    dve.wait_ge(s_rel, 16)
                    nc.vector.memset(rel[:, 0:FAR], 0.0).then_inc(s_ext, 1)
                    dve.wait_ge(s_ext, 1)
                    nc.vector.tensor_scalar(rel[:, 0:FAR], rel[:, 0:FAR], rel[:, FAR:FAR + 1], None,
                                            ALU.add).then_inc(s_ext, 1)
                    dve.wait_ge(s_ext, 2)
                    nc.vector.tensor_scalar(rel[:], rel[:], float(HD) ** 0.5, None, ALU.mult).then_inc(s_ext, 1)

                def convolve(t):
                    if t == 0:
                        for b in range(2):
                            dve.wait_ge(z_out[b], 2 + 2 * EARLY)
                    do.after(nc.vector.tensor_scalar(xc[:, t, :], ax[:, t, :], conv_w[3][:, t:t + 1],
                                                     conv_b[:, t:t + 1], ALU.mult, ALU.add))
                    for j in (2, 1, 0):
                        sh = 3 - j
                        ins = nc.vector.scalar_tensor_tensor(xc[:, t, sh:N], ax[:, t, 0:N - sh],
                                                             conv_w[j][:, t:t + 1], xc[:, t, sh:N],
                                                             ALU.mult, ALU.add)
                        if j:
                            do.after(ins)
                    ins.then_inc(s_xc, 1)

                def gelu_inner():
                    do.after(nc.vector.tensor_tensor(ge, ag, ag, ALU.mult))
                    do.after(nc.vector.tensor_scalar(ge, ge, GELU_C, 1.0, ALU.mult, ALU.add))
                    nc.vector.tensor_tensor(ge, ge, ag, ALU.mult).then_inc(s_in, 1)

                def softplus():
                    dve.wait_ge(s_e, 2)
                    e, s1, s2 = sp_lam[:, 1, :], sp_lam[:, 2, :], sp_lam[:, 3, :]
                    acc = sp_lam[:, 0, :]
                    do.after(nc.vector.tensor_scalar(s1, e, 2.0, None, ALU.add))
                    do.after(nc.vector.reciprocal(s1, s1))
                    do.after(nc.vector.tensor_tensor(s1, s1, e, ALU.mult))
                    do.after(nc.vector.tensor_tensor(s2, s1, s1, ALU.mult))
                    do.after(nc.vector.tensor_scalar(acc, s2, 1.0 / 17, 1.0 / 15, ALU.mult, ALU.add))
                    for m in (13, 11, 9, 7, 5, 3, 1):
                        do.after(nc.vector.tensor_tensor(acc, acc, s2, ALU.mult))
                        do.after(nc.vector.tensor_scalar(acc, acc, 1.0 / m, None, ALU.add))
                    do.after(nc.vector.tensor_tensor(acc, acc, s1, ALU.mult))
                    do.after(nc.vector.tensor_scalar(s1, lru_lam, -1.0, 0.0, ALU.mult, ALU.max))
                    do.after(nc.vector.scalar_tensor_tensor(acc, acc, 2.0, s1, ALU.mult, ALU.add))
                    do.after(nc.vector.tensor_scalar(acc, acc, 2.0, None, ALU.mult))
                    do.after(nc.vector.tensor_scalar(s1, lru_ba, 0.5, None, ALU.mult))
                    nc.vector.tensor_scalar(s2, lru_bx, 0.5, None, ALU.mult).then_inc(s_sp, 1)

                def gelu():
                    dve.wait_ge(s_th, 1)
                    do.after(nc.vector.scalar_tensor_tensor(ge, ge, 1.0, ag, ALU.add, ALU.mult))

                def recur(t):
                    dve.wait_ge(s_sq, t + 1)
                    do.after(nc.vector.tensor_scalar(tr[:, t, :], tr[:, t, :], 1.0, None, ALU.add))
                    do.after(nc.vector.reciprocal(tr[:, t, :], tr[:, t, :]))
                    do.after(nc.vector.tensor_tensor(sq[:, t, :], sq[:, t, :], tr[:, t, :], ALU.mult))
                    do.after(nc.vector.tensor_scalar(tr[:, t, :], tr[:, t, :], 2.0, -1.0, ALU.mult, ALU.add))
                    do.after(nc.vector.scalar_tensor_tensor(ti[:, t, :], ti[:, t, :], 1.0, xc[:, t, :],
                                                            ALU.add, ALU.mult))
                    do.after(nc.vector.tensor_tensor(sq[:, t, :], sq[:, t, :], ti[:, t, :], ALU.mult))
                    do.after(nc.vector.tensor_tensor_scan(xc[:, t, :], tr[:, t, :], sq[:, t, :], 0.0,
                                                          ALU.mult, ALU.add))
                    nc.vector.scalar_tensor_tensor(tr[:, t, :], xc[:, t, :], 0.5, ge[:, t, :],
                                                   ALU.mult, ALU.mult).then_inc(s_y, 1)

                def y_lo(t):
                    dve.wait_ge(s_yhi, t + 1)
                    nc.vector.tensor_tensor(zR[:, AG0 + t, :], tr[:, t, :], zR[:, AX0 + t, :].bitcast(F32),
                                            ALU.subtract
                                            ).then_inc(s_ylo, 1)

                over_chunks(dve, step, {
                    4: [rel_rows, softplus, lambda: convolve(0)], 5: [lambda: convolve(1), lambda: convolve(2)],
                    6: [gelu_inner, lambda: convolve(3)], 8: [gelu],
                    9: [lambda: recur(0)], 10: [lambda: recur(1)], 11: [lambda: recur(2), lambda: y_lo(0)],
                    12: [lambda: recur(3), lambda: y_lo(1)], 13: [lambda: y_lo(2)], 14: [lambda: y_lo(3)]})

        mix_in.close()
        free_semaphores()
        top = nc.sbuf_usable_end // 32 * 32
        alibi = nc.alloc_sbuf_tensor_at("alibi", [P, DIFF_HEADS, N], F32, offset=top - DIFF_HEADS * N * 4)
        g_raw = [nc.alloc_sbuf_tensor_at(f"g_raw{b}", [P, UNIT], F32,
                                         offset=top - DIFF_HEADS * N * 4 - (b + 1) * UNIT * 4) for b in range(2)]
        s_decay, s_alibi = sem("decay"), sem("alibi")
        s_g_raw = [sem(f"g_raw{b}") for b in range(2)]
        mem_sb = nc.alloc_sbuf_tensor_at("mem_sb", [P, MEM // P, D], F32, offset=top - DIFF_HEADS * N * 4)
        tables = ExitStack()
        decay = sbuf(tables, "decay", [P, HEADS, N])

        def y_turn(pe, s_y, s_tp, s_lo, src, ps, ready, ks=range(KB)):
            pe.wait_ge(s_y, ready)
            for k in ks:
                if k >= 2:
                    pe.wait_ge(s_lo, k - 1)
                for t in range(T):
                    last = nc.tensor.transpose(ps[k % 2][:, t * P:(t + 1) * P], src[:, t, k * P:(k + 1) * P],
                                               ident[:])
                last.then_inc(s_tp, 1)

        def y_hi_parts(act, s_tp, s_hi, at, ps, ks=range(KB)):
            for k in ks:
                act.wait_ge(s_tp, k + 1)
                nc.scalar.copy(zR[:, at + k, :], ps[k % 2][:]).then_inc(s_hi, 1)

        def y_lo_parts(dve, s_hi, s_lo, at, ps, ks=range(KB)):
            for k in ks:
                dve.wait_ge(s_hi, k + 1)
                nc.vector.tensor_tensor(zR[:, at + KB + k, :], ps[k % 2][:], zR[:, at + k, :].bitcast(F32),
                                        ALU.subtract
                                        ).then_inc(s_lo, 1)

        with ExitStack() as c:
            bias = sbuf(c, "rel_bias", [P, HEADS, N])
            neg = [sbuf(c, f"b_neg{i}", [P, N]) for i in range(2)]
            pr = [sbuf(c, f"b_p{i}", [P, N]) for i in range(3)]
            pT = [sbuf(c, f"b_pT{i}", [P, N]) for i in range(2)]
            otok = sbuf(c, "b_otok", [P, T, BW])
            nmax = sbuf(c, "b_nmax", [P, HEADS * T])
            rsum = sbuf(c, "b_rsum", [P, HEADS * T])
            ps_s = [psum(c, f"b_s{i}") for i in range(3)]
            ps_t = [psum(c, f"b_t{i}") for i in range(2)]
            ps_o = [psum(c, f"b_o{i}") for i in range(2)]
            s_bias = [sem(f"b_bias{h}") for h in range(HEADS)]
            s_mask, s_s, s_neg, s_exp, s_t, s_pt, s_pv, s_o, s_dve, s_tp, s_yhi, s_lo = (
                sem("b_" + n) for n in ("mask", "s", "neg", "exp", "t", "pt", "pv", "o", "dve", "tp", "yhi",
                                        "ylo"))
            U = HEADS * T
            SC = float(HD) ** -0.5
            block = c.enter_context(nc.Block())

            @block.sync
            def _(sp):
                for h in range(HEADS):
                    sp.dma_start(bias[:, h, :], bass.AP(rel_dram.tensor, h * P * 5 * P + P - 1,
                                                        [[5 * P - 1, P], [1, N]])).then_inc(s_bias[h], 16)
                sp.dma_start(decay[:], a["decay"]).then_inc(s_decay, 16)

            @block.gpsimd
            def _(pool):
                for h in range(HEADS):
                    pool.wait_ge(s_bias[h], 16)
                    nc.gpsimd.memset(bias[0:CHUNK, h, N - CHUNK:N], MASKED).then_inc(s_mask, 1)

            @block.tensor
            def _(pe):
                for st in range(U + 3):
                    if st < U:
                        h, t = divmod(st, T)
                        lo = (h % 2) * HD
                        if st >= 3:
                            pe.wait_ge(s_neg, st - 2)
                        nc.tensor.matmul(ps_s[st % 3][:, 0:(t + 1) * P],
                                         zT[lo:lo + HD, BQ0 + h // 2, t * P:(t + 1) * P],
                                         zT[lo:lo + HD, BK0 + h // 2, 0:(t + 1) * P],
                                         start=True, stop=True).then_inc(s_s, 1)
                    if 0 <= st - 2 < U:
                        u = st - 2
                        pe.wait_ge(s_exp, u + 1)
                        if u >= 2:
                            pe.wait_ge(s_pt, u - 1)
                        for b in range(u % T + 1):
                            last = nc.tensor.transpose(ps_t[u % 2][:, b * P:(b + 1) * P],
                                                       pr[u % 3][:, b * P:(b + 1) * P], ident[:])
                        last.then_inc(s_t, 1)
                    if 0 <= st - 3:
                        u = st - 3
                        h, t = divmod(u, T)
                        pe.wait_ge(s_pt, u + 1)
                        if t == 0 and h >= 2:
                            pe.wait_ge(s_o, h - 1)
                        for b in range(t + 1):
                            last = nc.tensor.matmul(ps_o[h % 2][:, t * HD:(t + 1) * HD],
                                                    pT[u % 2][:, b * P:(b + 1) * P],
                                                    ztok[:, BV, b, h * HD:(h + 1) * HD],
                                                    start=(b == 0), stop=(b == t))
                        last.then_inc(s_pv, 1)
                y_turn(pe, s_o, s_tp, s_lo, otok, ps_t, HEADS)

            @block.scalar
            def _(act):
                for u in range(U):
                    w = (u % T + 1) * P
                    act.wait_ge(s_neg, u + 1)
                    if u >= 3:
                        act.wait_ge(s_t, u - 2)
                    nc.scalar.activation(pr[u % 3][:, 0:w], neg[u % 2][:, 0:w], ACT.Exp, scale=-1.0,
                                         bias=nmax[:, u:u + 1], accum_out=rsum[:, u:u + 1]).then_inc(s_exp, 1)
                y_hi_parts(act, s_tp, s_yhi, BQ0, ps_t)

            @block.vector
            def _(dve):
                do = Steps(dve, s_dve)
                for st in range(U + 4):
                    if st < U:
                        h, t = divmod(st, T)
                        w = (t + 1) * P
                        if t == 0:
                            dve.wait_ge(s_mask, h + 1)
                        dve.wait_ge(s_s, st + 1)
                        if st >= 2:
                            dve.wait_ge(s_exp, st - 1)
                        nc.vector.tensor_tensor_reduce(neg[st % 2][:, 0:w], ps_s[st % 3][:, 0:w],
                                                       bias[:, h, N - w:N], -SC, 3e38, ALU.add, ALU.min,
                                                       nmax[:, st:st + 1]).then_inc(s_neg, 1)
                    if 0 <= st - 2 < U:
                        u = st - 2
                        w = (u % T + 1) * P
                        dve.wait_ge(s_t, u + 1)
                        if u >= 2:
                            dve.wait_ge(s_pv, u - 1)
                        nc.vector.tensor_copy(pT[u % 2][:, 0:w], ps_t[u % 2][:, 0:w]).then_inc(s_pt, 1)
                    if st >= 4 and (st - 4) % T == T - 1:
                        h = (st - 4) // T
                        rs = rsum[:, h * T:(h + 1) * T]
                        dve.wait_ge(s_pv, h * T + T)
                        do.after(nc.vector.reciprocal(rs, rs))
                        nc.vector.tensor_tensor(otok[:, :, h * HD:(h + 1) * HD],
                                                ps_o[h % 2][:, 0:T * HD].rearrange("p (t e) -> p t e", t=T),
                                                rs.unsqueeze(2).to_broadcast([P, T, HD]),
                                                ALU.mult).then_inc(s_o, 1)
                y_lo_parts(dve, s_yhi, s_lo, BQ0, ps_t)

        with ExitStack() as c:
            pd = [sbuf(c, f"c_p{i}", [P, 10 * P]) for i in range(2)]
            otok = sbuf(c, "c_otok", [P, T, BW])
            tmp = [sbuf(c, f"c_tmp{i}", [P, T, HD]) for i in range(2)]
            gate = sbuf(c, "c_gate", [P, T, BW])
            mu = sbuf(c, "c_mu", [P, HEADS, T])
            var = sbuf(c, "c_var", [P, HEADS, T])
            ps_s = [psum(c, f"c_s{i}") for i in range(4)]
            ps_o = [psum(c, f"c_o{i}") for i in range(2)]
            ps_t = [psum(c, f"c_t{i}") for i in range(2)]
            s_s, s_p, s_pv, s_o, s_dve, s_v, s_sq, s_th, s_y, s_tp, s_yhi, s_lo = (
                sem("c_" + n) for n in ("s", "p", "pv", "o", "dve", "var", "sqrt", "tanh", "y", "tp", "yhi",
                                        "ylo"))
            off = [0, 4 * P, 7 * P, 9 * P]
            block = c.enter_context(nc.Block())

            @block.sync
            def _(sp):
                sp.dma_start(alibi[:], a["alibi"]).then_inc(s_alibi, 16)

            @block.tensor
            def _(pe):
                def scores(h):
                    lo = (h % 2) * HD
                    for j in range(T):
                        u = h * T + j
                        if u >= 4:
                            pe.wait_ge(s_p, u - 3)
                        nc.tensor.matmul(ps_s[j][:, 0:N - j * P],
                                         zT[lo:lo + HD, CK0 + h // 2, j * P:(j + 1) * P],
                                         zT[lo:lo + HD, CQ0 + h // 2, j * P:N],
                                         start=True, stop=True).then_inc(s_s, 1)

                def outputs(h):
                    if h >= 2:
                        pe.wait_ge(s_o, h - 1)
                    pe.wait_ge(s_p, h * T + T)
                    for i in range(T):
                        for j in range(i + 1):
                            o = off[j] + (i - j) * P
                            last = nc.tensor.matmul(ps_o[h % 2][:, i * HD:(i + 1) * HD],
                                                    pd[h % 2][:, o:o + P],
                                                    ztok[:, CV, j, h * HD:(h + 1) * HD],
                                                    start=(j == 0), stop=(j == i))
                    last.then_inc(s_pv, 1)

                for st in range(HEADS + 1):
                    if st < HEADS:
                        scores(st)
                    if st:
                        outputs(st - 1)
                    if st >= 4 and st % 2 == 0:
                        y_turn(pe, s_y, s_tp, s_lo, otok, ps_t, st - 2, [st // 2 - 2])
                y_turn(pe, s_y, s_tp, s_lo, otok, ps_t, HEADS, [KB - 1])

            @block.scalar
            def _(act):
                nc.scalar.activation(gate[:], ztok[:, CG, :, :], ACT.Tanh, scale=0.5).then_inc(s_th, 1)
                for h in range(HEADS):
                    act.wait_ge(s_v, h + 1)
                    nc.scalar.activation(var[:, h, :], var[:, h, :], ACT.Sqrt).then_inc(s_sq, 1)
                    if h in (3, 5):
                        y_hi_parts(act, s_tp, s_yhi, CQ0, ps_t, [h // 2 - 1])
                y_hi_parts(act, s_tp, s_yhi, CQ0, ps_t, [KB - 2, KB - 1])

            @block.vector
            def _(dve):
                do = Steps(dve, s_dve)

                def heads(o, h):
                    return o[:, :, h * HD:(h + 1) * HD]

                def centre(h):
                    o, t, m, v = heads(otok, h), tmp[h % 2][:], mu[:, h, :], var[:, h, :]
                    dve.wait_ge(s_o, h + 1)
                    do.after(nc.vector.tensor_reduce(m, o, AX_X, ALU.add))
                    do.after(nc.vector.tensor_scalar(m, m, 1.0 / HD, None, ALU.mult))
                    do.after(nc.vector.tensor_tensor(o, o, m.unsqueeze(2).to_broadcast([P, T, HD]), ALU.subtract))
                    do.after(nc.vector.tensor_tensor(t, o, o, ALU.mult))
                    do.after(nc.vector.tensor_reduce(v, t, AX_X, ALU.add))
                    nc.vector.tensor_scalar(v, v, 1.0 / HD, GN_EPS, ALU.mult, ALU.add).then_inc(s_v, 1)

                def finish(h):
                    o, v = heads(otok, h), var[:, h, :]
                    dve.wait_ge(s_sq, h + 1)
                    do.after(nc.vector.reciprocal(v, v))
                    do.after(nc.vector.tensor_tensor(o, o, v.unsqueeze(2).to_broadcast([P, T, HD]), ALU.mult))
                    nc.vector.scalar_tensor_tensor(o, o, 0.5, heads(gate, h), ALU.mult, ALU.mult
                                                   ).then_inc(s_y, 1)

                dve.wait_ge(s_decay, 16)
                for st in range(HEADS + 1):
                    if st < HEADS:
                        if st >= 2:
                            dve.wait_ge(s_pv, st - 1)
                        for j in range(T):
                            dve.wait_ge(s_s, st * T + j + 1)
                            nc.vector.tensor_tensor(pd[st % 2][:, off[j]:off[j] + N - j * P],
                                                    ps_s[j][:, 0:N - j * P], decay[:, st, 0:N - j * P],
                                                    ALU.mult).then_inc(s_p, 1)
                    if st == 0:
                        dve.wait_ge(s_th, 1)
                        do.after(nc.vector.scalar_tensor_tensor(gate[:], gate[:], 1.0, ztok[:, CG, :, :],
                                                                ALU.add, ALU.mult))
                    if st >= 2:
                        finish(st - 2)
                    if st in (5, 7):
                        y_lo_parts(dve, s_yhi, s_lo, CQ0, ps_t, [(st - 5) // 2])
                    if st:
                        h = st - 1
                        dve.wait_ge(s_pv, h + 1)
                        nc.vector.tensor_copy(heads(otok, h), ps_o[h % 2][:, 0:T * HD].rearrange(
                            "p (t e) -> p t e", t=T)).then_inc(s_o, 1)
                        centre(h)
                finish(HEADS - 1)
                y_lo_parts(dve, s_yhi, s_lo, CQ0, ps_t, [KB - 2, KB - 1])
        tables.close()

        with ExitStack() as c:
            neg = [[sbuf(c, f"d_neg{i}{m}", [P, N]) for m in range(2)] for i in range(2)]
            pr = [[sbuf(c, f"d_p{i}{m}", [P, N]) for m in range(2)] for i in range(2)]
            pT = [sbuf(c, f"d_pT{i}", [P, N]) for i in range(2)]
            otok = sbuf(c, "d_otok", [P, T, BW])
            tmp = sbuf(c, "d_tmp", [P, T, P])
            U = DIFF_HEADS * T
            nmax = sbuf(c, "d_nmax", [P, 2, U])
            rsum = sbuf(c, "d_rsum", [P, 2, U])
            coef = sbuf(c, "d_coef", [P, U])
            lam = sbuf(c, "d_lam", [P, 4])
            lamt = sbuf(c, "d_lamt", [P, HD])
            ms = sbuf(c, "d_ms", [P, U])
            ps_s = [[psum(c, f"d_s{i}{m}") for m in range(2)] for i in range(2)]
            ps_t = [psum(c, f"d_t{i}") for i in range(2)]
            ps_o = [psum(c, f"d_o{i}") for i in range(2)]
            s_ld, s_s, s_neg, s_exp, s_at, s_t, s_pt, s_pv, s_o, s_dve, s_lam, s_le, s_v, s_sq, s_y, s_tp, s_yhi, s_lo = (
                sem("d_" + n) for n in ("ld", "s", "neg", "exp", "attn", "t", "pt", "pv", "o", "dve", "lam", "lexp",
                                        "var", "sqrt", "y", "tp", "yhi", "ylo"))
            SC = float(HD) ** -0.5
            block = c.enter_context(nc.Block())

            @block.sync
            def _(sp):
                for b in range(2):
                    sp.dma_start(g_raw[b][:], a["w_gb"][b]).then_inc(s_g_raw[b], 16)

            @block.tensor
            def _(pe):
                for st in range(U + 3):
                    if st < U:
                        h, t = divmod(st, T)
                        if st >= 2:
                            pe.wait_ge(s_neg, 2 * (st - 1))
                        for m in range(2):
                            nc.tensor.matmul(ps_s[st % 2][m][:, 0:(t + 1) * P],
                                             zT[m * HD:(m + 1) * HD, DQ0 + h, t * P:(t + 1) * P],
                                             zT[m * HD:(m + 1) * HD, DK0 + h, 0:(t + 1) * P],
                                             start=True, stop=True).then_inc(s_s, 1)
                    if 0 <= st - 2 < U:
                        u = st - 2
                        pe.wait_ge(s_at, u + 1)
                        if u >= 2:
                            pe.wait_ge(s_pt, u - 1)
                        for b in range(u % T + 1):
                            last = nc.tensor.transpose(ps_t[u % 2][:, b * P:(b + 1) * P],
                                                       pr[u % 2][0][:, b * P:(b + 1) * P], ident[:])
                        last.then_inc(s_t, 1)
                    if 0 <= st - 3:
                        u = st - 3
                        h, t = divmod(u, T)
                        pe.wait_ge(s_pt, u + 1)
                        if t == 0 and h >= 2:
                            pe.wait_ge(s_o, h - 1)
                        for b in range(t + 1):
                            last = nc.tensor.matmul(ps_o[h % 2][:, t * P:(t + 1) * P],
                                                    pT[u % 2][:, b * P:(b + 1) * P],
                                                    ztok[:, DV, b, h * P:(h + 1) * P],
                                                    start=(b == 0), stop=(b == t))
                        last.then_inc(s_pv, 1)
                y_turn(pe, s_y, s_tp, s_lo, otok, ps_t, DIFF_HEADS)

            @block.scalar
            def _(act):
                def root(h):
                    m = ms[:, h * T:(h + 1) * T]
                    act.wait_ge(s_v, h + 1)
                    nc.scalar.activation(m, m, ACT.Sqrt).then_inc(s_sq, 1)

                act.wait_ge(s_lam, 1)
                nc.scalar.activation(lam[:, 0:2], lam[:, 0:2], ACT.Exp).then_inc(s_le, 1)
                for u in range(U):
                    w = (u % T + 1) * P
                    if u >= 2:
                        act.wait_ge(s_t, u - 1)
                    for m in range(2):
                        act.wait_ge(s_neg, 2 * u + m + 1)
                        nc.scalar.activation(pr[u % 2][m][:, 0:w], neg[u % 2][m][:, 0:w], ACT.Exp, scale=-1.0,
                                             bias=nmax[:, m, u:u + 1],
                                             accum_out=rsum[:, m, u:u + 1]).then_inc(s_exp, 1)
                    if u >= 4 and (u - 4) % T == T - 1:
                        root((u - 4) // T)
                root(DIFF_HEADS - 1)
                y_hi_parts(act, s_tp, s_yhi, DQ0, ps_t)

            @block.vector
            def _(dve):
                do = Steps(dve, s_dve)
                for i in range(2):
                    ins = nc.vector.tensor_tensor_reduce(lamt[:], lam_vecs[:, 2 * i * HD:(2 * i + 1) * HD],
                                                         lam_vecs[:, (2 * i + 1) * HD:(2 * i + 2) * HD],
                                                         1.0, 0.0, ALU.mult, ALU.add, lam[:, i:i + 1])
                    if i == 0:
                        do.after(ins)
                ins.then_inc(s_lam, 1)
                dve.wait_ge(s_le, 1)
                do.after(nc.vector.tensor_tensor(lam[:, 2:3], lam[:, 1:2], lam[:, 0:1], ALU.subtract))
                do.after(nc.vector.tensor_scalar(lam[:, 3:4], lam[:, 2:3], -LAM_INIT, None, ALU.add))
                dve.wait_ge(s_alibi, 16)

                def squares(h):
                    o, m = otok[:, :, h * P:(h + 1) * P], ms[:, h * T:(h + 1) * T]
                    dve.wait_ge(s_o, h + 1)
                    do.after(nc.vector.tensor_tensor(tmp[:], o, o, ALU.mult))
                    do.after(nc.vector.tensor_reduce(m, tmp[:], AX_X, ALU.add))
                    nc.vector.tensor_scalar(m, m, 1.0 / P, GN_EPS, ALU.mult, ALU.add).then_inc(s_v, 1)

                def finish(h):
                    o, m = otok[:, :, h * P:(h + 1) * P], ms[:, h * T:(h + 1) * T]
                    wide = [P, T, P]
                    dve.wait_ge(s_sq, h + 1)
                    do.after(nc.vector.reciprocal(m, m))
                    do.after(nc.vector.tensor_scalar(m, m, 1.0 - LAM_INIT, None, ALU.mult))
                    do.after(nc.vector.tensor_tensor(o, o, m.unsqueeze(2).to_broadcast(wide), ALU.mult))
                    nc.vector.tensor_tensor(o, o, subln.unsqueeze(1).to_broadcast(wide), ALU.mult
                                            ).then_inc(s_y, 1)

                for st in range(U + 4):
                    if st < U:
                        h, t = divmod(st, T)
                        w = (t + 1) * P
                        if st >= 2:
                            dve.wait_ge(s_exp, 2 * (st - 1))
                        for m in range(2):
                            dve.wait_ge(s_s, 2 * st + m + 1)
                            nc.vector.tensor_tensor_reduce(neg[st % 2][m][:, 0:w], ps_s[st % 2][m][:, 0:w],
                                                           alibi[:, h, N - w:N], -SC, 3e38, ALU.add, ALU.min,
                                                           nmax[:, m, st:st + 1]).then_inc(s_neg, 1)
                    if 0 <= st - 1 < U:
                        u = st - 1
                        w = (u % T + 1) * P
                        dve.wait_ge(s_exp, 2 * u + 2)
                        do.after(nc.vector.reciprocal(coef[:, u:u + 1], rsum[:, 1, u:u + 1]))
                        do.after(nc.vector.tensor_scalar(coef[:, u:u + 1], coef[:, u:u + 1],
                                                         rsum[:, 0, u:u + 1], lam[:, 3:4], ALU.mult, ALU.mult))
                        nc.vector.scalar_tensor_tensor(pr[u % 2][0][:, 0:w], pr[u % 2][1][:, 0:w],
                                                       coef[:, u:u + 1], pr[u % 2][0][:, 0:w],
                                                       ALU.mult, ALU.add).then_inc(s_at, 1)
                    if 0 <= st - 2 < U:
                        u = st - 2
                        w = (u % T + 1) * P
                        dve.wait_ge(s_t, u + 1)
                        if u >= 2:
                            dve.wait_ge(s_pv, u - 1)
                        nc.vector.tensor_copy(pT[u % 2][:, 0:w], ps_t[u % 2][:, 0:w]).then_inc(s_pt, 1)
                    if st >= 4 and (st - 4) % T == T - 1:
                        h = (st - 4) // T
                        rs = rsum[:, 0, h * T:(h + 1) * T]
                        dve.wait_ge(s_pv, h * T + T)
                        do.after(nc.vector.reciprocal(rs, rs))
                        nc.vector.tensor_tensor(otok[:, :, h * P:(h + 1) * P],
                                                ps_o[h % 2][:].rearrange("p (t e) -> p t e", t=T),
                                                rs.unsqueeze(2).to_broadcast([P, T, P]),
                                                ALU.mult).then_inc(s_o, 1)
                        squares(h)
                    if st >= 6 and (st - 6) % T == T - 1:
                        finish((st - 6) // T)
                finish(DIFF_HEADS - 1)
                y_lo_parts(dve, s_yhi, s_lo, DQ0, ps_t)

        with ExitStack() as c:
            w_raw, s_raw = g_raw, s_g_raw
            w_hi = [sbuf(c, f"g_hi{b}", [P, UNIT], F32R) for b in range(2)]
            w_lo = [sbuf(c, f"g_lo{b}", [P, UNIT], F32R) for b in range(2)]
            tg = [sbuf(c, f"g_t{b}", [P, N]) for b in range(4)]
            m_sum = [sbuf(c, f"g_m{b}", [P, N]) for b in range(2)]
            m_hi, m_lo = (nc.alloc_sbuf_tensor_at(f"merged_{n}", [P, KD, N], F32R, offset=ztok_at + o)
                          for n, o in (("hi", 0), ("lo", KD * N * 4)))
            Y_HI = (AX0, BQ0, CQ0, DQ0)
            ps_g = [psum(c, f"g_g{b}") for b in range(2)]
            ps_b = [psum(c, f"g_p{b}") for b in range(2)]
            ps_w = [[psum(c, f"o_ps{t}") for t in range(T)], [ps_g[0], ps_g[1], ps_b[0], ps_b[1]]]
            s_hi, s_split, s_unit = ([sem(f"g_{n}{b}") for b in range(2)] for n in ("hi", "split", "unit"))
            s_g, s_t, s_mul = ([sem(f"g_{n}{b}") for b in range(4)] for n in ("gate", "tanh", "mul"))
            s_mem = sem("mem")
            s_sum, s_mhi, s_mlo, s_x = sem("g_sum"), sem("g_mhi"), sem("g_mlo"), sem("o_x")
            PIECES = 2 * KD // 2
            block = c.enter_context(nc.Block())

            def hi_part(act, n, b, w=UNIT):
                act.wait_ge(s_raw[b], n * 16 + 16)
                act.wait_ge(s_unit[b], n + 1)
                nc.scalar.copy(w_hi[b][:, 0:w], w_raw[b][:, 0:w]).then_inc(s_hi[b], 1)

            def lo_part(dve, n, b, w=UNIT):
                dve.wait_ge(s_hi[b], n + 1)
                nc.vector.tensor_tensor(w_lo[b][:, 0:w], w_raw[b][:, 0:w], w_hi[b][:, 0:w].bitcast(F32),
                                        ALU.subtract).then_inc(s_split[b], 1)

            def part_after(part, i, br, last=False):
                if last and br == 3:
                    part(2 * KD, 0, w=PIECE)
                else:
                    part(i * 2 + (br + 1) // 2, (br + 1) % 2)

            def passes(x_hi, x_lo, hi, lo):
                return (x_hi, hi), (x_hi, lo), (x_lo, hi)

            @block.sync
            def _(sp):
                for q in (*s_split, *s_unit, *s_t, *s_mul):
                    sp.sem_inc(q, 1)
                sp.dma_start(mem_sb[:], a["mem"].rearrange("b (t p) d -> p (b t) d", p=P)).then_inc(s_mem, 16)

                def load(i, br):
                    sp.wait_ge(s_split[br % 2], i * 2 + (br // 2 + 2))
                    sp.dma_start(w_raw[br % 2][:], a["w_gb"][bass.ds(i * 4 + (br + 2), 1)].rearrange(
                        "o p n -> p (o n)")).then_inc(s_raw[br % 2], 16)

                with sp.Fori(0, KD - 1) as i:
                    for br in range(4):
                        load(i, br)
                for br in range(2):
                    load(KD - 1, br)
                for u in range(PIECES):
                    b = u % 2
                    sp.wait_ge(s_split[b], 2 * KD + u // 2 + 1)
                    sp.dma_start(w_raw[b][:, 0:PIECE], a["w_out_pieces"][u]).then_inc(s_raw[b], 16)
                sp.wait_ge(s_mem, 16)

            @block.tensor
            def _(pe):
                with pe.Fori(0, KD) as i:
                    for br in range(4):
                        b = br % 2
                        pe.wait_ge(s_split[b], i * 2 + (br // 2 + 2))
                        pe.wait_ge(s_t[(br + 2) % 4], i + (2 if br >= 2 else 1))
                        for k in range(KD):
                            for n, (hp, wp) in enumerate(passes(hT_hi, hT_lo, w_hi[b], w_lo[b])):
                                last = nc.tensor.matmul(ps_g[b][:], wp[:, k * P:(k + 1) * P], hp[:, k, :],
                                                        start=(k == 0 and n == 0), stop=(k == KD - 1 and n == 2))
                        last.then_inc(s_g[br], 1)
                        pe.wait_ge(s_mul[(br + 2) % 4], i + (2 if br >= 2 else 1))
                        for k in range(KB):
                            for n, (at, wp) in enumerate(passes(Y_HI[br] + k, Y_HI[br] + KB + k,
                                                                w_hi[b], w_lo[b])):
                                last = nc.tensor.matmul(ps_b[b][:], wp[:, (KD + k) * P:(KD + k + 1) * P],
                                                        zR[:, at, :], start=(k == 0 and n == 0),
                                                        stop=(k == KB - 1 and n == 2))
                        last.then_inc(s_unit[b], 1)
                for u in range(PIECES):
                    b, half, pair = u % 2, u // (KD // 2), u % (KD // 2)
                    pe.wait_ge(s_split[b], 2 * KD + u // 2 + 2)
                    pe.wait_ge(s_mlo, min(KD, 2 * pair + 2) if half == 0 else KD)
                    if u == PIECES // 2:
                        for q in s_mul[2:]:
                            pe.wait_ge(q, KD + 1)
                    for t in range(T):
                        for kk in range(2):
                            k = pair * 2 + kk
                            for n, (mp, wp) in enumerate(passes(m_hi, m_lo, w_hi[b], w_lo[b])):
                                last = nc.tensor.matmul(ps_w[half][t][:], mp[:, k, t * P:(t + 1) * P],
                                                        wp[:, kk * BW:(kk + 1) * BW],
                                                        start=(k == 0 and n == 0), stop=(k == KD - 1 and n == 2))
                    last.then_inc(s_unit[b], 1)

            @block.scalar
            def _(act):
                def part(n, b, w=UNIT):
                    hi_part(act, n, b, w)

                def tile(i, m, last):
                    for br in range(4):
                        part_after(part, i, br, last)
                        act.wait_ge(s_g[br], i + 1)
                        act.wait_ge(s_mul[br], i + 1)
                        nc.scalar.activation(tg[br][:], ps_g[br % 2][:], ACT.Tanh, scale=0.5).then_inc(s_t[br], 1)
                    act.wait_ge(s_sum, i * 3 + 3)
                    nc.scalar.copy(m_hi[:, bass.ds(i, 1), :].rearrange("p o n -> p (o n)"), m_sum[m][:]
                                   ).then_inc(s_mhi, 1)

                hi_part(act, 0, 0)
                with act.Fori(0, KD // 2 - 1) as i:
                    tile(i * 2, 0, False)
                    tile(i * 2 + 1, 1, False)
                tile(KD - 2, 0, False)
                tile(KD - 1, 1, True)
                for u in range(1, PIECES):
                    hi_part(act, 2 * KD + u // 2, u % 2, PIECE)

            @block.vector
            def _(dve):
                def part(n, b, w=UNIT):
                    lo_part(dve, n, b, w)

                def tile(i, m, last):
                    m_sb = m_sum[m][:]
                    for br in range(4):
                        part_after(part, i, br, last)
                        b = br % 2
                        dve.wait_ge(s_t[br], i + 2)
                        dve.wait_ge(s_unit[b], i * 2 + (br // 2 + 2))
                        nc.vector.scalar_tensor_tensor(m_sb if br == 0 else tg[br][:], tg[br][:], 1.0,
                                                       ps_b[b][:], ALU.add, ALU.mult).then_inc(s_mul[br], 1)
                        if br:
                            dve.wait_ge(s_mul[br], i + 2)
                            if br == 1:
                                dve.wait_ge(s_mul[0], i + 2)
                            else:
                                dve.wait_ge(s_sum, i * 3 + (br - 1))
                            nc.vector.tensor_tensor(m_sb, m_sb, tg[br][:], ALU.add).then_inc(s_sum, 1)
                    dve.wait_ge(s_mhi, i + 1)
                    o = bass.ds(i, 1)
                    nc.vector.tensor_tensor(m_lo[:, o, :].rearrange("p o n -> p (o n)"), m_sb,
                                            m_hi[:, o, :].rearrange("p o n -> p (o n)").bitcast(F32),
                                            ALU.subtract).then_inc(s_mlo, 1)

                lo_part(dve, 0, 0)
                with dve.Fori(0, KD // 2 - 1) as i:
                    tile(i * 2, 0, False)
                    tile(i * 2 + 1, 1, False)
                tile(KD - 2, 0, False)
                tile(KD - 1, 1, True)

                def add(half):
                    u = (half + 1) * PIECES // 2 - 1
                    dve.wait_ge(s_unit[u % 2], 2 * KD + u // 2 + 2)
                    for t in range(T):
                        xs = x_sb[:, t, half * BW:(half + 1) * BW]
                        nc.vector.scalar_tensor_tensor(xs, ps_w[half][t][:], 0.5, xs, ALU.mult, ALU.add
                                                       ).then_inc(s_x, 1)

                for u in range(1, PIECES):
                    lo_part(dve, 2 * KD + u // 2, u % 2, PIECE)
                    if u == PIECES // 2:
                        add(0)
                add(1)
        mix.close()
        free_semaphores()

        with ExitStack() as c:
            qT = sbuf(c, "m_qT", [P, MX_HEADS, N])
            kT = sbuf(c, "m_kT", [P, MX_HEADS, MEM])
            v = sbuf(c, "m_v", [P, MEM // P, BW])
            MT = MEM // P
            HALF_W = KD * BW // 2
            SLOTS_W = 4
            wo_hi = [sbuf(c, f"m_hi{j}", [P, HALF_W], F32R) for j in (2, 3)]
            wo_lo = [sbuf(c, f"m_lo{j}", [P, HALF_W], F32R) for j in (2, 3)]
            with ExitStack() as c2:
                w_hi = [sbuf(c2, f"m_hi{j}", [P, HALF_W], F32R) for j in (0, 1)] + wo_hi
                w_lo = [sbuf(c2, f"m_lo{j}", [P, HALF_W], F32R) for j in (0, 1)] + wo_lo
                w_raw = [sbuf(c2, f"m_raw{b}", [P, HALF_W]) for b in range(2)]
                h_parts = [sbuf(c2, "h2T_" + n, [P, KD, N], F32R) for n in ("hi", "lo")]
                m_parts = [sbuf(c2, "memT_" + n, [P, KD, MEM], F32R) for n in ("hi", "lo")]
                xn = sbuf(c2, "m_xn", [P, T, D])
                junk = sbuf(c2, "m_junk", [P, D])
                ss = sbuf(c2, "m_ss", [P, MT + T])
                ps_t = [psum(c2, f"m_tp{i}") for i in range(2)]
                ps = [psum(c2, f"m_proj{i}") for i in range(4)]
                s_ss, s_ms, s_sq, s_rinv, s_xn, s_tp, s_thi, s_tlo, s_ps, s_out = (
                    sem("m_" + n) for n in ("ss", "ms", "sq", "rinv", "xn", "tp", "thi", "tlo", "ps", "out"))
                s_raw = [sem(f"m_raw{b}") for b in range(2)]
                s_hi, s_split = sem("m_hi"), sem("m_split")
                tiles = [(mem_sb[:, t, :], mem_sb[:, t, :]) for t in range(MT)] + [
                    (x_sb[:, t, :], xn[:, t, :]) for t in range(T)]
                groups = [("k", h) for h in range(MX_HEADS)] + [("v", t) for t in range(MT)] + [
                    ("q", h) for h in range(MX_HEADS)]
                first_piece = {"k": 0, "v": 2, "q": 4}
                PIECES_M = 8
                block = c2.enter_context(nc.Block())

                def piece_view(n):
                    if n < 6:
                        name = ("w_mk", "w_mv", "w_mq")[n // 2]
                        return a[name].rearrange("l (p k) n -> p (l k n)", k=KD)[:, n % 2 * HALF_W:
                                                                                 (n % 2 + 1) * HALF_W]
                    return a["w_mo_pieces"][n - 6]

                @block.sync
                def _(sp):
                    for n in range(PIECES_M):
                        if n >= 2:
                            sp.wait_ge(s_split, n - 1)
                        sp.dma_start(w_raw[n % 2][:], piece_view(n)).then_inc(s_raw[n % 2], 16)

                def hi_part(act, n):
                    act.wait_ge(s_raw[n % 2], 16 * (n // 2 + 1))
                    if n >= SLOTS_W:
                        act.wait_ge(s_ps, MX_HEADS if n < 6 else MX_HEADS + MT)
                    nc.scalar.copy(w_hi[n % 4][:], w_raw[n % 2][:]).then_inc(s_hi, 1)

                def lo_part(dve, n):
                    dve.wait_ge(s_hi, n + 1)
                    nc.vector.tensor_tensor(w_lo[n % 4][:], w_raw[n % 2][:], w_hi[n % 4][:].bitcast(F32),
                                            ALU.subtract).then_inc(s_split, 1)

                @block.tensor
                def _(pe):
                    def turn(lo_tile, n_tiles, base, ks):
                        for k in ks:
                            g = base + k
                            if g >= 2:
                                pe.wait_ge(s_tlo, g - 1)
                            for t in range(n_tiles):
                                if k == 0:
                                    pe.wait_ge(s_xn, lo_tile + t + 1)
                                last = nc.tensor.transpose(ps_t[g % 2][:, t * P:(t + 1) * P],
                                                           tiles[lo_tile + t][1][:, k::KD], ident[:])
                            last.then_inc(s_tp, 1)

                    turn(0, MT, 0, range(KD))
                    for g, (kind, h) in enumerate(groups):
                        if h == 0:
                            pe.wait_ge(s_tlo, 2 * KD if kind == "q" else KD)
                            pe.wait_ge(s_split, first_piece[kind] + 2)
                        if g >= 4:
                            pe.wait_ge(s_out, g - 3)
                        for k in range(KD):
                            at, kk = (first_piece[kind] + k // 4) % SLOTS_W, k % 4
                            for n in range(3):
                                w = (w_lo if n == 1 else w_hi)[at]
                                xp = (h_parts if kind == "q" else m_parts)[n // 2]
                                ends = {"start": k == 0 and n == 0, "stop": k == KD - 1 and n == 2}
                                if kind == "v":
                                    last = nc.tensor.matmul(ps[g % 4][:], xp[:, k, h * P:(h + 1) * P],
                                                            w[:, kk * BW:(kk + 1) * BW], **ends)
                                else:
                                    o = kk * BW + h * P
                                    last = nc.tensor.matmul(ps[g % 4][:, 0:N if kind == "q" else MEM],
                                                            w[:, o:o + P], xp[:, k, :], **ends)
                        last.then_inc(s_ps, 1)
                        if 1 <= g <= 4:
                            turn(MT, T, KD, range(2 * (g - 1), 2 * g))

                def turned(base):
                    return (m_parts, gain_memn, MEM) if base == 0 else (h_parts, gain_mem, N)

                def turned_hi(act, base, ks):
                    parts, gain, w = turned(base)
                    for k in ks:
                        act.wait_ge(s_tp, base + k + 1)
                        nc.scalar.activation(parts[0][:, k, :], ps_t[k % 2][:, 0:w], ACT.Copy,
                                             scale=gain[:, k:k + 1]).then_inc(s_thi, 1)

                @block.scalar
                def _(act):
                    for st in range(MT + T + 1):
                        if st < MT + T:
                            if st:
                                act.wait_ge(s_ss, st)
                            nc.scalar.activation(junk[:], tiles[st][0], ACT.Square, accum_out=ss[:, st:st + 1]
                                                 ).then_inc(s_ss, 1)
                        if st:
                            act.wait_ge(s_ms, st)
                            nc.scalar.activation(ss[:, st - 1:st], ss[:, st - 1:st], ACT.Sqrt).then_inc(s_sq, 1)
                        if st == MT:
                            hi_part(act, 0)
                            hi_part(act, 1)
                            turned_hi(act, 0, range(KD))
                    hi_part(act, 2)
                    hi_part(act, 3)
                    turned_hi(act, KD, range(6))
                    hi_part(act, 4)
                    hi_part(act, 5)
                    turned_hi(act, KD, range(6, KD))
                    hi_part(act, 6)
                    hi_part(act, 7)

                @block.vector
                def _(dve):
                    def turned_lo(base, ks):
                        parts, gain, w = turned(base)
                        for k in ks:
                            dve.wait_ge(s_thi, base + k + 1)
                            nc.vector.scalar_tensor_tensor(parts[1][:, k, :], ps_t[k % 2][:, 0:w], gain[:, k:k + 1],
                                                           parts[0][:, k, :].bitcast(F32),
                                                           ALU.mult, ALU.subtract).then_inc(s_tlo, 1)

                    def out(g):
                        kind, h = groups[g]
                        dve.wait_ge(s_ps, g + 1)
                        nc.vector.tensor_copy({"q": qT, "k": kT, "v": v}[kind][:, h, :],
                                              ps[g % 4][:, 0:MEM if kind == "k" else N]).then_inc(s_out, 1)

                    for st in range(MT + T + 1):
                        if st < MT + T:
                            dve.wait_ge(s_ss, st + 1)
                            nc.vector.tensor_scalar(ss[:, st:st + 1], ss[:, st:st + 1], 1.0 / D, NORM_EPS,
                                                    ALU.mult, ALU.add).then_inc(s_ms, 1)
                        if st:
                            t = st - 1
                            dve.wait_ge(s_sq, st)
                            nc.vector.reciprocal(ss[:, t:st], ss[:, t:st]).then_inc(s_rinv, 1)
                            dve.wait_ge(s_rinv, st)
                            nc.vector.tensor_scalar(tiles[t][1], tiles[t][0], ss[:, t:st], None, ALU.mult
                                                    ).then_inc(s_xn, 1)
                        if st == MT:
                            lo_part(dve, 0)
                            lo_part(dve, 1)
                            turned_lo(0, range(KD))
                    lo_part(dve, 2)
                    lo_part(dve, 3)
                    turned_lo(KD, range(0, 2))
                    out(0)
                    out(1)
                    turned_lo(KD, range(2, 4))
                    out(2)
                    turned_lo(KD, range(4, 6))
                    lo_part(dve, 4)
                    out(3)
                    lo_part(dve, 5)
                    turned_lo(KD, range(6, KD))
                    out(4)
                    out(5)
                    lo_part(dve, 6)
                    lo_part(dve, 7)
                    for g in range(MX_HEADS + MT, len(groups)):
                        out(g)

            o_parts = [sbuf(c, "m_oT_" + n, [P, MX_HEADS, N], F32R) for n in ("hi", "lo")]
            pr = [sbuf(c, f"m_p{i}", [P, MEM]) for i in range(3)]
            pT = [sbuf(c, f"m_pT{i}", [P, MEM // P, N]) for i in range(2)]
            U = MX_HEADS * T
            nmax, rsum = sbuf(c, "m_nmax", [P, U]), sbuf(c, "m_rsum", [P, U])
            SC = float(P) ** -0.5
            with ExitStack() as c2:
                ps_s = [psum(c2, f"m_s{i}") for i in range(2)]
                ps_t = [psum(c2, f"m_t{i}") for i in range(2 * MT)]
                ps_o = [psum(c2, f"m_o{i}") for i in range(2)]
                s_s, s_mx, s_exp, s_nrm, s_t, s_pt, s_o, s_ohi, s_ot, s_dve, s_x = (
                    sem("m_" + n) for n in ("s", "mx", "exp", "nrm", "t", "pt", "o", "ohi", "ot", "dve", "x"))
                block = c2.enter_context(nc.Block())

                @block.tensor
                def _(pe):
                    for st in range(U + 3):
                        if st < U:
                            h, t = divmod(st, T)
                            if st >= 2:
                                pe.wait_ge(s_exp, st - 1)
                            nc.tensor.matmul(ps_s[st % 2][:, 0:MEM], qT[:, h, t * P:(t + 1) * P], kT[:, h, :],
                                             start=True, stop=True).then_inc(s_s, 1)
                        if 0 <= st - 2 < U:
                            u = st - 2
                            h, t = divmod(u, T)
                            pe.wait_ge(s_nrm, u + 1)
                            if t == 0 and h >= 2:
                                pe.wait_ge(s_pt, MT * (h - 1))
                            for m in range(MT):
                                last = nc.tensor.transpose(ps_t[MT * (h % 2) + m][:, t * P:(t + 1) * P],
                                                           pr[u % 3][:, m * P:(m + 1) * P], ident[:])
                            last.then_inc(s_t, 1)
                        if st - 3 >= 0 and (st - 3) % T == T - 1:
                            h = (st - 3) // T
                            pe.wait_ge(s_pt, MT * (h + 1))
                            if h >= 2:
                                pe.wait_ge(s_ot, h - 1)
                            for m in range(MT):
                                last = nc.tensor.matmul(ps_o[h % 2][:], v[:, m, h * P:(h + 1) * P],
                                                        pT[h % 2][:, m, :], start=(m == 0), stop=(m == MT - 1))
                            last.then_inc(s_o, 1)
                    pe.wait_ge(s_ot, MX_HEADS)
                    for g in range(2 * T):
                        t, h = divmod(g, 2)
                        if g >= 4:
                            pe.wait_ge(s_x, g - 3)
                        for k in range(KB):
                            for n in range(3):
                                w = (wo_lo if n == 1 else wo_hi)[k // 2]
                                at = k % 2 * D + h * BW
                                last = nc.tensor.matmul(ps_t[g % 4][:], o_parts[n // 2][:, k, t * P:(t + 1) * P],
                                                        w[:, at:at + BW], start=(k == 0 and n == 0),
                                                        stop=(k == KB - 1 and n == 2))
                        last.then_inc(s_o, 1)

                @block.scalar
                def _(act):
                    def o_hi(h):
                        act.wait_ge(s_o, h + 1)
                        nc.scalar.copy(o_parts[0][:, h, :], ps_o[h % 2][:]).then_inc(s_ohi, 1)

                    for u in range(U):
                        act.wait_ge(s_mx, u + 1)
                        if u >= 3:
                            act.wait_ge(s_t, u - 2)
                        nc.scalar.activation(pr[u % 3][:], ps_s[u % 2][:, 0:MEM], ACT.Exp, scale=SC,
                                             bias=nmax[:, u:u + 1], accum_out=rsum[:, u:u + 1]
                                             ).then_inc(s_exp, 1)
                        if u % T == T - 1 and u >= 2 * T - 1:
                            o_hi(u // T - 1)
                    o_hi(MX_HEADS - 1)

                @block.vector
                def _(dve):
                    do = Steps(dve, s_dve)

                    def o_lo(h):
                        dve.wait_ge(s_ohi, h + 1)
                        nc.vector.tensor_tensor(o_parts[1][:, h, :], ps_o[h % 2][:],
                                                o_parts[0][:, h, :].bitcast(F32), ALU.subtract).then_inc(s_ot, 1)

                    for st in range(U + 4):
                        if st < U:
                            dve.wait_ge(s_s, st + 1)
                            do.after(nc.vector.reduce_max(nmax[:, st:st + 1], ps_s[st % 2][:, 0:MEM], AX_X))
                            nc.vector.tensor_scalar(nmax[:, st:st + 1], nmax[:, st:st + 1], -SC, None,
                                                    ALU.mult).then_inc(s_mx, 1)
                        if 0 <= st - 1 < U:
                            u = st - 1
                            dve.wait_ge(s_exp, u + 1)
                            do.after(nc.vector.reciprocal(rsum[:, u:u + 1], rsum[:, u:u + 1]))
                            nc.vector.tensor_scalar(pr[u % 3][:], pr[u % 3][:], rsum[:, u:u + 1], None,
                                                    ALU.mult).then_inc(s_nrm, 1)
                        if st - 2 >= 0 and st - 2 < U and (st - 2) % T == T - 1:
                            h = (st - 2) // T
                            dve.wait_ge(s_t, h * T + T)
                            if h >= 2:
                                dve.wait_ge(s_o, h - 1)
                            for m in range(MT):
                                nc.vector.tensor_copy(pT[h % 2][:, m, :], ps_t[MT * (h % 2) + m][:]
                                                      ).then_inc(s_pt, 1)
                        if st - 3 >= 0 and (st - 3) % T == T - 1:
                            h = (st - 3) // T
                            if h:
                                o_lo(h - 1)
                    o_lo(MX_HEADS - 1)
                    for g in range(2 * T):
                        t, h = divmod(g, 2)
                        dve.wait_ge(s_o, MX_HEADS + g + 1)
                        xs = x_sb[:, t, h * BW:(h + 1) * BW]
                        nc.vector.tensor_tensor(xs, ps_t[g % 4][:], xs, ALU.add).then_inc(s_x, 1)

        PIECES, PW = 6, KD * FF // 2
        raw = [sbuf(stack, f"w_raw{j}", [P, PW]) for j in range(PIECES)]
        s_raw = [sem(f"e_raw{j}") for j in range(PIECES)]
        s_scattered = sem("scattered")
        w13v = [a[n].rearrange("l e (p k) f -> (l e) p (k f)", k=KD) for n in ("w1", "w1", "w3", "w3")]
        w2v = a["w2"].rearrange("l e (p k) d -> (l e) p (k d)", k=KF)

        w_hi, w_lo = ([sbuf(stack, f"w_{n}{j}", [P, PW], F32R) for j in range(4)] for n in ("hi", "lo"))
        s_hi, s_split = ([sem(f"e_{n}{j}") for j in range(PIECES)] for n in ("hi", "split"))

        def hi_of(act, j, q):
            act.wait_ge(s_raw[j], q * 16 + 16)
            nc.scalar.copy(w_hi[j][:], raw[j][:]).then_inc(s_hi[j], 1)

        def lo_of(dve, j, q):
            dve.wait_ge(s_hi[j], q + 1)
            nc.vector.tensor_tensor(w_lo[j][:], raw[j][:], w_hi[j][:].bitcast(F32), ALU.subtract
                                    ).then_inc(s_split[j], 1)

        def load_piece(sp, j, e):
            src, h = (w13v[j], j % 2) if j < 4 else (w2v, j - 4)
            sp.dma_start(raw[j][:], src[bass.ds(e, 1), :, h * PW:(h + 1) * PW].rearrange("o p f -> p (o f)")
                         ).then_inc(s_raw[j], 16)

        idx = sbuf(stack, "idx", [P, EXPERTS], U32)
        wsel = sbuf(stack, "wsel", [P, 2, T])
        asg = sbuf(stack, "asg", [P, 2, T], I32)
        destu = sbuf(stack, "destu", [P, 2, T], U32)
        xs = [sbuf(stack, f"xs{b}", [P, D]) for b in range(2)]
        rc = sbuf(stack, "rc", [P, ROUTE_CONSTS])
        cnt = sbuf(stack, "cnt", [P, EXPERTS])
        act_b, rank = sbuf(stack, "act_b", [P, EXPERTS, 4]), sbuf(stack, "rank", [P, P])
        jobs, jobsi = sbuf(stack, "jobs", [P, 4]), sbuf(stack, "jobsi", [P, 4], I32)
        with ExitStack() as c:
            h3T = sbuf(c, "h3T", [P, KD, N])
            xn = sbuf(c, "xn", [P, T, D])
            ffn_gain = sbuf(c, "ffn_gain", [P, D])

            def load_gain(sp):
                sp.dma_start(ffn_gain[:], bass.AP(a["rows"].tensor, ROWS, [[0, P], [1, D]])).then_inc(s_start, 16)
                for j in range(PIECES):
                    load_piece(sp, j, 0)
                sp.wait_ge(s_start, 64)

            load_gain.ready = 64
            load_gain.tiles = None
            load_gain.beside = None
            rms_transposed(c, "rf", x_sb, T, None, h3T, first=load_gain, keep=xn,
                           gain_row=ffn_gain[:])
            w_rt = sbuf(c, "w_rt", [P, KD, LOGITS])
            ones = rc[:, P:2 * P]
            iota = rc[:, 2 * P:2 * P + EXPERTS]
            r0 = 2 * P + EXPERTS
            blk_thr, blk_at, blk_e, slot_no = (rc[:, r0 + P * i:r0 + P * (i + 1)] for i in range(4))
            rank1 = rc[:, r0 + 4 * P:r0 + 4 * P + 1]
            fill = sbuf(c, "fill", [P, EXPERTS * LIST // P], I32)
            before_ones = sbuf(c, "before_ones", [P, 2 * P], F32R)
            hot2 = sbuf(c, "hot2", [P, T, EXPERTS], F32R)
            lg = sbuf(c, "lg", [P, T, LOGITS])
            gpad = sbuf(c, "gpad", [P, T, PER_GROUP])
            sel = sbuf(c, "sel", [P, T, PER_GROUP])
            top = sbuf(c, "top", [P, 2, T, PER_GROUP])
            topi = sbuf(c, "topi", [P, 2, T, PER_GROUP], U32)
            topf = sbuf(c, "topf", [P, 2, T, PER_GROUP])
            oh = sbuf(c, "oh", [P, T, GROUPS])
            junk = sbuf(c, "r_junk", [P, 2, T, EXPERTS])
            sm = sbuf(c, "r_small", [P, 8, T])
            e_of = sbuf(c, "e_of", [P, 2, T])
            hot = sbuf(c, "hot", [P, 2, T, EXPERTS])
            pos = sbuf(c, "pos", [P, T, EXPERTS])
            dest = sbuf(c, "dest", [P, 2, T])
            idf = sbuf(c, "idf", [P, EXPERTS])
            asg_no = sbuf(c, "asg_no", [P, 2, T])
            hot_id = sbuf(c, "hot_id", [P, 2, T, EXPERTS], F32R)
            at_slot = sbuf(c, "at_slot", [P, 2 * T, P], F32R)
            lrow = sbuf(c, "lrow", [LOGITS, N])
            ps_r, ps_l, ps_p, ps_c, ps_i = (psum(c, "r_" + n) for n in ("r", "l", "p", "c", "i"))
            s_lrow, s_lcopy = sem("r_lrow"), sem("r_lcopy")
            s_w, s_c, s_xw, s_l, s_dve, s_gm, s_ex, s_d01, s_e2, s_hot, s_pc, s_at, s_dest, s_fl, s_fw, s_it = (
                sem("r_" + n) for n in ("w", "const", "xw", "l", "dve", "gmax", "gexp", "d01", "e2", "hot", "pc",
                                        "at", "dest", "fill", "fillw", "ids"))
            block = c.enter_context(nc.Block())

            @block.sync
            def _(sp):
                sp.dma_start(w_rt[:], a["w_route"].rearrange("(p k) n -> p k n", k=KD)).then_inc(s_w, 16)
                sp.dma_start(rc[:], a["route_consts"]).then_inc(s_c, 16)
                sp.dma_start(asg[:], a["asg_ids"]).then_inc(s_c, 16)
                for ch in range(2):
                    sp.dma_start(xn_dram[ch * N:(ch + 1) * N, :].rearrange("(t p) d -> p t d", p=P), xn[:]
                                 ).then_inc(s_xw, 16)
                for j in range(4):
                    sp.wait_ge(s_split[j], 1)
                    load_piece(sp, j, 1)
                sp.wait_ge(s_xw, 32)

            @block.gpsimd
            def _(pool):
                nc.gpsimd.memset(fill[:], NO_SLOT).then_inc(s_fl, 1)
                pool.wait_ge(s_fl, 1)
                pool.dma_start(list_dram.rearrange("(q s) o -> q (s o)", q=P), fill[:]).then_inc(s_fw, 16)
                pool.wait_ge(s_fw, 16)
                for b in range(2):
                    nc.gpsimd.memset(xs[b][:], 0.0).then_inc(s_fl, 1)
                pool.wait_ge(s_fl, 3)

            @block.tensor
            def _(pe):
                pe.wait_ge(s_w, 16)
                for k in range(KD):
                    last = nc.tensor.matmul(ps_r[0:LOGITS, :], w_rt[:, k, :], h3T[:, k, :],
                                            start=(k == 0), stop=(k == KD - 1))
                last.then_inc(s_lrow, 1)
                pe.wait_ge(s_lcopy, 1)
                for t in range(T):
                    last = nc.tensor.transpose(ps_l[:, t * LOGITS:(t + 1) * LOGITS], lrow[:, t * P:(t + 1) * P],
                                               ident[0:LOGITS, 0:LOGITS])
                last.then_inc(s_l, 1)
                pe.wait_ge(s_c, 32)
                pe.wait_ge(s_hot, 1)
                for t in range(T):
                    o = ps_p[:, t * EXPERTS:(t + 1) * EXPERTS]
                    for q in range(t):
                        nc.tensor.matmul(o, before_ones[:, P:2 * P], hot2[:, q, :], start=(q == 0), stop=False)
                    nc.tensor.matmul(o, before_ones[:, 0:P], hot2[:, t, :], start=(t == 0), stop=True)
                for t in range(T):
                    last = nc.tensor.matmul(ps_c[:, 0:EXPERTS], before_ones[:, P:2 * P], hot2[:, t, :],
                                            start=(t == 0), stop=(t == T - 1))
                last.then_inc(s_pc, 1)
                for n in range(2 * T):
                    ch, t = divmod(n, T)
                    pe.wait_ge(s_at, n + 1)
                    last = nc.tensor.matmul(ps_i[:, 0:EXPERTS], at_slot[:, n, :], hot_id[:, ch, t, :],
                                            start=(n == 0), stop=(n == 2 * T - 1))
                last.then_inc(s_it, 1)

            @block.scalar
            def _(act):
                for j in range(4):
                    hi_of(act, j, 0)
                act.wait_ge(s_lrow, 1)
                nc.scalar.copy(lrow[:], ps_r[0:LOGITS, :]).then_inc(s_lcopy, 1)
                act.wait_ge(s_gm, 1)
                for t in range(T):
                    nc.scalar.activation(junk[:, 0, t, 0:GROUPS], lg[:, t, 0:GROUPS], ACT.Exp,
                                         bias=sm[:, 0, t:t + 1], accum_out=sm[:, 1, t:t + 1]).then_inc(s_ex, 1)
                act.wait_ge(s_d01, 1)
                nc.scalar.activation(sm[:, 3, :], sm[:, 2, :], ACT.Exp).then_inc(s_e2, 1)

            @block.vector
            def _(dve):
                do = Steps(dve, s_dve)
                for j in range(4):
                    lo_of(dve, j, 0)
                do.after(nc.vector.memset(gpad[:], -3e38))
                dve.wait_ge(s_c, 32)
                do.after(nc.vector.tensor_copy(before_ones[:], rc[:, 0:2 * P]))
                do.after(nc.vector.tensor_copy(asg_no[:], asg[:]))
                do.after(nc.vector.tensor_scalar(asg_no[:], asg_no[:], 1.0, None, ALU.add))
                dve.wait_ge(s_l, 1)
                bias = router_bias.unsqueeze(1).to_broadcast([P, T, LOGITS])
                do.after(nc.vector.tensor_tensor(lg[:], ps_l[:, 0:T * LOGITS].rearrange("p (t n) -> p t n", t=T),
                                                 bias, ALU.add))
                do.after(nc.vector.tensor_copy(gpad[:, :, 0:GROUPS], lg[:, :, 0:GROUPS]))
                for t in range(T):
                    do.after(nc.vector.max(top[:, 0, t, :], gpad[:, t, :]))
                    do.after(nc.vector.max_index(topi[:, 0, t, :], top[:, 0, t, :], gpad[:, t, :]))
                nc.vector.tensor_scalar(sm[:, 0, :], top[:, 0, :, 0], -1.0, None, ALU.mult).then_inc(s_gm, 1)
                do.after(nc.vector.tensor_copy(topf[:, 0, :, :], topi[:, 0, :, :]))
                do.after(nc.vector.tensor_tensor(oh[:], iota[:, 0:GROUPS].unsqueeze(1).to_broadcast([P, T, GROUPS]),
                                                 topf[:, 0, :, 0:1].to_broadcast([P, T, GROUPS]), ALU.is_equal))
                prod = junk[:, 1, :, :].rearrange("p t (g e) -> p t g e", g=GROUPS)
                do.after(nc.vector.tensor_tensor(prod, lg[:, :, GROUPS:LOGITS].rearrange(
                    "p t (g e) -> p t g e", g=GROUPS), oh[:].unsqueeze(3).to_broadcast(
                    [P, T, GROUPS, PER_GROUP]), ALU.mult))
                do.after(nc.vector.tensor_reduce(sel[:], prod.rearrange("p t g e -> p t e g"), AX_X, ALU.add))
                for t in range(T):
                    do.after(nc.vector.max(top[:, 1, t, :], sel[:, t, :]))
                    do.after(nc.vector.max_index(topi[:, 1, t, :], top[:, 1, t, :], sel[:, t, :]))
                do.after(nc.vector.tensor_copy(topf[:, 1, :, :], topi[:, 1, :, :]))
                nc.vector.tensor_tensor(sm[:, 2, :], top[:, 1, :, 1], top[:, 1, :, 0], ALU.subtract
                                        ).then_inc(s_d01, 1)
                for ch in range(2):
                    do.after(nc.vector.scalar_tensor_tensor(e_of[:, ch, :], topf[:, 0, :, 0], float(PER_GROUP),
                                                            topf[:, 1, :, ch], ALU.mult, ALU.add))
                    do.after(nc.vector.tensor_tensor(hot[:, ch, :, :],
                                                     iota.unsqueeze(1).to_broadcast([P, T, EXPERTS]),
                                                     e_of[:, ch, :].unsqueeze(2).to_broadcast([P, T, EXPERTS]),
                                                     ALU.is_equal))
                nc.vector.tensor_tensor(hot2[:], hot[:, 0, :, :], hot[:, 1, :, :], ALU.add
                                        ).then_inc(s_hot, 1)
                do.after(nc.vector.tensor_tensor(hot_id[:], hot[:],
                                                 asg_no[:].unsqueeze(3).to_broadcast([P, 2, T, EXPERTS]),
                                                 ALU.mult))
                dve.wait_ge(s_e2, 1)
                dve.wait_ge(s_ex, T)
                do.after(nc.vector.tensor_scalar(sm[:, 4, :], sm[:, 3, :], 1.0, None, ALU.add))
                do.after(nc.vector.tensor_tensor(sm[:, 4, :], sm[:, 4, :], sm[:, 1, :], ALU.mult))
                do.after(nc.vector.reciprocal(sm[:, 4, :], sm[:, 4, :]))
                do.after(nc.vector.tensor_scalar(wsel[:, 0, :], sm[:, 4, :], 0.5, None, ALU.mult))
                do.after(nc.vector.tensor_tensor(wsel[:, 1, :], wsel[:, 0, :], sm[:, 3, :], ALU.mult))
                dve.wait_ge(s_pc, 1)
                do.after(nc.vector.tensor_copy(pos[:], ps_p[:, 0:T * EXPERTS].rearrange("p (t e) -> p t e", t=T)))
                do.after(nc.vector.tensor_copy(cnt[:], ps_c[:, 0:EXPERTS]))
                for ch in range(2):
                    do.after(nc.vector.tensor_tensor(junk[:, ch, :, :], hot[:, ch, :, :], pos[:], ALU.mult))
                    do.after(nc.vector.tensor_reduce(dest[:, ch, :], junk[:, ch, :, :], AX_X, ALU.add))
                for n in range(2 * T):
                    ch, t = divmod(n, T)
                    nc.vector.tensor_scalar(at_slot[:, n, :], slot_no, dest[:, ch, t:t + 1], None, ALU.is_equal
                                            ).then_inc(s_at, 1)
                dve.wait_ge(s_at, 2 * T)
                do.after(nc.vector.scalar_tensor_tensor(dest[:], e_of[:], float(LIST), dest[:], ALU.mult, ALU.add))
                nc.vector.tensor_copy(destu[:], dest[:]).then_inc(s_dest, 1)
                dve.wait_ge(s_it, 1)
                do.after(nc.vector.tensor_scalar(idf[:], ps_i[:, 0:EXPERTS], 0.0, float(NO_SLOT + 1),
                                                 ALU.is_equal, ALU.mult))
                do.after(nc.vector.scalar_tensor_tensor(idf[:], ps_i[:, 0:EXPERTS], -1.0, idf[:],
                                                        ALU.add, ALU.add))
                do.after(nc.vector.tensor_copy(idx[:], idf[:]))

        with ExitStack() as c:
            w_hi += [sbuf(c, f"w_hi{j}", [P, PW], F32R) for j in (4, 5)]
            w_lo += [sbuf(c, f"w_lo{j}", [P, PW], F32R) for j in (4, 5)]
            ibx, iby = ([sbuf(c, f"ib{n}{b}", [P, 1], U32) for b in range(2)] for n in "xy")
            xT_hi, xT_lo = (sbuf(c, "xT_" + n, [P, KD * P], F32R) for n in ("hi", "lo"))
            hT_hi, hT_lo = (sbuf(c, "hidT_" + n, [P, KF * P], F32R) for n in ("hi", "lo"))
            tn = sbuf(c, "tn", [P, FF])
            hd = sbuf(c, "hd", [P, FF])
            yo = [sbuf(c, f"yo{b}", [P, D]) for b in range(2)]
            ps_x = psum(c, "e_x", (P, KD * P))
            ps_1, ps_3, ps_h = psum(c, "e_1"), psum(c, "e_3"), psum(c, "e_h")
            ps_y = psum(c, "e_y", (P, D))

            s_ibx, s_iby, s_xs, s_ys, s_stored = (
                [sem(f"e_{n}{b}") for b in range(2)] for n in ("ibx", "iby", "xs", "ys", "stored"))
            s_tx, s_xhi, s_xlo, s_th, s_hm, s_hd, s_ht, s_hhi, s_hlo, s_yo = (
                sem("e_" + n) for n in ("tx", "xhi", "xlo", "tanh", "hm", "hd", "ht", "hhi", "hlo", "yo"))
            s_used = [sem(f"e_used{j}") for j in range(PIECES)]
            s_lst, s_jobs, s_jobs_out, s_dve = (sem("e_" + n) for n in ("list", "jobs", "jobs_out", "dve"))
            s_turn = sem("e_turn")
            NI = EXPERTS // 2
            last_row = nc.gpsimd.alloc_register("last_row")

            class Job:

                def __init__(self, q, b, i, tx):
                    self.q, self.b, self.i, self.tx = q, b, i, tx

            def job(s, i, odd, shift):
                at = (1 if odd else 2) + shift
                return Job(s + shift, at % 2, i + at // 2, s + (shift + 1))

            def extra(r):
                return Job(r + EXPERTS, 0, r + NI, r + (EXPERTS + 2))

            def wait(eng, q, n):
                if not (isinstance(n, int) and n <= 0):
                    eng.wait_ge(q, n)

            def load(sp, j, e, q):
                sp.wait_ge(s_split[j], q)
                load_piece(sp, j, e)

            def hi_part(act, j, q):
                act.wait_ge(s_used[j], q + 1)
                hi_of(act, j, q)

            lo_part = lo_of

            def fetch(pool, b, n, tx, rows=FIRST):
                wait(pool, s_ibx[b], n)
                pool.wait_ge(s_tx, tx)
                pool.sem_inc(s_turn, 1)
                pool.indirect_dma_start(xs[b][0:rows, :], None, xn_dram,
                                        bass.IndirectOffsetOnAxis(ibx[b][0:rows, :], 0),
                                        bounds_check=last_row, oob_is_err=False).then_inc(s_xs[b], 16)

            def store(pool, jb, listed=True, rows=FIRST):
                b = jb.b
                if listed:
                    pool.wait_ge(s_iby[b], jb.i + 1)
                pool.wait_ge(s_yo, jb.q + 1)
                pool.sem_inc(s_turn, 1)
                pool.indirect_dma_start(ys_dram, bass.IndirectOffsetOnAxis(iby[b][0:rows, :], 0),
                                        yo[b][0:rows, :], None,
                                        bounds_check=last_row, oob_is_err=False).then_inc(s_ys[b], 16)
                pool.wait_ge(s_ys[b], jb.i * 16 + 16)
                pool.sem_inc(s_stored[b], 1)

            def turn_rows(pe, jb):
                pe.wait_ge(s_xs[jb.b], jb.i * 16 + 16)
                wait(pe, s_xlo, jb.q)
                for k in range(KD):
                    last = nc.tensor.transpose(ps_x[:, k * P:(k + 1) * P], xs[jb.b][:, k::KD], ident[:])
                last.then_inc(s_tx, 1)

            def product(o, x_parts, j, k, w_cols, start, stop):
                x_hi, x_lo = x_parts
                for n, (xp, wp) in enumerate(((x_hi, w_hi[j]), (x_hi, w_lo[j]), (x_lo, w_hi[j]))):
                    last = nc.tensor.matmul(o, xp[:, k * P:(k + 1) * P], wp[:, w_cols:w_cols + FF],
                                            start=start and n == 0, stop=stop and n == 2)
                return last

            def up(pe, q, pieces):
                if 0 in pieces:
                    pe.wait_ge(s_xlo, q + 1)
                    wait(pe, s_hd, q)
                for j in pieces:
                    pe.wait_ge(s_split[j], q + 1)
                    half = j % 2
                    for k in range(4):
                        last = product((ps_1 if j < 2 else ps_3)[:], (xT_hi, xT_lo), j, half * 4 + k, k * FF,
                                       half == 0 and k == 0, half == 1 and k == 3)
                    last.then_inc(s_used[j], 1)

            def turn_hidden(pe, q):
                pe.wait_ge(s_hd, q + 1)
                wait(pe, s_hlo, q)
                for k in range(KF):
                    last = nc.tensor.transpose(ps_h[:, k * P:(k + 1) * P], hd[:, k::KF], ident[:])
                last.then_inc(s_ht, 1)

            def down(pe, q):
                pe.wait_ge(s_hlo, q + 1)
                wait(pe, s_yo, q)
                for j in (4, 5):
                    pe.wait_ge(s_split[j], q + 1)
                    for h in range(2):
                        for k in range(2):
                            last = product(ps_y[:, h * FF:(h + 1) * FF], (hT_hi, hT_lo), j, (j - 4) * 2 + k,
                                           k * D + h * FF, j == 4 and k == 0, j == 5 and k == 1)
                    last.then_inc(s_used[j], 1)

            def x_hi(act, q):
                act.wait_ge(s_tx, q + 3)
                nc.scalar.copy(xT_hi[:], ps_x[:]).then_inc(s_xhi, 1)

            def tanh_step(act, q):
                act.wait_ge(s_used[1], q + 2)
                wait(act, s_hd, q)
                nc.scalar.activation(tn[:], ps_1[:], ACT.Tanh, scale=0.5).then_inc(s_th, 1)

            def h_hi(act, q):
                act.wait_ge(s_ht, q + 1)
                nc.scalar.copy(hT_hi[:], ps_h[:]).then_inc(s_hhi, 1)

            def y_copy(act, jb):
                act.wait_ge(s_used[5], jb.q + 2)
                act.wait_ge(s_stored[jb.b], jb.i + 1)
                nc.scalar.copy(yo[jb.b][:], ps_y[:]).then_inc(s_yo, 1)

            def x_lo(dve, q):
                dve.wait_ge(s_xhi, q + 1)
                nc.vector.tensor_tensor(xT_lo[:], ps_x[:], xT_hi[:].bitcast(F32), ALU.subtract).then_inc(s_xlo, 1)

            def silu_step(dve, q):
                dve.wait_ge(s_th, q + 1)
                nc.vector.scalar_tensor_tensor(tn[:], tn[:], 1.0, ps_1[:], ALU.add, ALU.mult).then_inc(s_hm, 1)

            def hidden(dve, q):
                dve.wait_ge(s_hm, q + 1)
                dve.wait_ge(s_used[3], q + 2)
                wait(dve, s_ht, q)
                nc.vector.tensor_tensor(hd[:], tn[:], ps_3[:], ALU.mult).then_inc(s_hd, 1)

            def h_lo(dve, q):
                dve.wait_ge(s_hhi, q + 1)
                nc.vector.tensor_tensor(hT_lo[:], ps_h[:], hT_hi[:].bitcast(F32), ALU.subtract).then_inc(s_hlo, 1)

            def pick_x(dve, e, jb):
                dve.wait_ge(s_tx, jb.tx)
                nc.vector.tensor_copy(ibx[jb.b][:], idx[:, bass.ds(e, 1)]).then_inc(s_ibx[jb.b], 1)

            def pick_y(dve, e, jb):
                dve.wait_ge(s_stored[jb.b], jb.i + 1)
                nc.vector.tensor_copy(iby[jb.b][:], idx[:, bass.ds(e, 1)]).then_inc(s_iby[jb.b], 1)

            def pool_step(pool, s, i, odd, rows_in=True):
                if rows_in:
                    jb = job(s, i, odd, 2)
                    fetch(pool, jb.b, jb.i + 1, jb.tx)
                store(pool, job(s, i, odd, -1))

            def pe_step(pe, s, i, odd, rows_in=True):
                up(pe, s, (0, 1, 2))
                turn_hidden(pe, s - 1)
                up(pe, s, (3,))
                if rows_in:
                    turn_rows(pe, job(s, i, odd, 1))
                down(pe, s - 1)

            def act_step(act, s, i, odd, ups=True, last=True):
                if ups:
                    hi_part(act, 0, s + 1)
                    hi_part(act, 1, s + 1)
                tanh_step(act, s)
                if last:
                    h_hi(act, s - 1)
                if ups:
                    hi_part(act, 2, s + 1)
                    x_hi(act, s + 1)
                    hi_part(act, 3, s + 1)
                hi_part(act, 4, s)
                hi_part(act, 5, s)
                if last:
                    y_copy(act, job(s, i, odd, -1))

            def dve_step(dve, s, i, odd, ups=True, last=True, rows_in=True):
                if ups:
                    lo_part(dve, 0, s + 1)
                    lo_part(dve, 1, s + 1)
                silu_step(dve, s)
                if last:
                    h_lo(dve, s - 1)
                if ups:
                    lo_part(dve, 2, s + 1)
                hidden(dve, s)
                if ups:
                    x_lo(dve, s + 1)
                    if rows_in:
                        pick_x(dve, s + 3, job(s, i, odd, 3))
                    lo_part(dve, 3, s + 1)
                lo_part(dve, 4, s)
                lo_part(dve, 5, s)
                pick_y(dve, s, job(s, i, odd, 0))

            def in_pairs(eng, step, passes):
                with eng.Fori(0, passes) as i:
                    step(eng, i * 2 + 1, i, True)
                    step(eng, i * 2 + 2, i, False)

            late = [(EXPERTS - 3, NI - 2, True), (EXPERTS - 2, NI - 2, False), (EXPERTS - 1, NI - 1, True)]
            final_jobs = [Job(EXPERTS - 2, 0, NI - 1, None), Job(EXPERTS - 1, 1, NI - 1, None)]
            block = c.enter_context(nc.Block())

            @block.sync
            def _(sp):
                sp.sem_inc(s_tx, 2)
                for q in (*s_used, *s_stored):
                    sp.sem_inc(q, 1)
                sp.wait_ge(s_jobs, 1)
                sp.dma_start(jobs_dram[0:1, 0:4 * JOBS].rearrange("o (j q) -> (o j) q", q=4),
                             jobsi[0:JOBS, :]).then_inc(s_jobs_out, 16)
                with sp.Fori(2, EXPERTS) as s:
                    for j in range(PIECES):
                        load(sp, j, s if j < 4 else s - 1, s if j < 4 else s - 1)
                for j in (4, 5):
                    load(sp, j, EXPERTS - 1, EXPERTS - 1)
                sp.wait_ge(s_jobs_out, 16)
                n = sp.value_load(jobs_dram[0:1, 2:3], min_val=0, max_val=MAX_EXTRA)
                with sp.If(n > 0):
                    with sp.Fori(0, n) as r:
                        e = sp.value_load(jobs_dram[0:1, bass.ds(r * 4 + 1, 1)], min_val=0, max_val=EXPERTS - 1)
                        for j in range(PIECES):
                            load(sp, j, e, r + EXPERTS)
                    sp.nop()

            @block.gpsimd
            def _(pool):
                pool.reg_mov(last_row, SLOTS - 1)
                fetch(pool, 0, 1, 1)
                fetch(pool, 1, 1, 2)
                for ch in range(2):
                    for t in range(T):
                        pool.indirect_dma_start(list_dram, bass.IndirectOffsetOnAxis(destu[:, ch, t:t + 1], 0),
                                                asg[:, ch, t:t + 1], None).then_inc(s_scattered, 16)
                fetch(pool, 0, 2, 3)
                in_pairs(pool, pool_step, NI - 2)
                pool_step(pool, *late[0])
                pool_step(pool, *late[1], rows_in=False)
                for jb in final_jobs:
                    store(pool, jb)
                pool.wait_ge(s_scattered, 16 * 2 * T)
                pool.wait_ge(s_jobs_out, 16)
                n = pool.value_load(jobs_dram[0:1, 2:3], min_val=0, max_val=MAX_EXTRA)
                with pool.If(n > 0):
                    with pool.Fori(0, n) as r:
                        j = pool.value_load(jobs_dram[0:1, bass.ds(r * 4, 1)], min_val=0, max_val=(EXPERTS * LIST - P) // LIST_UNIT)
                        for ib in (ibx[0], iby[0]):
                            pool.dma_start(ib[:], list_dram[bass.ds(j * LIST_UNIT, P), :].bitcast(U32)).then_inc(s_lst, 16)
                        pool.wait_ge(s_lst, r * 32 + 32)
                        jb = extra(r)
                        fetch(pool, 0, 0, jb.tx, P)
                        store(pool, jb, listed=False, rows=P)
                    pool.nop()

            @block.tensor
            def _(pe):
                turn_rows(pe, Job(0, 0, 0, None))
                up(pe, 0, (0, 1, 2, 3))
                turn_rows(pe, Job(1, 1, 0, None))
                in_pairs(pe, pe_step, NI - 1)
                pe_step(pe, *late[2], rows_in=False)
                turn_hidden(pe, EXPERTS - 1)
                down(pe, EXPERTS - 1)
                pe.wait_ge(s_jobs_out, 16)
                n = pe.value_load(jobs_dram[0:1, 2:3], min_val=0, max_val=MAX_EXTRA)
                with pe.If(n > 0):
                    with pe.Fori(0, n) as r:
                        jb = extra(r)
                        turn_rows(pe, jb)
                        up(pe, jb.q, (0, 1, 2, 3))
                        turn_hidden(pe, jb.q)
                        down(pe, jb.q)
                    pe.nop()

            @block.scalar
            def _(act):
                x_hi(act, 0)
                act_step(act, 0, None, False, last=False)
                in_pairs(act, act_step, NI - 1)
                act_step(act, *late[2], ups=False)
                h_hi(act, EXPERTS - 1)
                y_copy(act, final_jobs[1])
                act.wait_ge(s_jobs_out, 16)
                n = act.value_load(jobs_dram[0:1, 2:3], min_val=0, max_val=MAX_EXTRA)
                with act.If(n > 0):
                    with act.Fori(0, n) as r:
                        jb = extra(r)
                        x_hi(act, jb.q)
                        for j in range(4):
                            hi_part(act, j, jb.q)
                        tanh_step(act, jb.q)
                        hi_part(act, 4, jb.q)
                        hi_part(act, 5, jb.q)
                        h_hi(act, jb.q)
                        y_copy(act, jb)
                    act.nop()

            @block.vector
            def _(dve):
                for b in range(2):
                    pick_x(dve, b, Job(b, b, 0, b + 1))
                do = Steps(dve, s_dve)
                ones = rc[:, P:2 * P]
                thr = blk_thr.rearrange("p (e b) -> p e b", b=4)
                do.after(nc.vector.tensor_tensor(act_b[:], cnt[:].unsqueeze(2).to_broadcast([P, EXPERTS, 4]),
                                                 thr, ALU.is_gt))
                av = act_b[:].rearrange("p e b -> p (e b)")
                do.after(nc.vector.tensor_tensor_scan(rank[:], ones, av, 0.0, ALU.mult, ALU.add))
                do.after(nc.vector.tensor_copy(jobs[:, 2:3], rank[:, P - 1:P]))
                do.after(nc.vector.tensor_tensor(rank[:], rank[:], av, ALU.mult))
                do.after(nc.vector.tensor_scalar(rank[:], rank[:], rank1, None, ALU.is_equal))
                do.after(nc.vector.tensor_tensor_reduce(av, rank[:], blk_at, 1.0, 0.0, ALU.mult, ALU.add,
                                                        jobs[:, 0:1]))
                do.after(nc.vector.tensor_tensor_reduce(av, rank[:], blk_e, 1.0, 0.0, ALU.mult, ALU.add,
                                                        jobs[:, 1:2]))
                do.after(nc.vector.memset(jobs[:, 3:4], 0.0))
                nc.vector.tensor_copy(jobsi[:], jobs[:]).then_inc(s_jobs, 1)
                x_lo(dve, 0)
                pick_x(dve, 2, Job(2, 0, 1, 3))
                dve_step(dve, 0, -1, False, last=False)
                in_pairs(dve, dve_step, NI - 2)
                dve_step(dve, *late[0], rows_in=False)
                dve_step(dve, *late[1], rows_in=False)
                dve_step(dve, *late[2], ups=False)
                h_lo(dve, EXPERTS - 1)
                dve.wait_ge(s_jobs_out, 16)
                n = dve.value_load(jobs_dram[0:1, 2:3], min_val=0, max_val=MAX_EXTRA)
                with dve.If(n > 0):
                    with dve.Fori(0, n) as r:
                        jb = extra(r)
                        x_lo(dve, jb.q)
                        for j in range(4):
                            lo_part(dve, j, jb.q)
                        silu_step(dve, jb.q)
                        hidden(dve, jb.q)
                        lo_part(dve, 4, jb.q)
                        lo_part(dve, 5, jb.q)
                        h_lo(dve, jb.q)
                    dve.nop()

        with ExitStack() as c:
            yk = sbuf(c, "yk", [P, 2, T, D])
            junk = sbuf(c, "f_junk", [P, D])
            ss = sbuf(c, "f_ss", [P, T])
            s_ld = [[sem(f"f_ld{ch}{t}") for t in range(T)] for ch in range(2)]
            s_dve, s_x, s_ss, s_ms, s_sq, s_o, s_done = (sem("f_" + n) for n in ("dve", "x", "ss", "ms", "sq", "o",
                                                                                "done"))
            block = c.enter_context(nc.Block())

            @block.sync
            def _(sp):
                for t in range(T):
                    for ch in range(2):
                        r = ch * N + t * P
                        sp.dma_start(yk[:, ch, t, :], ys_dram[r:r + P, :]).then_inc(s_ld[ch][t], 16)
                for t in range(T):
                    sp.wait_ge(s_o, t + 1)
                    sp.dma_start(out[0, t * P:(t + 1) * P, :], x_sb[:, t, :]).then_inc(s_done, 16)
                sp.wait_ge(s_done, 16 * T)

            @block.scalar
            def _(act):
                for t in range(T):
                    act.wait_ge(s_x, t + 1)
                    nc.scalar.activation(junk[:], x_sb[:, t, :], ACT.Square, accum_out=ss[:, t:t + 1]
                                         ).then_inc(s_ss, 1)
                    act.wait_ge(s_ms, t + 1)
                    nc.scalar.activation(ss[:, t:t + 1], ss[:, t:t + 1], ACT.Sqrt).then_inc(s_sq, 1)

            @block.vector
            def _(dve):
                do = Steps(dve, s_dve)

                def scale(t):
                    dve.wait_ge(s_sq, t + 1)
                    do.after(nc.vector.reciprocal(ss[:, t:t + 1], ss[:, t:t + 1]))
                    nc.vector.scalar_tensor_tensor(x_sb[:, t, :], x_sb[:, t, :], ss[:, t:t + 1], final_gain,
                                                   ALU.mult, ALU.mult).then_inc(s_o, 1)

                for t in range(T):
                    for ch in range(2):
                        dve.wait_ge(s_ld[ch][t], 16)
                        ins = nc.vector.scalar_tensor_tensor(x_sb[:, t, :], yk[:, ch, t, :],
                                                             wsel[:, ch, t:t + 1], x_sb[:, t, :],
                                                             ALU.mult, ALU.add)
                        if ch == 0:
                            do.after(ins)
                    ins.then_inc(s_x, 1)
                    if t:
                        scale(t - 1)
                    dve.wait_ge(s_ss, t + 1)
                    nc.vector.tensor_scalar(ss[:, t:t + 1], ss[:, t:t + 1], 1.0 / D, NORM_EPS,
                                            ALU.mult, ALU.add).then_inc(s_ms, 1)
                scale(T - 1)


def constants():
    p = np.arange(P)[:, None]
    c = np.arange(N)[None, :]
    ident = np.eye(P, dtype=np.float32)
    log_g = np.log(1.0 - 2.0 ** (-5.0 - np.arange(HEADS))).astype(np.float32).astype(np.float64)
    decay = np.where((c >= p)[:, None, :], np.exp(log_g[None, :, None] * np.maximum(c - p, 0)[:, None, :]), 0.0)
    decay = (decay * HD ** -0.5).astype(np.float32)
    slopes = (2.0 ** (-8.0 * np.arange(1, DIFF_HEADS + 1) / DIFF_HEADS)).astype(np.float32)
    dist = np.abs(p - (c - (N - P))).astype(np.float32)
    alibi = -slopes[None, :, None] * dist[:, None, :] * np.float32(HD ** 0.5)
    late = (c - (N - P)) // CHUNK > p // CHUNK
    alibi = np.where(late[:, None, :], np.float32(MASKED), alibi).astype(np.float32)
    f = np.arange(P)
    thr = FIRST + P * (f % 4)
    route = np.concatenate([
        (np.arange(P)[:, None] < np.arange(P)[None, :]).astype(np.float32),
        np.ones((P, P), np.float32),
        np.tile(np.arange(EXPERTS, dtype=np.float32), (P, 1)),
        np.tile(thr.astype(np.float32), (P, 1)),
        np.tile(((f // 4 * LIST + thr) / LIST_UNIT).astype(np.float32), (P, 1)),
        np.tile((f // 4).astype(np.float32), (P, 1)),
        np.tile(f.astype(np.float32), (P, 1)),
        np.arange(1, P + 1, dtype=np.float32)[:, None],
    ], axis=1)
    asg = (np.arange(2)[None, :, None] * N + np.arange(T)[None, None, :] * P + np.arange(P)[:, None, None])
    return {"ident": ident, "decay": decay, "alibi": alibi, "route_consts": route,
            "asg_ids": asg.astype(np.int32)}


def laid_out(i):
    w_in = i["w_in"][0]
    at = [512 * n for n in range(13)]
    ax, ag, bq, bk, bv, cq, ck, cv, cg, dq, dk, dv = (w_in[:, at[n]:at[n + 1]] for n in range(12))
    w_mix = np.stack([ax, ag, bq, bk, cq, ck, dq, dk, bv, cv, cg, dv])
    w_mix = w_mix.reshape(12, D, 2, CW).transpose(0, 2, 1, 3).reshape(24, D, CW)
    gates = w_in[:, at[12]:].reshape(P, KD, 4, KD, P).transpose(3, 2, 0, 1, 4)
    branch = i["w_branch"][0].reshape(4, KB, P, KD, P).transpose(3, 0, 2, 1, 4)
    w_gb = np.concatenate([gates, branch], axis=3).reshape(4 * KD, P, UNIT)
    w_out = i["w_out"][0].reshape(KD // 2, 2, P, 2, BW).transpose(3, 0, 2, 1, 4).reshape(KD, P, PIECE)

    def cols(v, k):
        return v.reshape(P, k)

    def tiles(v):
        return v.reshape(KB, P).T

    small = np.concatenate(
        [cols(i["norm_mix"], KD), cols(i["norm_mem"], KD), cols(i["mem_norm"], KD)]
        + [tiles(i["conv_w"][0, j]) for j in range(4)]
        + [tiles(i[n][0]) for n in ("conv_b", "lru_ba", "lru_bx", "lru_lambda")], axis=1)
    rows = np.concatenate([i["final_norm"], i["b_group"][0], i["b_router"][0], i["diff_subln"][0],
                           i["diff_lambda"][0].reshape(-1), i["norm_ffn"][0]])[None, :]
    got = {"small": small, "rows": rows, "w_mix": w_mix, "w_gb": w_gb, "w_out_pieces": w_out,
           "w_mo_pieces": i["w_mo"][0].reshape(2, 2, P, D).transpose(0, 2, 1, 3).reshape(2, P, 2 * D),
           "rel_flipped": i["ca_rel_bias"][0, :, ::-1],
           "w_route": np.concatenate([i["w_group"][0], i["w_router"][0]], axis=1)}
    for n in ("wa", "wx"):
        blocks = i["lru_" + n][0]
        bd = np.zeros((KB, P, P), blocks.dtype)
        for k in range(2 * KB):
            o = (k % 2) * HD
            bd[k // 2, o:o + HD, o:o + HD] = blocks[k]
        got[n + "_bd"] = bd
    for n in ("x", "mem", "w_mq", "w_mk", "w_mv", "w1", "w3", "w2"):
        got[n] = i[n]
    return got


def kernel(**inputs):
    import concourse.bacc as bacc
    from concourse.bass_utils import run_bass_kernel_spmd

    inputs = {k: np.asarray(v) for k, v in inputs.items()}
    arrays = {n: np.ascontiguousarray(v) for n, v in {**laid_out(inputs), **constants()}.items()}
    nc = bacc.Bacc("TRN2", target_bir_lowering=False, num_devices=1)
    a = {n: nc.dram_tensor("in_" + n, list(v.shape), mybir.dt.from_np(v.dtype), kind="ExternalInput").ap()
         for n, v in arrays.items()}
    out = nc.dram_tensor("out_x", [1, N, D], F32, kind="ExternalOutput").ap()
    trunk(nc, a, out)
    r = run_bass_kernel_spmd(nc, [{"in_" + n: v for n, v in arrays.items()}], core_ids=[0])
    return r.results[0]["out_x"]
```
